# Optimizing a Trainium2 kernel written in Bass

```python
import jax, jax.numpy as jnp
from jax import lax
import numpy as np

D_MODEL = 2048
BATCH = 1
SEQ = 512
DEPTH = 1

N_Q_HEADS = 8
N_KV_HEADS = 4
HEAD_DIM = 128
GQA_GROUP = N_Q_HEADS // N_KV_HEADS
ROPE_THETA = 10000.0
AXIS_ROPE_DIM = HEAD_DIM // 2
Q_BLOCK = 128
GRID_W = 64
CONV_CH = 1024
CONV_K = 31
FFN_DIM = 5632
FFN_CONV_K = 3
EPS = 1e-6

ATTN_Q = N_Q_HEADS * HEAD_DIM
ATTN_KV = N_KV_HEADS * HEAD_DIM
IN_COLS = ATTN_Q + 2 * ATTN_KV + 2 * CONV_CH + 2 * D_MODEL
SPLITS = (ATTN_Q, ATTN_Q + ATTN_KV, ATTN_Q + 2 * ATTN_KV, ATTN_Q + 2 * ATTN_KV + 2 * CONV_CH)

kernel_name = 'hybrid_gqa_axialrope_conformer_convffn_encoder'

def rmsnorm(x, g):
    xf = x.astype(jnp.float32)
    y = xf * lax.rsqrt(jnp.mean(xf * xf, axis=-1, keepdims=True) + EPS)
    return (y * g.astype(jnp.float32)).astype(x.dtype)

def layernorm(x, g, b):
    xf = x.astype(jnp.float32)
    mu = jnp.mean(xf, axis=-1, keepdims=True)
    var = jnp.mean(jnp.square(xf - mu), axis=-1, keepdims=True)
    y = (xf - mu) * lax.rsqrt(var + EPS)
    return (y * g.astype(jnp.float32) + b.astype(jnp.float32)).astype(x.dtype)

def depthwise_conv(x, w, b):
    k = w.shape[0]
    pad = k // 2
    y = lax.conv_general_dilated(
        x, w[:, None, :].astype(x.dtype), window_strides=(1,),
        padding=[(pad, pad)], dimension_numbers=('NWC', 'WIO', 'NWC'),
        feature_group_count=x.shape[-1])
    return y + b.astype(x.dtype)

def axial_rope_tables(seq_len):
    rows = seq_len // GRID_W
    row = jnp.repeat(jnp.arange(rows), GRID_W).astype(jnp.float32)
    col = jnp.tile(jnp.arange(GRID_W), rows).astype(jnp.float32)
    inv_freq = ROPE_THETA ** (-jnp.arange(0, AXIS_ROPE_DIM, 2, dtype=jnp.float32) / AXIS_ROPE_DIM)
    ang = jnp.concatenate([row[:, None] * inv_freq, col[:, None] * inv_freq], axis=-1)
    return jnp.cos(ang), jnp.sin(ang)

def apply_rope(x, cos, sin):
    xf = x.astype(jnp.float32).reshape(x.shape[:-1] + (HEAD_DIM // 2, 2))
    x0, x1 = xf[..., 0], xf[..., 1]
    c = cos[None, :, None, :]
    s = sin[None, :, None, :]
    out = jnp.stack([x0 * c - x1 * s, x0 * s + x1 * c], axis=-1).reshape(x.shape)
    return out.astype(x.dtype)

def block_attention(q, k, v):
    b, s = q.shape[0], q.shape[1]
    nb = s // Q_BLOCK
    qb = q.reshape(b, nb, Q_BLOCK, N_KV_HEADS, GQA_GROUP, HEAD_DIM).transpose(1, 0, 2, 3, 4, 5)
    scale = HEAD_DIM ** -0.5

    def one_block(qi):
        sc = jnp.einsum('bqkgd,bskd->bkgqs', qi, k, preferred_element_type=jnp.float32) * scale
        p = jax.nn.softmax(sc, axis=-1)
        return jnp.einsum('bkgqs,bskd->bqkgd', p.astype(v.dtype), v)

    o = lax.map(one_block, qb)
    return o.transpose(1, 0, 2, 3, 4, 5).reshape(b, s, ATTN_Q)

def setup_inputs(seed: int = 0) -> dict:
    key = jax.random.key(seed)
    ks = jax.random.split(key, 20)
    f32 = jnp.float32

    def nrm(k, shape, scale):
        return jax.random.normal(k, shape, f32) * scale

    L = DEPTH
    return {
        'x': jax.random.normal(ks[0], (BATCH, SEQ, D_MODEL), f32),
        'norm_mix_g': 1.0 + nrm(ks[1], (L, D_MODEL), 0.02),
        'w_in': nrm(ks[2], (L, D_MODEL, IN_COLS), D_MODEL ** -0.5),
        'b_in': nrm(ks[3], (L, IN_COLS), 0.01),
        'q_norm_g': 1.0 + nrm(ks[4], (L, HEAD_DIM), 0.02),
        'k_norm_g': 1.0 + nrm(ks[5], (L, HEAD_DIM), 0.02),
        'w_attn_o': nrm(ks[6], (L, ATTN_Q, D_MODEL), ATTN_Q ** -0.5),
        'conv_dw_w': nrm(ks[7], (L, CONV_K, CONV_CH), CONV_K ** -0.5),
        'conv_dw_b': nrm(ks[8], (L, CONV_CH), 0.01),
        'conv_ln_g': 1.0 + nrm(ks[9], (L, CONV_CH), 0.02),
        'conv_ln_b': nrm(ks[10], (L, CONV_CH), 0.01),
        'w_conv_o': nrm(ks[11], (L, CONV_CH, D_MODEL), CONV_CH ** -0.5),
        'w_out': nrm(ks[12], (L, D_MODEL, D_MODEL), D_MODEL ** -0.5),
        'norm_ffn_g': 1.0 + nrm(ks[13], (L, D_MODEL), 0.02),
        'w_ffn_up': nrm(ks[14], (L, D_MODEL, 2 * FFN_DIM), D_MODEL ** -0.5),
        'ffn_dw_w': nrm(ks[15], (L, FFN_CONV_K, FFN_DIM), FFN_CONV_K ** -0.5),
        'ffn_dw_b': nrm(ks[16], (L, FFN_DIM), 0.01),
        'w_ffn_down': nrm(ks[17], (L, FFN_DIM, D_MODEL), FFN_DIM ** -0.5),
        'norm_final_g': 1.0 + nrm(ks[18], (D_MODEL,), 0.02),
    }

def reference(x, norm_mix_g, w_in, b_in, q_norm_g, k_norm_g, w_attn_o, conv_dw_w, conv_dw_b,
              conv_ln_g, conv_ln_b, w_conv_o, w_out, norm_ffn_g, w_ffn_up, ffn_dw_w, ffn_dw_b,
              w_ffn_down, norm_final_g):
    b, s, _ = x.shape
    cos, sin = axial_rope_tables(s)
    for l in range(DEPTH):
        h = rmsnorm(x, norm_mix_g[l])
        z = h @ w_in[l] + b_in[l]
        q, k, v, cv, gates = jnp.split(z, SPLITS, axis=-1)

        q = apply_rope(rmsnorm(q.reshape(b, s, N_Q_HEADS, HEAD_DIM), q_norm_g[l]), cos, sin)
        k = apply_rope(rmsnorm(k.reshape(b, s, N_KV_HEADS, HEAD_DIM), k_norm_g[l]), cos, sin)
        v = v.reshape(b, s, N_KV_HEADS, HEAD_DIM)
        a = block_attention(q, k, v) @ w_attn_o[l]

        u, ug = jnp.split(cv, 2, axis=-1)
        c = u * jax.nn.sigmoid(ug)
        c = depthwise_conv(c, conv_dw_w[l], conv_dw_b[l])
        c = jax.nn.silu(layernorm(c, conv_ln_g[l], conv_ln_b[l]))
        c = c @ w_conv_o[l]

        g_a, g_c = jnp.split(jax.nn.sigmoid(gates), 2, axis=-1)
        x = x + (g_a * a + g_c * c) @ w_out[l]

        h2 = rmsnorm(x, norm_ffn_g[l])
        gt, val = jnp.split(h2 @ w_ffn_up[l], 2, axis=-1)
        gt = depthwise_conv(gt, ffn_dw_w[l], ffn_dw_b[l])
        x = x + (jax.nn.silu(gt) * val) @ w_ffn_down[l]
    return rmsnorm(x, norm_final_g)


_drawn_inputs = setup_inputs


def setup_inputs(seed=0):
    import zlib

    import numpy as np

    out = dict(_drawn_inputs(seed))
    spreads = {}
    factors = {'norm_mix_g': 6.524,
     'b_in': 8.0,
     'q_norm_g': 8.0,
     'k_norm_g': 8.0,
     'conv_dw_b': 32.026,
     'conv_ln_g': 23.795,
     'conv_ln_b': 49.937,
     'norm_ffn_g': 11.503,
     'ffn_dw_b': 24.074,
     'norm_final_g': 22.976}
    for name, (base, spread) in spreads.items():
        noise = np.random.default_rng([zlib.crc32(name.encode()), seed]).standard_normal(out[name].shape)
        drawn = base * np.exp(spread * noise) if base else spread * noise
        out[name] = __import__('jax').numpy.asarray(drawn.astype(out[name].dtype))
    for name, factor in factors.items():
        out[name] = (out[name] * factor).astype(out[name].dtype)
    return out
```

```python
from contextlib import ExitStack

import numpy as np

import concourse.bass as bass
import concourse.mybir as mybir

ACT = mybir.ActivationFunctionType
ALU = mybir.AluOpType
AX = mybir.AxisListType
F32 = mybir.dt.float32
F32R = mybir.dt.float32r

P = 128
SEQ = 512
D = 2048
HEADS = 8
KV_HEADS = 4
HD = 128
CONV_CH = 1024
CONV_K = 31
FFN = 5632
FFN_K = 3
GRID_W = 64
ROPE_THETA = 10000.0
EPS = 1e-6

TT = SEQ // P
KD = D // P
KC = CONV_CH // P
KA = HEADS
KF = FFN // P
ROUNDS = KF // 4
ATTN_Q = HEADS * HD
ATTN_KV = KV_HEADS * HD
Q_COL = 0
K_COL = ATTN_Q
V_COL = ATTN_Q + ATTN_KV
GLU_COL = ATTN_Q + 2 * ATTN_KV
GATE_COL = GLU_COL + 2 * CONV_CH
PADDED = SEQ + 32
REACH = CONV_K // 2
POOL_CONV_TILES = 4

COL = {}
_at = 0
for _name, _n in (("g_mix", KD), ("g_ffn", KD), ("b_glu", 2 * KC), ("b_gate", 2 * KD), ("conv_b", KC),
                  ("ln_g", KC), ("ln_b", KC), ("conv_w", KC * CONV_K), ("ffn_w", KF * FFN_K), ("ffn_b", KF)):
    COL[_name] = _at
    _at += _n
N_COLS = _at

GLU_C = 0
QKV_C = GLU_C + 4 * 8
GATE_C = QKV_C + 4 * 8
MIX_C = GATE_C + 8 * 8
OUT_C = MIX_C + 8 * 4
FFN_C = OUT_C + 4 * 8
GLU_G, QKV_G, MIX_G, OUT_G = 0, 4, 8, 16
N_RAW = 4
N_SPLIT = 2


def val(const, i=None, per=0):
    return const if i is None else i * per + const


def build(nc, x, w_in, w_attn_o, w_conv_o, w_out, w_up, w_down, cols, b_qkv, qk_g, g_final, rope, y):
    ctx = ExitStack()
    with ctx:
        base = (nc.sbuf_base + 63) // 32 * 32
        cursor = [base]

        def at(name, shape, dt, offset):
            return nc.alloc_sbuf_tensor_at(name, [P] + shape, dt, offset=offset)

        def region(nbytes):
            o = cursor[0]
            cursor[0] += (nbytes + 31) // 32 * 32
            return o

        KB = 1024
        r_ring = region(32 * KB)
        r_act = region(64 * KB)
        r_mix = region(64 * KB)
        r_conv = region(KC * PADDED * 4)
        r_o = region(16 * KB)
        r_cols = region(N_COLS * 4)
        r_ident = region(512)
        r_mean_w = region(512)
        r_qkg = region(1024)
        r_rope = region(2048)
        r_small = region(1600)
        r_work = region(20 * KB)
        assert cursor[0] <= nc.sbuf_top, (cursor[0], nc.sbuf_top)

        w_raw = at("w_raw", [N_RAW, 1024], F32, r_ring)
        w_high = at("w_high", [N_SPLIT, 1024], F32R, r_ring + 16 * KB)
        w_low = at("w_low", [N_SPLIT, 1024], F32R, r_ring + 24 * KB)
        h_high = at("h_high", [KD, SEQ], F32R, r_act)
        h_low = at("h_low", [KD, SEQ], F32R, r_act + 32 * KB)
        o_high = at("o_high", [KA, SEQ], F32R, r_act)
        o_low = at("o_low", [KA, SEQ], F32R, r_act + 32 * KB)
        c_high = at("c_high", [KC, SEQ], F32R, r_act + 16 * KB)
        c_low = at("c_low", [KC, SEQ], F32R, r_act + 48 * KB)
        x_in = at("x_in", [TT, D], F32, r_mix)
        x_scaled = at("x_scaled", [TT, D], F32, r_mix + 32 * KB)
        glu_gate = at("glu_gate", [2, SEQ], F32, r_mix + 32 * KB)
        qkv = at("qkv", [TT, D], F32, r_mix)
        qk_sq = at("qk_sq", [TT * 4, HD], F32, r_mix + 40 * KB)
        rope_a = at("rope_a", [TT, 4, HD // 2], F32, r_mix + 48 * KB)
        rope_b = at("rope_b", [TT, 4, HD // 2], F32, r_mix + 52 * KB)
        rope_d = at("rope_d", [TT, 4, HD // 2], F32, r_mix + 56 * KB)
        probs = at("probs", [2, TT, SEQ], F32, r_mix + 32 * KB)
        pt_high = at("pt_high", [TT, SEQ], F32R, r_mix + 48 * KB)
        pt_low = at("pt_low", [TT, SEQ], F32R, r_mix + 56 * KB)
        gate_a = at("gate_a", [KD, SEQ], F32, r_mix)
        gate_c = at("gate_c", [KD, SEQ], F32, r_mix + 32 * KB)
        m_high = at("m_high", [KD, SEQ], F32R, r_mix)
        m_low = at("m_low", [KD, SEQ], F32R, r_mix + 32 * KB)
        u_high = at("u_high", [2, 4, SEQ], F32R, r_mix)
        u_low = at("u_low", [2, 4, SEQ], F32R, r_mix + 16 * KB)
        g_fin = at("g_fin", [D], F32, r_work)
        conv = at("conv", [KC, PADDED], F32, r_conv)
        b_qkv_all = at("b_qkv_all", [D], F32, r_o)
        o_full = at("o_full", [KA, SEQ], F32, r_o)
        x_res = at("x_res", [TT, D], F32, r_conv)
        par = at("par", [N_COLS], F32, r_cols)
        ident = at("ident", [P], F32, r_ident)
        mean_w = at("mean_w", [P], F32, r_mean_w)
        qkg = at("qkg", [2, HD], F32, r_qkg)
        rope_cs = at("rope_cs", [2, TT, HD // 2], F32, r_rope)
        small = [r_small]

        def tiny(name, n):
            t = at(name, [n], F32, small[0])
            small[0] += (n * 4 + 31) // 32 * 32
            return t

        sumsq = tiny("sumsq", 3 * TT)
        meansq = tiny("meansq", 3 * TT)
        rstd = tiny("rstd", 3 * TT)
        neg_half = tiny("neg_half", 1)
        qk_ss = tiny("qk_ss", 16)
        qk_ms = tiny("qk_ms", 16)
        qk_root = tiny("qk_root", 16)
        qk_r0 = tiny("qk_r0", 16)
        qk_t = tiny("qk_t", 16)
        qk_rstd = tiny("qk_rstd", 16)
        neg_max = tiny("neg_max", 4 * HEADS)
        exp_bias = tiny("exp_bias", 4 * HEADS)
        row_sum = tiny("row_sum", 4 * HEADS)
        row_inv = tiny("row_inv", 4 * HEADS)
        assert small[0] - r_small <= 1600
        xg = at("xg", [4, SEQ], F32, r_work)
        kq_high = at("kq_high", [3, SEQ], F32R, r_work)
        kq_low = at("kq_low", [3, SEQ], F32R, r_work + 6 * KB)
        v_high = at("v_high", [TT, HD], F32R, r_work + 12 * KB)
        v_low = at("v_low", [TT, HD], F32R, r_work + 14 * KB)
        pool_acc = at("pool_acc", [SEQ], F32, r_work + 16 * KB)
        pool_tap = at("pool_tap", [SEQ], F32, r_work + 18 * KB)
        vec_acc = at("vec_acc", [SEQ], F32, r_work)
        ch_sum = at("ch_sum", [SEQ], F32, r_work + 2 * KB)
        mean_sb = at("mean_sb", [SEQ], F32, r_work + 4 * KB)
        ch_sq = at("ch_sq", [2, SEQ], F32, r_work + 6 * KB)
        sq_sum = at("sq_sum", [SEQ], F32, r_work + 10 * KB)
        var_sb = at("var_sb", [SEQ], F32, r_work + 12 * KB)
        ln_rstd = at("ln_rstd", [SEQ], F32, r_work + 14 * KB)
        mix_a = at("mix_a", [2, SEQ], F32, r_work)
        mix_c = at("mix_c", [2, SEQ], F32, r_work + 4 * KB)
        mix_m = at("mix_m", [2, SEQ], F32, r_work + 8 * KB)
        f_gate = at("f_gate", [2, SEQ], F32, r_work + 8 * KB)
        f_val = at("f_val", [2, SEQ], F32, r_work + 12 * KB)
        f_u = at("f_u", [2, SEQ], F32, r_work + 16 * KB)

        bank = [ctx.enter_context(nc.psum_tensor(f"bank{b}", [P, 512], F32)) for b in range(8)]

        def sem(name):
            return ctx.enter_context(nc.semaphore(name))

        chunk_loaded = [sem(f"chunk_loaded{s}") for s in range(N_RAW)]
        high_split = sem("high_split")
        low_split = sem("low_split")
        chunk_used = sem("chunk_used")
        group_freed = sem("group_freed")
        x_loaded = [sem(f"x_loaded{t}") for t in range(TT)]
        xres_loaded = sem("xres_loaded")
        par_loaded = sem("par_loaded")
        consts_made = sem("consts_made")
        squares_summed = sem("squares_summed")
        meansq_ready = sem("meansq_ready")
        rstd_ready = sem("rstd_ready")
        xs_ready = sem("xs_ready")
        x_turned = sem("x_turned")
        xg_ready = sem("xg_ready")
        h_high_ready = sem("h_high_ready")
        h_low_ready = sem("h_low_ready")
        glu_gate_ready = sem("glu_gate_ready")
        pool_step = sem("pool_step")
        vec_step = sem("vec_step")
        vec_conv_done = sem("vec_conv_done")
        pool_conv_done = sem("pool_conv_done")
        ch_sum_ready = sem("ch_sum_ready")
        mean_ready = sem("mean_ready")
        mean_copied = sem("mean_copied")
        centred = sem("centred")
        ch_sq_ready = sem("ch_sq_ready")
        ch_sq_added = sem("ch_sq_added")
        var_ready = sem("var_ready")
        var_copied = sem("var_copied")
        ln_rstd_ready = sem("ln_rstd_ready")
        c_normed = sem("c_normed")
        c_swished = sem("c_swished")
        qk_squared = sem("qk_squared")
        qk_ms_ready = sem("qk_ms_ready")
        qk_root_ready = sem("qk_root_ready")
        roped = sem("roped")
        kq_turned = sem("kq_turned")
        kq_high_ready = sem("kq_high_ready")
        kq_low_ready = sem("kq_low_ready")
        v_high_ready = sem("v_high_ready")
        v_low_ready = sem("v_low_ready")
        scores_ready = sem("scores_ready")
        exp_bias_ready = sem("exp_bias_ready")
        exp_ready = sem("exp_ready")
        probs_ready = sem("probs_ready")
        probs_turned = sem("probs_turned")
        pt_high_ready = sem("pt_high_ready")
        pt_low_ready = sem("pt_low_ready")
        o_summed = sem("o_summed")
        o_ready = sem("o_ready")
        gate_stored = sem("gate_stored")
        oc_high_ready = sem("oc_high_ready")
        oc_low_ready = sem("oc_low_ready")
        mix_gated = sem("mix_gated")
        m_ready = sem("m_ready")
        m_high_ready = sem("m_high_ready")
        m_low_ready = sem("m_low_ready")
        tap_mid_ready = sem("tap_mid_ready")
        tap_left_ready = sem("tap_left_ready")
        val_saved = sem("val_saved")
        taps_ready = sem("taps_ready")
        silu_ready = sem("silu_ready")
        u_ready = sem("u_ready")
        u_high_ready = sem("u_high_ready")
        u_low_ready = sem("u_low_ready")
        gfin_loaded = sem("gfin_loaded")
        down_freed = sem("down_freed")
        y_ready = sem("y_ready")
        y_stored = sem("y_stored")

        def freed(index, i=None, per=0):
            return val(index + 3, i, per)

        def used(c, i=None, per=0):
            return val(c + 1, i, per)

        def chunk_slot(c):
            return c % N_RAW, 16 * (c // N_RAW + 1)

        def col(name, n=0, width=1):
            a = COL[name] + n
            return par[:, a:a + width]

        wi = w_in.rearrange("(k p) n -> p k n", p=P)
        wu = w_up.rearrange("(k p) n -> p k n", p=P)
        wd = w_down.rearrange("(k p) n -> p k n", p=P)
        wo = w_out.rearrange("(k p) n -> p k n", p=P)
        wa = w_attn_o.rearrange("(k p) n -> p k n", p=P)
        wc = w_conv_o.rearrange("(k p) n -> p k n", p=P)
        x_tiles = x.rearrange("(t p) d -> t p d", p=P)
        y_tiles = y.rearrange("(t p) d -> t p d", p=P)

        block = ctx.enter_context(nc.Block())

        @block.sync
        def _(sp):
            def load(c, src, i=None, per=0):
                slot, landed = chunk_slot(c)
                if c >= N_RAW or i is not None:
                    sp.wait_ge(low_split, val(c - N_RAW + 1, i, per))
                dst = w_raw[:, slot, :].rearrange("p (k n) -> p k n", k=src.shape[1])
                sp.dma_start(dst, src).then_inc(chunk_loaded[slot], 16)

            def load_pair(c, src_a, src_b, col_a, col_b, chunks, i=None, per=0):
                for half, (src, c0) in enumerate(((src_a, col_a), (src_b, col_b))):
                    for q in range(chunks):
                        load(c + half * chunks + q, src[:, 4 * q:4 * q + 4, bass.ds(c0, 256)], i, per)

            def load_wide(c, src, col0, i=None, per=0):
                for q in range(8):
                    load(c + q, src[:, 2 * q:2 * q + 2, bass.ds(col0, 512)], i, per)

            for t in range(TT):
                sp.dma_start(x_in[:, t, :], x_tiles[t]).then_inc(x_loaded[t], 16)
            load_pair(GLU_C, wi, wi, GLU_COL, GLU_COL + CONV_CH, 4)
            with sp.Fori(0, 3) as i:
                load_pair(GLU_C + 8, wi, wi, i * 256 + (GLU_COL + 256),
                          i * 256 + (GLU_COL + CONV_CH + 256), 4, i, 8)
            load_wide(QKV_C, wi, K_COL)
            with sp.Fori(0, 2) as i:
                load_wide(QKV_C + 8, wi, i * 512 + Q_COL, i, 8)
            load_wide(QKV_C + 24, wi, V_COL)
            with sp.Fori(0, 8) as i:
                load_pair(GATE_C, wi, wi, i * 256 + GATE_COL, i * 256 + (GATE_COL + D), 4, i, 8)
            with sp.Fori(0, 8) as i:
                load_pair(MIX_C, wa, wc, i * 256, i * 256, 2, i, 4)
            sp.wait_ge(oc_low_ready, 4)
            for t in range(TT):
                sp.dma_start(x_res[:, t, :], x_tiles[t]).then_inc(xres_loaded, 16)
            with sp.Fori(0, 4) as i:
                load_wide(OUT_C, wo, i * 512, i, 8)
            for a in range(4):
                load_pair(FFN_C + 8 * a, wu, wu, 256 * a, FFN + 256 * a, 4)

            def load_down(c, r, i=None, per=0):
                for q in range(4):
                    for k in range(2):
                        src = wd[:, bass.ds(r + 2 * k, 2), 512 * q:512 * q + 512]
                        load(c + 2 * q + k, src, i, per)

            with sp.Fori(0, ROUNDS - 2) as i:
                load_down(FFN_C + 32, i * 4, i, 24)
                for a in range(2):
                    load_pair(FFN_C + 40 + 8 * a, wu, wu, i * 512 + (1024 + 256 * a),
                              i * 512 + (FFN + 1024 + 256 * a), 4, i, 24)
            for k in range(2):
                r = ROUNDS - 2 + k
                load_down(FFN_C + 32 + 24 * (ROUNDS - 2) + 8 * k, 4 * r)
            for t in range(TT):
                sp.wait_ge(y_ready, t + 1)
                sp.dma_start(y_tiles[t], x_res[:, t, :]).then_inc(y_stored, 16)
            sp.wait_ge(y_stored, 16 * TT)

        @block.gpsimd
        def _(pool):
            steps = [0]

            def step(ins):
                ins.then_inc(pool_step, 1)
                steps[0] += 1
                pool.wait_ge(pool_step, steps[0])

            step(pool.memset(ident[:, :], 0.0))
            pool.affine_select(out=ident[:, :], in_=ident[:, :], compare_op=ALU.not_equal, fill=1.0,
                               base=0, pattern=[[-1, P]], channel_multiplier=1).then_inc(consts_made, 1)
            pool.memset(mean_w[:, :], 1.0 / CONV_CH).then_inc(consts_made, 1)
            pool.memset(neg_half[:, :], -0.5).then_inc(consts_made, 1)
            pool.memset(conv[:, :, 0:REACH], 0.0).then_inc(consts_made, 1)
            pool.memset(conv[:, :, REACH + SEQ:PADDED], 0.0).then_inc(consts_made, 1)
            pool.wait_ge(consts_made, 5)

            def root(q):
                pool.wait_ge(meansq_ready, q + 1)
                pool.tensor_tensor(rstd[:, q:q + 1], meansq[:, q:q + 1], neg_half[:, :],
                                   ALU.pow).then_inc(rstd_ready, 1)

            def norm_low(w, t):
                for kq in range(4):
                    n = 16 * w + 4 * t + kq
                    pool.wait_ge(h_high_ready, n + 1)
                    blk = h_high[:, 4 * kq:4 * kq + 4, t * P:(t + 1) * P]
                    pool.tensor_tensor(h_low[:, 4 * kq:4 * kq + 4, t * P:(t + 1) * P],
                                       xg[:, n % 4, :].rearrange("p (k n) -> p k n", k=4),
                                       blk.bitcast(F32), ALU.subtract).then_inc(h_low_ready, 1)

            def norm(w):
                root(4 * w)
                for t in range(TT):
                    if t + 1 < TT:
                        root(4 * w + t + 1)
                    norm_low(w, t)

            norm(0)

            def centre(i):
                return conv[:, i, REACH:REACH + SEQ]

            for i in range(POOL_CONV_TILES):
                if i % 2 == 0:
                    pool.wait_ge(group_freed, freed(GLU_G + i // 2))
                if i == 0:
                    pool.wait_ge(par_loaded, 16 * 4)
                w0 = COL["conv_w"] + i * CONV_K
                step(pool.tensor_tensor(pool_acc[:, :], conv[:, i, 0:SEQ],
                                        par[:, w0:w0 + 1].to_broadcast([P, SEQ]), ALU.mult))
                for k in range(1, CONV_K):
                    step(pool.tensor_tensor(pool_tap[:, :], conv[:, i, k:k + SEQ],
                                            par[:, w0 + k:w0 + k + 1].to_broadcast([P, SEQ]), ALU.mult))
                    step(pool.tensor_tensor(pool_acc[:, :], pool_acc[:, :], pool_tap[:, :], ALU.add))
                step(pool.tensor_tensor(centre(i), pool_acc[:, :],
                                        col("conv_b", i).to_broadcast([P, SEQ]), ALU.add))
            pool.wait_ge(o_ready, HEADS)
            step(pool.tensor_tensor(ch_sum[:, :], centre(0), centre(1), ALU.add))
            for i in range(2, KC):
                if i >= POOL_CONV_TILES:
                    pool.wait_ge(vec_conv_done, i - POOL_CONV_TILES + 1)
                ins = pool.tensor_tensor(ch_sum[:, :], ch_sum[:, :], centre(i), ALU.add)
                if i < KC - 1:
                    step(ins)
                else:
                    ins.then_inc(ch_sum_ready, 1)
            pool.wait_ge(ch_sq_ready, 2)
            pool.tensor_tensor(sq_sum[:, :], ch_sq[:, 0, :], ch_sq[:, 1, :], ALU.add).then_inc(ch_sq_added, 2)
            for i in range(2, KC):
                pool.wait_ge(ch_sq_ready, i + 1)
                pool.wait_ge(ch_sq_added, i)
                pool.tensor_tensor(sq_sum[:, :], sq_sum[:, :], ch_sq[:, i % 2, :],
                                   ALU.add).then_inc(ch_sq_added, 1)
            pool.wait_ge(var_copied, 1)
            pool.tensor_tensor(ln_rstd[:, :], var_sb[:, :], neg_half[:, :].to_broadcast([P, SEQ]),
                               ALU.pow).then_inc(ln_rstd_ready, 1)

            def mix_tile(b, i):
                if b == 0:
                    pool.wait_ge(mix_gated, i + 1)
                else:
                    pool.wait_ge(group_freed, i + freed(MIX_G))
                pool.wait_ge(m_low_ready, i * 2)
                pool.tensor_tensor(mix_m[:, b, :], mix_a[:, b, :], mix_c[:, b, :],
                                   ALU.add).then_inc(m_ready, 1)

            def one(t, j):
                return t[:, bass.ds(j, 1), :].rearrange("p a n -> p (a n)")

            with pool.Fori(0, KD // 2) as i:
                for b in range(2):
                    mix_tile(b, i)
                for b in range(2):
                    pool.wait_ge(m_high_ready, i * 2 + (b + 1))
                    pool.tensor_tensor(one(m_low, i * 2 + b), mix_m[:, b, :],
                                       one(m_high, i * 2 + b).bitcast(F32),
                                       ALU.subtract).then_inc(m_low_ready, 1)
            norm(1)

            def u_lows(n, i=None):
                buf, k = n // 4 % 2, n % 4
                for b in range(2):
                    pool.wait_ge(u_high_ready, val(n + b + 1, i, 8))
                    pool.tensor_tensor(u_low[:, buf, k + b, :], f_u[:, b, :],
                                       u_high[:, buf, k + b, :].bitcast(F32),
                                       ALU.subtract).then_inc(u_low_ready, 1)

            with pool.Fori(0, KF // 8) as i:
                for n in range(0, 8, 2):
                    u_lows(n, i)
            for n in range(KF // 8 * 8, KF, 2):
                u_lows(n)
            for t in range(TT):
                root(2 * TT + t)

        @block.scalar
        def _(act):
            for dst, src in ((par[:, :], cols), (qkg[:, :, :], qk_g.partition_broadcast(P)),
                             (rope_cs[:, :, :, :], rope), (b_qkv_all[:, :], b_qkv.partition_broadcast(P))):
                act.dma_start(dst, src).then_inc(par_loaded, 16)

            def split(c, i=None, per=0):
                slot, landed = chunk_slot(c)
                act.wait_ge(chunk_loaded[slot], val(landed, i, per * 16 // N_RAW))
                if c >= N_SPLIT or i is not None:
                    act.wait_ge(chunk_used, val(c - N_SPLIT + 1, i, per))
                act.activation(w_high[:, c % N_SPLIT, :], w_raw[:, slot, :], ACT.Copy).then_inc(high_split, 1)

            def square(w, t, src):
                act.activation(x_scaled[:, t, :], src[:, t, :], ACT.Square,
                               accum_out=sumsq[:, 4 * w + t:4 * w + t + 1]).then_inc(squares_summed, 1)

            def norm_high(w, t):
                for kq in range(4):
                    n = 16 * w + 4 * t + kq
                    act.wait_ge(xg_ready, n + 1)
                    act.activation(h_high[:, 4 * kq:4 * kq + 4, t * P:(t + 1) * P],
                                   xg[:, n % 4, :].rearrange("p (k n) -> p k n", k=4),
                                   ACT.Copy).then_inc(h_high_ready, 1)

            act.wait_ge(x_loaded[0], 16)
            square(0, 0, x_in)
            for t in range(TT):
                if t + 1 < TT:
                    act.wait_ge(x_loaded[t + 1], 16)
                    square(0, t + 1, x_in)
                norm_high(0, t)

            def glu_out(g):
                s = 4 * (g % 2)
                act.wait_ge(chunk_used, used(GLU_C + 8 * g + 7))
                if g == 0:
                    act.wait_ge(par_loaded, 16 * 4)
                if g >= 1:
                    act.wait_ge(group_freed, freed(GLU_G + g - 1))
                for b in range(2):
                    act.activation(glu_gate[:, b, :], bank[s + 2 + b][:, :], ACT.Sigmoid,
                                   bias=col("b_glu", KC + 2 * g + b)).then_inc(glu_gate_ready, 1)

            for g in range(4):
                for q in range(8):
                    split(GLU_C + 8 * g + q)
                    if g >= 1 and q == 1:
                        glu_out(g - 1)

            qk_cols = (K_COL, Q_COL, Q_COL + 512)
            for g in range(4):
                for q in range(8):
                    split(QKV_C + 8 * g + q)
                    if g == 0 and q == 1:
                        glu_out(3)
                    if g >= 1 and q == 2:
                        act.wait_ge(group_freed, freed(QKV_G + g - 1))
                        if g >= 2:
                            act.wait_ge(qk_ms_ready, g - 1)
                        act.activation(qk_sq[:, :, :].rearrange("p (t h) d -> p t (h d)", t=TT),
                                       qkv[:, :, qk_cols[g - 1]:qk_cols[g - 1] + 512],
                                       ACT.Square).then_inc(qk_squared, 1)
                    if g >= 1 and q == 3:
                        act.wait_ge(qk_ms_ready, g)
                        act.activation(qk_root[:, :], qk_ms[:, :], ACT.Sqrt).then_inc(qk_root_ready, 1)
            split(GATE_C)
            split(GATE_C + 1)

            def kq_evac(g):
                for b in range(3):
                    act.wait_ge(kq_turned, 3 * g + b + 1)
                    act.activation(kq_high[:, b, :], bank[5 + b][:, :], ACT.Copy).then_inc(kq_high_ready, 1)

            def v_split(g):
                if g == 0:
                    act.wait_ge(group_freed, freed(QKV_G + 3))
                else:
                    act.wait_ge(o_summed, 2 * g)
                act.activation(v_high[:, :, :], qkv[:, :, V_COL + g * HD:V_COL + (g + 1) * HD],
                               ACT.Copy).then_inc(v_high_ready, 1)

            def exps(h):
                for t in range(TT):
                    n = 4 * h + t
                    act.wait_ge(exp_bias_ready, n + 1)
                    if h >= 2:
                        act.wait_ge(probs_turned, 4 * (h - 1))
                    act.activation(probs[:, h % 2, t, :], bank[t][:, :], ACT.Exp, bias=exp_bias[:, n:n + 1],
                                   scale=float(HD) ** -0.5,
                                   accum_out=row_sum[:, n:n + 1]).then_inc(exp_ready, 1)

            def pt_evac(h):
                for k in range(TT):
                    act.wait_ge(probs_turned, 4 * h + k + 1)
                    act.activation(pt_high[:, k, :], bank[4 + k][:, :], ACT.Copy).then_inc(pt_high_ready, 1)

            kq_evac(0)
            v_split(0)
            exps(0)
            for h in range(HEADS):
                if h + 1 < HEADS:
                    exps(h + 1)
                if h % 2 == 0 and h > 0:
                    v_split(h // 2)
                pt_evac(h)
                act.wait_ge(o_summed, h + 1)
                act.activation(o_full[:, h, :], bank[4][:, :], ACT.Copy).then_inc(o_ready, 1)
                if h % 2 == 0 and h // 2 + 1 < KV_HEADS:
                    kq_evac(h // 2 + 1)
            act.wait_ge(o_ready, HEADS)
            act.sem_inc(gate_stored, 8)

            def gate_out(g, b):
                s = 4 * (g % 2)
                act.wait_ge(chunk_used, used(GATE_C + 8 * g + 7))
                j = 2 * g + b
                act.activation(gate_a[:, j, :], bank[s + b][:, :], ACT.Sigmoid,
                               bias=col("b_gate", j)).then_inc(gate_stored, 1)
                act.activation(gate_c[:, j, :], bank[s + 2 + b][:, :], ACT.Sigmoid,
                               bias=col("b_gate", KD + j)).then_inc(gate_stored, 1)

            def oc_high(n):
                act.wait_ge(chunk_used, used(GATE_C + 7 * 8 + 4 + n))
                if n < 2:
                    act.activation(o_high[:, 4 * n:4 * n + 4, :], o_full[:, 4 * n:4 * n + 4, :],
                                   ACT.Copy).then_inc(oc_high_ready, 1)
                else:
                    k = 4 * (n - 2)
                    act.wait_ge(c_swished, k + 4)
                    act.activation(c_high[:, k:k + 4, :], conv[:, k:k + 4, REACH:REACH + SEQ],
                                   ACT.Copy).then_inc(oc_high_ready, 1)

            def centre(i):
                return conv[:, i, REACH:REACH + SEQ]

            for g in range(8):
                for q in range(8):
                    if g > 0 or q > 1:
                        split(GATE_C + 8 * g + q)
                    if g >= 1 and q in (1, 2):
                        gate_out(g - 1, q - 1)
                    if g == 5 and 3 <= q <= 6:
                        for i in (2 * (q - 3), 2 * (q - 3) + 1):
                            act.wait_ge(centred, i + 1)
                            if i >= 2:
                                act.wait_ge(ch_sq_added, i - 1 if i > 2 else 2)
                            act.activation(ch_sq[:, i % 2, :], centre(i), ACT.Square).then_inc(ch_sq_ready, 1)
                    if g == 6 and 4 <= q <= 7:
                        for i in (2 * (q - 4), 2 * (q - 4) + 1):
                            act.wait_ge(c_normed, i + 1)
                            act.activation(centre(i), centre(i), ACT.Silu, bias=col("ln_b", i),
                                           scale=col("ln_g", i)).then_inc(c_swished, 1)
                    if g == 7 and q >= 6:
                        oc_high(q - 6)

            def m_highs(j, b, dst, i=None, per=0):
                act.wait_ge(m_ready, val(j + 1, i, per))
                act.activation(dst, mix_m[:, b, :], ACT.Copy).then_inc(m_high_ready, 1)

            for q in range(4):
                split(MIX_C + q)
                if q < 2:
                    oc_high(2 + q)
                if q in (1, 2):
                    gate_out(7, q - 1)
            with act.Fori(0, 7) as i:
                for q in range(4):
                    split(MIX_C + 4 + q, i, 4)
                    if q >= 2:
                        j = i * 2 + (q - 2)
                        m_highs(q - 2, q - 2, m_high[:, bass.ds(j, 1), :].rearrange("p a n -> p (a n)"), i, 2)
            for g in range(4):
                for q in range(8):
                    split(OUT_C + 8 * g + q)
                    if g == 0 and q in (2, 3):
                        m_highs(KD - 2 + q - 2, q - 2, m_high[:, KD - 2 + q - 2, :])
            split(FFN_C)
            split(FFN_C + 1)

            act.wait_ge(group_freed, freed(OUT_G + 3))
            square(1, 0, x_res)
            for t in range(TT):
                if t + 1 < TT:
                    square(1, t + 1, x_res)
                norm_high(1, t)

            act.wait_ge(h_low_ready, 32)
            act.dma_start(g_fin[:, :], g_final.partition_broadcast(P)).then_inc(gfin_loaded, 16)

            def up_slot(q, n, last, buf, i=None):
                s, a = 4 * (n // 2 % 2), n // 2 % 2
                for b in range(2):
                    ft = val(n + b, i, 8)
                    if q == 1:
                        if b == 0:
                            act.wait_ge(chunk_used, used(last, i, 48))
                            if n >= 2:
                                act.wait_ge(u_ready, val(n, i, 8))
                        act.activation(f_gate[:, b, :], bank[s + b][:, :], ACT.Identity,
                                       bias=par[:, bass.ds(ft + COL["ffn_b"], 1)],
                                       scale=par[:, bass.ds(ft * 3 + (COL["ffn_w"] + 1), 1)]
                                       ).then_inc(tap_mid_ready, 1)
                        act.activation(f_val[:, b, :], bank[s + 2 + b][:, :], ACT.Copy).then_inc(val_saved, 1)
                    if q == 2:
                        act.wait_ge(taps_ready, val(n + b + 1, i, 8))
                        act.activation(f_gate[:, b, :], f_gate[:, b, :], ACT.Silu).then_inc(silu_ready, 1)
                    if q == 5:
                        act.wait_ge(u_ready, val(n + b + 1, i, 8))
                        act.activation(u_high[:, buf, 2 * a + b, :], f_u[:, b, :],
                                       ACT.Copy).then_inc(u_high_ready, 1)

            for q in range(2, 8):
                split(FFN_C + q)
            for g in range(1, 4):
                for q in range(8):
                    split(FFN_C + 8 * g + q)
                    up_slot(q, 2 * g - 2, FFN_C + 8 * g - 1, (g - 1) // 2)

            def ffn_round(r, i=None):
                c = FFN_C + 32 + 24 * r
                for q in range(8):
                    split(c + q, i, 48)
                    up_slot(q, 4 * r + 6, c - 1, (r + 1) % 2, i)
                for q in range(8):
                    split(c + 8 + q, i, 48)
                for q in range(8):
                    split(c + 16 + q, i, 48)
                    up_slot(q, 4 * r + 8, c + 15, r % 2, i)

            with act.Fori(0, (ROUNDS - 3) // 2) as i:
                ffn_round(0, i)
                ffn_round(1, i)
            ffn_round(ROUNDS - 3)
            c = FFN_C + 32 + 24 * (ROUNDS - 2)
            for q in range(8):
                split(c + q)
                up_slot(q, KF - 2, c - 1, (ROUNDS - 1) % 2)
            for q in range(8):
                split(c + 8 + q)
            act.wait_ge(down_freed, 4 * ROUNDS)
            for t in range(TT):
                square(2, t, x_res)

        @block.vector
        def _(dve):
            steps = [0]

            def step(ins, wait=True):
                ins.then_inc(vec_step, 1)
                steps[0] += 1
                if wait:
                    dve.wait_ge(vec_step, steps[0])

            def split(c, i=None, per=0):
                slot, _ = chunk_slot(c)
                b = c % N_SPLIT
                dve.wait_ge(high_split, val(c + 1, i, per))
                dve.tensor_tensor(w_low[:, b, :], w_raw[:, slot, :], w_high[:, b, :].bitcast(F32),
                                  ALU.subtract).then_inc(low_split, 1)

            def scale_tile(w, t, src):
                q = 4 * w + t
                dve.wait_ge(squares_summed, q + 1)
                dve.tensor_scalar(meansq[:, q:q + 1], sumsq[:, q:q + 1], 1.0 / D, EPS, ALU.mult,
                                  ALU.add).then_inc(meansq_ready, 1)
                dve.wait_ge(rstd_ready, q + 1)
                dve.tensor_scalar(x_scaled[:, t, :], src[:, t, :], rstd[:, q:q + 1], None,
                                  ALU.mult).then_inc(xs_ready, 1)

            def norm(w, src, gamma):
                scale_tile(w, 0, src)
                for t in range(TT):
                    if t + 1 < TT:
                        scale_tile(w, t + 1, src)
                    for kq in range(4):
                        n = 16 * w + 4 * t + kq
                        dve.wait_ge(x_turned, n + 1)
                        if n % 16 >= 4:
                            dve.wait_ge(h_low_ready, n - 3)
                        dve.tensor_tensor(xg[:, n % 4, :].rearrange("p (k n) -> p k n", k=4),
                                          bank[n % 8][:, :].rearrange("p (k n) -> p k n", k=4),
                                          col(gamma, 4 * kq, 4).unsqueeze(2).to_broadcast([P, 4, P]),
                                          ALU.mult).then_inc(xg_ready, 1)

            dve.wait_ge(par_loaded, 16 * 4)
            norm(0, x_in, "g_mix")
            dve.wait_ge(xg_ready, 16)
            dve.sem_inc(group_freed, 2)

            def glu_out(g):
                s = 4 * (g % 2)
                for b in range(2):
                    dve.wait_ge(glu_gate_ready, 2 * g + b + 1)
                    if g == 0 and b == 0:
                        dve.wait_ge(consts_made, 5)
                    ins = dve.scalar_tensor_tensor(out=conv[:, 2 * g + b, REACH:REACH + SEQ],
                                                   in0=bank[s + b][:, :], scalar=col("b_glu", 2 * g + b),
                                                   in1=glu_gate[:, b, :], op0=ALU.add, op1=ALU.mult)
                ins.then_inc(group_freed, 1)

            for g in range(4):
                for q in range(8):
                    split(GLU_C + 8 * g + q)
                    if g >= 1 and q == 2:
                        glu_out(g - 1)

            qk_cols = (K_COL, Q_COL, Q_COL + 512)

            def add_bias(e, c0):
                for t in range(TT):
                    ins = dve.tensor_tensor(qkv[:, t, c0:c0 + 512], bank[4 * (e % 2) + t][:, :],
                                            b_qkv_all[:, c0:c0 + 512], ALU.add)
                ins.then_inc(group_freed, 1)

            def qk_slot(q, e):
                c0 = qk_cols[e]
                h = qkv[:, :, c0:c0 + 512].rearrange("p t (h d) -> p t h d", h=4)
                if q == 1:
                    dve.wait_ge(chunk_used, used(QKV_C + 8 * e + 7))
                    add_bias(e, c0)
                if q == 3:
                    dve.wait_ge(qk_squared, e + 1)
                    step(dve.tensor_reduce(qk_ss[:, :], qk_sq[:, :, :], AX.X, ALU.add))
                    dve.tensor_scalar(qk_ms[:, :], qk_ss[:, :], 1.0 / HD, EPS, ALU.mult,
                                      ALU.add).then_inc(qk_ms_ready, 1)
                if q == 4:
                    dve.wait_ge(qk_root_ready, e + 1)
                    step(dve.reciprocal(qk_r0[:, :], qk_root[:, :]))
                    step(dve.tensor_tensor(qk_t[:, :], qk_r0[:, :], qk_r0[:, :], ALU.mult))
                    step(dve.tensor_tensor(qk_t[:, :], qk_t[:, :], qk_ms[:, :], ALU.mult))
                    step(dve.tensor_scalar(qk_t[:, :], qk_t[:, :], -0.5, 1.5, ALU.mult, ALU.add))
                    step(dve.tensor_tensor(qk_rstd[:, :], qk_r0[:, :], qk_t[:, :], ALU.mult))
                    dve.wait_ge(group_freed, freed(QKV_G + e))
                    for t in range(TT):
                        ins = dve.tensor_tensor(h[:, t], h[:, t],
                                                qk_rstd[:, 4 * t:4 * t + 4].unsqueeze(2).to_broadcast([P, 4, HD]),
                                                ALU.mult)
                    step(ins)
                if q == 5:
                    g = qkg[:, 1 if e == 0 else 0, :].unsqueeze(1).to_broadcast([P, 4, HD])
                    for t in range(TT):
                        ins = dve.tensor_tensor(h[:, t], h[:, t], g, ALU.mult)
                    step(ins)
                if q in (6, 7):
                    pairs = qkv[:, :, c0:c0 + 512].rearrange("p t (h j two) -> p t h j two", h=4, two=2)
                    for t in range(TT):
                        x0, x1 = pairs[:, t, :, :, 0], pairs[:, t, :, :, 1]
                        cos = rope_cs[:, 0, t, :].unsqueeze(1).to_broadcast([P, 4, HD // 2])
                        sin = rope_cs[:, 1, t, :].unsqueeze(1).to_broadcast([P, 4, HD // 2])
                        if q == 6:
                            if e >= 1 and t == 0:
                                dve.wait_ge(roped, e)
                            dve.tensor_tensor(rope_a[:, t], x0, cos, ALU.mult)
                            dve.tensor_tensor(rope_b[:, t], x1, sin, ALU.mult)
                            ins = dve.tensor_tensor(rope_d[:, t], x0, sin, ALU.mult)
                        else:
                            dve.tensor_tensor(x0, rope_a[:, t], rope_b[:, t], ALU.subtract)
                            ins = dve.tensor_tensor(x1, x1, cos, ALU.mult)
                    step(ins)
                    if q == 7:
                        for t in range(TT):
                            x1 = pairs[:, t, :, :, 1]
                            ins = dve.tensor_tensor(x1, x1, rope_d[:, t], ALU.add)
                        ins.then_inc(roped, 1)

            for g in range(4):
                for q in range(8):
                    split(QKV_C + 8 * g + q)
                    if g == 0 and q == 2:
                        glu_out(3)
                    if g >= 1:
                        qk_slot(q, g - 1)
            split(GATE_C)
            split(GATE_C + 1)
            dve.wait_ge(chunk_used, used(QKV_C + 31))
            add_bias(3, V_COL)

            def kq_evac(g):
                for b in range(3):
                    dve.wait_ge(kq_high_ready, 3 * g + b + 1)
                    dve.tensor_tensor(kq_low[:, b, :], bank[5 + b][:, :], kq_high[:, b, :].bitcast(F32),
                                      ALU.subtract).then_inc(kq_low_ready, 1)

            def v_split(g):
                dve.wait_ge(v_high_ready, g + 1)
                dve.tensor_tensor(v_low[:, :, :], qkv[:, :, V_COL + g * HD:V_COL + (g + 1) * HD],
                                  v_high[:, :, :].bitcast(F32), ALU.subtract).then_inc(v_low_ready, 1)

            def maxima(h):
                for t in range(TT):
                    n = 4 * h + t
                    dve.wait_ge(scores_ready, n + 1)
                    step(dve.tensor_reduce(neg_max[:, n:n + 1], bank[t][:, :], AX.X, ALU.max, negate=True))
                    dve.tensor_scalar(exp_bias[:, n:n + 1], neg_max[:, n:n + 1], float(HD) ** -0.5, None,
                                      ALU.mult).then_inc(exp_bias_ready, 1)

            def normalise(h):
                for t in range(TT):
                    n = 4 * h + t
                    dve.wait_ge(exp_ready, n + 1)
                    step(dve.reciprocal(row_inv[:, n:n + 1], row_sum[:, n:n + 1]))
                    dve.tensor_scalar(probs[:, h % 2, t, :], probs[:, h % 2, t, :], row_inv[:, n:n + 1], None,
                                      ALU.mult).then_inc(probs_ready, 1)

            def pt_evac(h):
                for k in range(TT):
                    dve.wait_ge(pt_high_ready, 4 * h + k + 1)
                    dve.tensor_tensor(pt_low[:, k, :], bank[4 + k][:, :], pt_high[:, k, :].bitcast(F32),
                                      ALU.subtract).then_inc(pt_low_ready, 1)

            kq_evac(0)
            v_split(0)
            maxima(0)
            normalise(0)
            for h in range(HEADS):
                if h + 1 < HEADS:
                    maxima(h + 1)
                if h % 2 == 0 and h > 0:
                    v_split(h // 2)
                pt_evac(h)
                if h + 1 < HEADS:
                    normalise(h + 1)
                if h % 2 == 0 and h // 2 + 1 < KV_HEADS:
                    kq_evac(h // 2 + 1)

            def centre(i):
                return conv[:, i, REACH:REACH + SEQ]

            def conv_taps(i, k0, k1):
                w0 = COL["conv_w"] + i * CONV_K
                for k in range(k0, k1):
                    if k == 0:
                        step(dve.tensor_scalar(vec_acc[:, :], conv[:, i, 0:SEQ], par[:, w0:w0 + 1],
                                               col("conv_b", i), ALU.mult, ALU.add))
                    elif k < CONV_K:
                        step(dve.scalar_tensor_tensor(out=vec_acc[:, :], in0=conv[:, i, k:k + SEQ],
                                                      scalar=par[:, w0 + k:w0 + k + 1], in1=vec_acc[:, :],
                                                      op0=ALU.mult, op1=ALU.add))
                    else:
                        dve.tensor_copy(centre(i), vec_acc[:, :]).then_inc(vec_conv_done, 1)
                        dve.wait_ge(vec_conv_done, i - POOL_CONV_TILES + 1)

            def oc_low(n):
                dve.wait_ge(oc_high_ready, n + 1)
                k = 4 * (n % 2)
                if n < 2:
                    low, high, full = o_low, o_high, o_full[:, k:k + 4, :]
                else:
                    low, high, full = c_low, c_high, conv[:, k:k + 4, REACH:REACH + SEQ]
                dve.tensor_tensor(low[:, k:k + 4, :], full, high[:, k:k + 4, :].bitcast(F32),
                                  ALU.subtract).then_inc(oc_low_ready, 1)

            dve.wait_ge(o_ready, HEADS)
            for g in range(8):
                for q in range(8):
                    if g > 0 or q > 1:
                        split(GATE_C + 8 * g + q)
                    if g < KC - POOL_CONV_TILES:
                        conv_taps(POOL_CONV_TILES + g, 4 * q, 4 * q + 4)
                    if g == 5 and q == 1:
                        dve.wait_ge(mean_ready, 1)
                        dve.tensor_copy(mean_sb[:, :], bank[7][:, :]).then_inc(mean_copied, 1)
                        dve.wait_ge(mean_copied, 1)
                    if g == 5 and 2 <= q <= 5:
                        for i in (2 * (q - 2), 2 * (q - 2) + 1):
                            dve.tensor_tensor(centre(i), centre(i), mean_sb[:, :],
                                              ALU.subtract).then_inc(centred, 1)
                    if g == 6 and q == 1:
                        dve.wait_ge(var_ready, 1)
                        dve.tensor_scalar(var_sb[:, :], bank[3][:, :], EPS, None, ALU.add).then_inc(var_copied, 1)
                    if g == 6 and 3 <= q <= 6:
                        for i in (2 * (q - 3), 2 * (q - 3) + 1):
                            dve.wait_ge(ln_rstd_ready, 1)
                            dve.tensor_tensor(centre(i), centre(i), ln_rstd[:, :],
                                              ALU.mult).then_inc(c_normed, 1)
                    if g == 7 and q >= 6:
                        oc_low(q - 6)

            def mix_slot(q, g, i=None):
                if q not in (1, 2):
                    return
                b, s = q - 1, 4 * (g % 2)
                j = val(2 * g + b, i, 4)
                if b == 0:
                    dve.wait_ge(chunk_used, used(MIX_C + 4 * g + 3, i, 8))
                    if g > 0:
                        dve.wait_ge(m_ready, val(2 * g, i, 4))
                for mixed, gate, ps in ((mix_a, gate_a, bank[s + b]), (mix_c, gate_c, bank[s + 2 + b])):
                    ins = dve.tensor_tensor(mixed[:, b, :], ps[:, :],
                                            gate[:, bass.ds(j, 1), :].rearrange("p a n -> p (a n)"), ALU.mult)
                ins.then_inc(mix_gated if b == 0 else group_freed, 1)

            for g in range(2):
                for q in range(4):
                    split(MIX_C + 4 * g + q)
                    if g == 0 and q < 2:
                        oc_low(2 + q)
                    if g == 1:
                        if q == 1:
                            dve.wait_ge(gate_stored, 8 + 4 * 8)
                        mix_slot(q, 0)
            with dve.Fori(0, 3) as i:
                for g in (1, 2):
                    for q in range(4):
                        split(MIX_C + 4 * g + 4 + q, i, 8)
                        mix_slot(q, g, i)

            def out_slot(q, g):
                if q in (1, 2):
                    dve.wait_ge(chunk_used, used(OUT_C + 8 * g + 7))
                    dve.wait_ge(xres_loaded, 16 * TT)
                    for t in (2 * q - 2, 2 * q - 1):
                        piece = x_res[:, t, 512 * g:512 * g + 512]
                        ins = dve.tensor_tensor(piece, piece, bank[4 * (g % 2) + t][:, :], ALU.add)
                    if q == 2:
                        ins.then_inc(group_freed, 1)

            for g in range(4):
                for q in range(8):
                    split(OUT_C + 8 * g + q)
                    if g == 0:
                        mix_slot(q, 7)
                    else:
                        out_slot(q, g - 1)
            split(FFN_C)
            split(FFN_C + 1)
            for q in (1, 2):
                out_slot(q, 3)
            dve.wait_ge(group_freed, freed(OUT_G + 3))
            norm(1, x_res, "g_ffn")

            def up_slot(q, n, i=None):
                s = 4 * (n // 2 % 2)
                for b in range(2):
                    ft = val(n + b, i, 8)
                    gate = f_gate[:, b, :]
                    if q == 1:
                        dve.wait_ge(tap_mid_ready, ft + 1)
                        for tap, out, src, done in ((0, slice(1, SEQ), slice(0, SEQ - 1), tap_left_ready),
                                                    (2, slice(0, SEQ - 1), slice(1, SEQ), taps_ready)):
                            if tap == 2:
                                dve.wait_ge(tap_left_ready, ft + 1)
                            dve.scalar_tensor_tensor(out=gate[:, out], in0=bank[s + b][:, src],
                                                     scalar=par[:, bass.ds(ft * 3 + (COL["ffn_w"] + tap), 1)],
                                                     in1=gate[:, out], op0=ALU.mult, op1=ALU.add).then_inc(done, 1)
                    if q == 4:
                        dve.wait_ge(silu_ready, ft + 1)
                        if n >= 2:
                            dve.wait_ge(u_low_ready, val(n + b - 1, i, 8))
                        dve.tensor_tensor(f_u[:, b, :], gate, f_val[:, b, :], ALU.mult).then_inc(u_ready, 1)

            def down_out(r, q, i=None):
                dve.wait_ge(chunk_used, used(FFN_C + 32 + 24 * min(r, ROUNDS - 2)
                                             + 8 * (r == ROUNDS - 1) + 2 * q + 1, i, 48))
                if r > 0:
                    dve.wait_ge(down_freed, val(4 * r - 3 + q, i, 8))
                for t in range(TT):
                    piece = x_res[:, t, 512 * q:512 * q + 512]
                    ins = dve.tensor_tensor(piece, piece, bank[4 * (q % 2) + t][:, :], ALU.add)
                ins.then_inc(down_freed, 1)

            for q in range(2, 8):
                split(FFN_C + q)
            for g in range(1, 4):
                for q in range(8):
                    split(FFN_C + 8 * g + q)
                    up_slot(q, 2 * g - 2)

            def ffn_round(r, i=None):
                c = FFN_C + 32 + 24 * r
                for q in range(8):
                    split(c + q, i, 48)
                    up_slot(q, 4 * r + 6, i)
                    if q in (3, 5, 7):
                        down_out(r, (q - 3) // 2, i)
                for q in range(8):
                    split(c + 8 + q, i, 48)
                    if q == 1:
                        down_out(r, 3, i)
                for q in range(8):
                    split(c + 16 + q, i, 48)
                    up_slot(q, 4 * r + 8, i)

            with dve.Fori(0, (ROUNDS - 3) // 2) as i:
                ffn_round(0, i)
                ffn_round(1, i)
            ffn_round(ROUNDS - 3)
            c = FFN_C + 32 + 24 * (ROUNDS - 2)
            for q in range(16):
                split(c + q)
                if q < 8:
                    up_slot(q, KF - 2)
                if q in (3, 5, 7, 9):
                    down_out(ROUNDS - 2, (q - 3) // 2)
                if q in (11, 13, 15):
                    down_out(ROUNDS - 1, (q - 11) // 2)
            down_out(ROUNDS - 1, 3)
            dve.wait_ge(gfin_loaded, 16)
            dve.wait_ge(down_freed, 4 * ROUNDS)
            for t in range(TT):
                q = 2 * TT + t
                dve.wait_ge(squares_summed, q + 1)
                dve.tensor_scalar(meansq[:, q:q + 1], sumsq[:, q:q + 1], 1.0 / D, EPS, ALU.mult,
                                  ALU.add).then_inc(meansq_ready, 1)
                dve.wait_ge(rstd_ready, q + 1)
                dve.scalar_tensor_tensor(out=x_res[:, t, :], in0=x_res[:, t, :], scalar=rstd[:, q:q + 1],
                                         in1=g_fin[:, :], op0=ALU.mult, op1=ALU.mult).then_inc(y_ready, 1)

        @block.tensor
        def _(pe):
            def products(ps, a_high, a_low, b_high, b_low, first, last):
                pe.matmul(ps, a_high, b_high, start=first, stop=False)
                pe.matmul(ps, a_high, b_low, start=False, stop=False)
                return pe.matmul(ps, a_low, b_high, start=False, stop=last)

            def pair_group(c, s, high, low, chunks=4, i=None, per=0, before=(), high2=None, low2=None):
                for half in range(2):
                    xh, xl = (high, low) if half == 0 or high2 is None else (high2, low2)
                    for q in range(chunks):
                        n = c + half * chunks + q
                        pe.wait_ge(low_split, val(n + 1, i, per))
                        for waits in before[half * chunks + q:half * chunks + q + 1]:
                            for sem_, count in waits:
                                pe.wait_ge(sem_, count)
                        for kk in range(4):
                            k = 4 * q + kk
                            for b in range(2):
                                w = slice(256 * kk + P * b, 256 * kk + P * b + P)
                                ins = products(bank[s + 2 * half + b][:, :],
                                               w_high[:, n % N_SPLIT, w], w_low[:, n % N_SPLIT, w],
                                               xh[:, k, :], xl[:, k, :], k == 0, k == 4 * chunks - 1)
                        ins.then_inc(chunk_used, 1)

            def wide_group(c, s, high, low, chunks=8, i=None, per=0, before=None):
                for q in range(chunks):
                    n = c + q
                    pe.wait_ge(low_split, val(n + 1, i, per))
                    if before is not None:
                        pe.wait_ge(before, 2 * q + 2)
                    for kk in range(2):
                        k = 2 * q + kk
                        w = slice(512 * kk, 512 * kk + 512)
                        for t in range(TT):
                            tok = slice(P * t, P * t + P)
                            ins = products(bank[s + t][:, :], high[:, k, tok], low[:, k, tok],
                                           w_high[:, n % N_SPLIT, w], w_low[:, n % N_SPLIT, w],
                                           k == 0, k == 2 * chunks - 1)
                    ins.then_inc(chunk_used, 1)

            def turn(w):
                for t in range(TT):
                    pe.wait_ge(xs_ready, 4 * w + t + 1)
                    for kq in range(4):
                        n = 16 * w + 4 * t + kq
                        if n % 16 >= 8:
                            pe.wait_ge(xg_ready, n - 7)
                        for k in range(4):
                            ch = slice(P * (4 * kq + k), P * (4 * kq + k + 1))
                            ins = pe.transpose(bank[n % 8][:, P * k:P * k + P], x_scaled[:, t, ch], ident[:, :])
                        ins.then_inc(x_turned, 1)

            pe.wait_ge(consts_made, 5)
            turn(0)
            pe.wait_ge(h_low_ready, 16)
            with pe.Fori(0, 2) as i:
                for g in range(2):
                    pe.wait_ge(group_freed, i * 2 + freed(GLU_G + g - 2))
                    pair_group(GLU_C + 8 * g, 4 * g, h_high, h_low, 4, i, 16)
            with pe.Fori(0, 2) as i:
                for g in range(2):
                    pe.wait_ge(group_freed, i * 2 + freed(QKV_G + g - 2))
                    wide_group(QKV_C + 8 * g, 4 * g, h_high, h_low, 8, i, 16)

            def turn_kq(g):
                for b, c0 in enumerate((K_COL + g * HD, Q_COL + 2 * g * HD, Q_COL + (2 * g + 1) * HD)):
                    for t in range(TT):
                        ins = pe.transpose(bank[5 + b][:, P * t:P * t + P], qkv[:, t, c0:c0 + HD], ident[:, :])
                    ins.then_inc(kq_turned, 1)

            def scores(h):
                pe.wait_ge(kq_low_ready, 3 * (h // 2 + 1))
                b = 1 + h % 2
                for t in range(TT):
                    if h >= 1:
                        pe.wait_ge(exp_ready, 4 * (h - 1) + t + 1)
                    tok = slice(P * t, P * t + P)
                    products(bank[t][:, :], kq_high[:, b, tok], kq_low[:, b, tok],
                             kq_high[:, 0, :], kq_low[:, 0, :], True, True).then_inc(scores_ready, 1)

            def turn_probs(h):
                pe.wait_ge(probs_ready, 4 * h + 4)
                if h >= 1:
                    pe.wait_ge(o_ready, h)
                if h % 2 == 1:
                    pe.wait_ge(kq_low_ready, min(3 * (h // 2 + 2), 3 * KV_HEADS))
                for k in range(TT):
                    for t in range(TT):
                        ins = pe.transpose(bank[4 + k][:, P * t:P * t + P],
                                           probs[:, h % 2, t, P * k:P * k + P], ident[:, :])
                    ins.then_inc(probs_turned, 1)

            def weighted_sum(h):
                pe.wait_ge(v_low_ready, h // 2 + 1)
                pe.wait_ge(pt_low_ready, 4 * h + 4)
                for k in range(TT):
                    ins = products(bank[4][:, :], v_high[:, k, :], v_low[:, k, :],
                                   pt_high[:, k, :], pt_low[:, k, :], k == 0, k == TT - 1)
                ins.then_inc(o_summed, 1)

            pe.wait_ge(roped, 3)
            pe.wait_ge(group_freed, freed(QKV_G + 3))
            turn_kq(0)
            scores(0)
            for h in range(HEADS):
                if h + 1 < HEADS:
                    scores(h + 1)
                turn_probs(h)
                weighted_sum(h)
                if h % 2 == 0 and h // 2 + 1 < KV_HEADS:
                    turn_kq(h // 2 + 1)

            with pe.Fori(0, 2) as i:
                for g in range(2):
                    pe.wait_ge(gate_stored, i * 8 + (4 * g + 4))
                    pair_group(GATE_C + 8 * g, 4 * g, h_high, h_low, 4, i, 16)
            pe.wait_ge(gate_stored, 8 + 4 * 3)
            pair_group(GATE_C + 32, 0, h_high, h_low)
            pe.wait_ge(gate_stored, 8 + 4 * 4)
            pe.wait_ge(ch_sum_ready, 1)
            pe.matmul(bank[7][:, :], mean_w[:, :], ch_sum[:, :], start=True, stop=True).then_inc(mean_ready, 1)
            pair_group(GATE_C + 40, 4, h_high, h_low, before=[()] * 4 + [((mean_copied, 1),)])
            pe.wait_ge(gate_stored, 8 + 4 * 5)
            pe.wait_ge(ch_sq_added, KC)
            pe.matmul(bank[3][:, :], mean_w[:, :], sq_sum[:, :], start=True, stop=True).then_inc(var_ready, 1)
            pair_group(GATE_C + 48, 0, h_high, h_low, before=[()] * 4 + [((var_copied, 1),)])
            pe.wait_ge(gate_stored, 8 + 4 * 6)
            pair_group(GATE_C + 56, 4, h_high, h_low)

            with pe.Fori(0, 4) as i:
                for g in range(2):
                    pe.wait_ge(gate_stored, 8 + 4 * (7 + g))
                    pe.wait_ge(group_freed, i * 2 + freed(MIX_G + g - 2))
                    pair_group(MIX_C + 4 * g, 4 * g, o_high, o_low, 2, i, 8,
                               [((oc_low_ready, n + 1),) for n in range(4)], c_high, c_low)
            with pe.Fori(0, 2) as i:
                for g in range(2):
                    pe.wait_ge(group_freed, i * 2 + freed(OUT_G + g - 2))
                    wide_group(OUT_C + 8 * g, 4 * g, m_high, m_low, 8, i, 16, m_low_ready)

            turn(1)
            pe.wait_ge(h_low_ready, 32)
            for g in range(4):
                if g >= 2:
                    pe.wait_ge(taps_ready, 2 * g - 2)
                    pe.wait_ge(val_saved, 2 * g - 2)
                pair_group(FFN_C + 8 * g, 4 * (g % 2), h_high, h_low)

            def down(r, c, i=None):
                pe.wait_ge(u_low_ready, val(4 * r + 4, i, 8))
                for q in range(4):
                    if q < 2 and r < ROUNDS - 1:
                        n = 4 * r + 6 + 2 * q
                        pe.wait_ge(taps_ready, val(n, i, 8))
                        pe.wait_ge(val_saved, val(n, i, 8))
                    else:
                        pe.wait_ge(down_freed, val(4 * r + q - 1, i, 8))
                    wide_group(c + 2 * q, 4 * (q % 2), u_high[:, r % 2], u_low[:, r % 2], 2, i, 48)

            def ffn_round(r, i=None):
                c = FFN_C + 32 + 24 * r
                down(r, c, i)
                for a in range(2):
                    pe.wait_ge(down_freed, val(4 * r + 3 + a, i, 8))
                    pair_group(c + 8 + 8 * a, 4 * a, h_high, h_low, 4, i, 48)

            with pe.Fori(0, (ROUNDS - 3) // 2) as i:
                ffn_round(0, i)
                ffn_round(1, i)
            ffn_round(ROUNDS - 3)
            c = FFN_C + 32 + 24 * (ROUNDS - 2)
            down(ROUNDS - 2, c)
            down(ROUNDS - 1, c + 8)


def rope_tables():
    f32 = np.float32
    rows = SEQ // GRID_W
    row = np.repeat(np.arange(rows), GRID_W).astype(f32)
    column = np.tile(np.arange(GRID_W), rows).astype(f32)
    inv_freq = f32(ROPE_THETA) ** (-np.arange(0, HD // 2, 2, dtype=f32) / f32(HD // 2))
    angle = np.concatenate([row[:, None] * inv_freq, column[:, None] * inv_freq], axis=-1).astype(f32)
    return np.stack([np.cos(angle), np.sin(angle)]).astype(f32)


def kernel(x, norm_mix_g, w_in, b_in, q_norm_g, k_norm_g, w_attn_o, conv_dw_w, conv_dw_b, conv_ln_g,
           conv_ln_b, w_conv_o, w_out, norm_ffn_g, w_ffn_up, ffn_dw_w, ffn_dw_b, w_ffn_down, norm_final_g):
    import concourse.bacc as bacc
    from concourse.bass_utils import run_bass_kernel_spmd

    def tiles(v):
        return np.asarray(v).reshape(-1, P).T

    def taps(w):
        w = np.asarray(w)
        return w.reshape(w.shape[0], -1, P).transpose(2, 1, 0).reshape(P, -1)

    b = np.asarray(b_in)[0]
    cols = np.concatenate([
        tiles(norm_mix_g[0]), tiles(norm_ffn_g[0]), tiles(b[GLU_COL:GATE_COL]), tiles(b[GATE_COL:]),
        tiles(conv_dw_b[0]), tiles(conv_ln_g[0]), tiles(conv_ln_b[0]), taps(conv_dw_w[0]),
        taps(ffn_dw_w[0]), tiles(ffn_dw_b[0])], axis=1)
    rope = rope_tables().reshape(2, TT, P, HD // 2).transpose(2, 0, 1, 3)
    arrays = {
        "x_dram": np.asarray(x)[0], "w_in_dram": np.asarray(w_in)[0],
        "w_attn_o_dram": np.asarray(w_attn_o)[0], "w_conv_o_dram": np.asarray(w_conv_o)[0],
        "w_out_dram": np.asarray(w_out)[0], "w_up_dram": np.asarray(w_ffn_up)[0],
        "w_down_dram": np.asarray(w_ffn_down)[0], "cols_dram": cols, "b_qkv_dram": b[:GLU_COL],
        "qk_g_dram": np.stack([np.asarray(q_norm_g)[0], np.asarray(k_norm_g)[0]]),
        "g_final_dram": np.asarray(norm_final_g), "rope_dram": rope,
    }
    arrays = {name: np.ascontiguousarray(a) for name, a in arrays.items()}
    nc = bacc.Bacc("TRN2", target_bir_lowering=False, num_devices=1, dynamic_dma_scratch_size=1024)
    ins = [nc.dram_tensor(name, a.shape, mybir.dt.from_np(a.dtype), kind="ExternalInput").ap()
           for name, a in arrays.items()]
    y = nc.dram_tensor("y_dram", (SEQ, D), F32, kind="ExternalOutput").ap()
    build(nc, *ins, y)
    result = run_bass_kernel_spmd(nc, [arrays], core_ids=[0])
    return result.results[0]["y_dram"].reshape(1, SEQ, D)
```

```python
from contextlib import ExitStack
from functools import partial

import numpy as np

import concourse.bass as bass
import concourse.mybir as mybir

ACT = mybir.ActivationFunctionType
ALU = mybir.AluOpType
AX = mybir.AxisListType
F32 = mybir.dt.float32
F32R = mybir.dt.float32r

P = 128
SEQ = 512
D = 2048
HEADS = 8
KV_HEADS = 4
HD = 128
CONV_CH = 1024
CONV_K = 31
FFN = 5632
FFN_K = 3
GRID_W = 64
ROPE_THETA = 10000.0
EPS = 1e-6

TT = SEQ // P
KD = D // P
KC = CONV_CH // P
KA = HEADS
KF = FFN // P
ROUNDS = KF // 4
ATTN_Q = HEADS * HD
ATTN_KV = KV_HEADS * HD
Q_COL = 0
K_COL = ATTN_Q
V_COL = ATTN_Q + ATTN_KV
GLU_COL = ATTN_Q + 2 * ATTN_KV
GATE_COL = GLU_COL + 2 * CONV_CH
PADDED = SEQ + 32
REACH = CONV_K // 2
POOL_CONV_TILES = 4

COL = {}
_at = 0
for _name, _n in (("g_mix", KD), ("g_ffn", KD), ("b_glu", 2 * KC), ("b_gate", 2 * KD), ("conv_b", KC),
                  ("ln_g", KC), ("ln_b", KC), ("conv_w", KC * CONV_K), ("ffn_w", KF * FFN_K), ("ffn_b", KF)):
    COL[_name] = _at
    _at += _n
N_COLS = _at

GLU_C = 0
QKV_C = GLU_C + 4 * 8
GATE_C = QKV_C + 4 * 8
MIX_C = GATE_C + 8 * 8
OUT_C = MIX_C + 8 * 4
FFN_C = OUT_C + 4 * 8
GLU_G, QKV_G, GATE_G, MIX_G, OUT_G, FFN_G = 0, 4, 8, 16, 24, 28
DOWN_G = FFN_G + 4
N_RAW = 4
N_SPLIT = 2


def val(const, i=None, per=0):
    return const if i is None else i * per + const


def build(nc, x, w_in, w_attn_o, w_conv_o, w_out, w_up, w_down, cols, b_qkv, qk_g, g_final, rope, y):
    ctx = ExitStack()
    with ctx:
        base = (nc.sbuf_base + 63) // 32 * 32
        cursor = [base]

        def at(name, shape, dt, offset):
            return nc.alloc_sbuf_tensor_at(name, [P] + shape, dt, offset=offset)

        def region(nbytes):
            o = cursor[0]
            cursor[0] += (nbytes + 31) // 32 * 32
            return o

        KB = 1024
        r_ring = region(32 * KB)
        r_act = region(64 * KB)
        r_mix = region(64 * KB)
        r_conv = region(KC * PADDED * 4)
        r_o = region(16 * KB)
        r_cols = region(N_COLS * 4)
        r_ident = region(512)
        r_mean_w = region(512)
        r_qkg = region(1024)
        r_rope = region(2048)
        r_rstd_all = region(2048)
        r_small = region(1792)
        r_work = region(20 * KB)
        assert cursor[0] <= nc.sbuf_top, (cursor[0], nc.sbuf_top)

        w_raw = at("w_raw", [N_RAW, 1024], F32, r_ring)
        w_high = at("w_high", [N_SPLIT, 1024], F32R, r_ring + 16 * KB)
        w_low = at("w_low", [N_SPLIT, 1024], F32R, r_ring + 24 * KB)
        h_high = at("h_high", [KD, SEQ], F32R, r_act)
        h_low = at("h_low", [KD, SEQ], F32R, r_act + 32 * KB)
        o_high = at("o_high", [KA, SEQ], F32R, r_act)
        o_low = at("o_low", [KA, SEQ], F32R, r_act + 32 * KB)
        c_high = at("c_high", [KC, SEQ], F32R, r_act + 16 * KB)
        c_low = at("c_low", [KC, SEQ], F32R, r_act + 48 * KB)
        x_in = at("x_in", [TT, D], F32, r_mix)
        glu_gate = at("glu_gate", [2, SEQ], F32, r_mix + 32 * KB)
        qkv = at("qkv", [TT, D], F32, r_mix)
        qk_sq = at("qk_sq", [TT * 4, HD], F32, r_mix + 40 * KB)
        rope_a = at("rope_a", [TT, 4, HD // 2], F32, r_mix + 48 * KB)
        rope_b = at("rope_b", [TT, 4, HD // 2], F32, r_mix + 52 * KB)
        rope_d = at("rope_d", [TT, 4, HD // 2], F32, r_mix + 56 * KB)
        probs = at("probs", [2, TT, SEQ], F32, r_mix + 32 * KB)
        pt_high = at("pt_high", [TT, SEQ], F32R, r_mix + 48 * KB)
        pt_low = at("pt_low", [TT, SEQ], F32R, r_mix + 56 * KB)
        gate_a = at("gate_a", [KD, SEQ], F32, r_mix)
        gate_c = at("gate_c", [KD, SEQ], F32, r_mix + 32 * KB)
        m_high = at("m_high", [KD, SEQ], F32R, r_mix)
        m_low = at("m_low", [KD, SEQ], F32R, r_mix + 32 * KB)
        u_high = at("u_high", [2, 4, SEQ], F32R, r_mix)
        u_low = at("u_low", [2, 4, SEQ], F32R, r_mix + 16 * KB)
        g_fin = at("g_fin", [D], F32, r_mix + 32 * KB)
        y_junk = at("y_junk", [D], F32, r_mix + 40 * KB)
        f_raw = at("f_raw", [2, SEQ], F32, r_mix + 48 * KB)
        conv = at("conv", [KC, PADDED], F32, r_conv)
        b_qkv_all = at("b_qkv_all", [D], F32, r_o)
        o_full = at("o_full", [KA, SEQ], F32, r_o)
        x_res = at("x_res", [TT, D], F32, r_conv)
        par = at("par", [N_COLS], F32, r_cols)
        ident = at("ident", [P], F32, r_ident)
        mean_w = at("mean_w", [P], F32, r_mean_w)
        qkg = at("qkg", [2, HD], F32, r_qkg)
        rstd_all = at("rstd_all", [SEQ], F32, r_rstd_all)
        rope_cs = at("rope_cs", [2, TT, HD // 2], F32, r_rope)
        small = [r_small]

        def tiny(name, n):
            t = at(name, [n], F32, small[0])
            small[0] += (n * 4 + 31) // 32 * 32
            return t

        sq_part = tiny("sq_part", 2 * 16)
        sumsq = tiny("sumsq", 3 * TT)
        meansq = tiny("meansq", 3 * TT)
        rstd = tiny("rstd", 3 * TT)
        neg_half = tiny("neg_half", 1)
        qk_ss = tiny("qk_ss", 16)
        qk_ms = tiny("qk_ms", 16)
        qk_root = tiny("qk_root", 16)
        qk_r0 = tiny("qk_r0", 16)
        qk_t = tiny("qk_t", 16)
        qk_rstd = tiny("qk_rstd", 16)
        neg_max = tiny("neg_max", 4 * HEADS)
        exp_bias = tiny("exp_bias", 4 * HEADS)
        row_sum = tiny("row_sum", 4 * HEADS)
        row_inv = tiny("row_inv", 4 * HEADS)
        assert small[0] - r_small <= 1792
        sq_junk = at("sq_junk", [SEQ], F32, r_work + 16 * KB)
        qkv_high = at("qkv_high", [TT, D], F32R, r_mix)
        kq_low = at("kq_low", [2, 3, SEQ], F32R, r_work)
        v_high = at("v_high", [TT, HD], F32R, r_work + 12 * KB)
        v_low = at("v_low", [TT, HD], F32R, r_work + 14 * KB)
        pool_acc = at("pool_acc", [SEQ], F32, r_work + 16 * KB)
        pool_tap = at("pool_tap", [SEQ], F32, r_work + 18 * KB)
        vec_acc = at("vec_acc", [SEQ], F32, r_work)
        ch_sum = at("ch_sum", [SEQ], F32, r_work + 2 * KB)
        mean_sb = at("mean_sb", [SEQ], F32, r_work + 4 * KB)
        ch_sq = at("ch_sq", [2, SEQ], F32, r_work + 6 * KB)
        sq_sum = at("sq_sum", [SEQ], F32, r_work + 10 * KB)
        var_sb = at("var_sb", [SEQ], F32, r_work + 12 * KB)
        ln_rstd = at("ln_rstd", [SEQ], F32, r_work + 14 * KB)
        mix_a = at("mix_a", [2, SEQ], F32, r_work)
        mix_c = at("mix_c", [2, SEQ], F32, r_work + 4 * KB)
        mix_m = at("mix_m", [2, SEQ], F32, r_work + 8 * KB)
        f_gate = at("f_gate", [2, SEQ], F32, r_work + 8 * KB)
        f_val = at("f_val", [2, SEQ], F32, r_work + 12 * KB)
        f_u = at("f_u", [2, SEQ], F32, r_work + 16 * KB)

        bank = [ctx.enter_context(nc.psum_tensor(f"bank{b}", [P, 512], F32)) for b in range(8)]

        def sem(name):
            return ctx.enter_context(nc.semaphore(name))

        chunk_loaded = [sem(f"chunk_loaded{s}") for s in range(N_RAW)]
        high_split = sem("high_split")
        low_split = sem("low_split")
        chunk_used = sem("chunk_used")
        group_freed = sem("group_freed")
        x_loaded = [sem(f"x_loaded{t}") for t in range(TT)]
        xres_loaded = sem("xres_loaded")
        par_loaded = sem("par_loaded")
        qkv_par_loaded = sem("qkv_par_loaded")
        consts_made = sem("consts_made")
        squares_summed = sem("squares_summed")
        meansq_ready = sem("meansq_ready")
        rstd_ready = sem("rstd_ready")
        x_turned = sem("x_turned")
        rstd_spread = sem("rstd_spread")
        rstd_copied = sem("rstd_copied")
        h_high_ready = sem("h_high_ready")
        h_low_ready = sem("h_low_ready")
        glu_scaled = sem("glu_scaled")
        glu_gate_ready = sem("glu_gate_ready")
        glu_done = sem("glu_done")
        pool_step = sem("pool_step")
        vec_step = sem("vec_step")
        vec_conv_done = sem("vec_conv_done")
        pool_conv_done = sem("pool_conv_done")
        ch_sum_ready = sem("ch_sum_ready")
        mean_ready = sem("mean_ready")
        mean_copied = sem("mean_copied")
        centred = sem("centred")
        ch_sq_ready = sem("ch_sq_ready")
        ch_sq_added = sem("ch_sq_added")
        var_ready = sem("var_ready")
        var_copied = sem("var_copied")
        ln_root_ready = sem("ln_root_ready")
        c_normed = sem("c_normed")
        c_swished = sem("c_swished")
        qk_squared = sem("qk_squared")
        qk_ms_ready = sem("qk_ms_ready")
        qk_root_ready = sem("qk_root_ready")
        roped = sem("roped")
        kq_turned = sem("kq_turned")
        kq_high_ready = sem("kq_high_ready")
        kq_low_ready = sem("kq_low_ready")
        v_high_ready = sem("v_high_ready")
        v_low_ready = sem("v_low_ready")
        scores_ready = sem("scores_ready")
        exp_bias_ready = sem("exp_bias_ready")
        exp_ready = sem("exp_ready")
        probs_ready = sem("probs_ready")
        probs_turned = sem("probs_turned")
        pt_high_ready = sem("pt_high_ready")
        pt_low_ready = sem("pt_low_ready")
        o_summed = sem("o_summed")
        o_ready = sem("o_ready")
        gate_scaled = sem("gate_scaled")
        gate_stored = sem("gate_stored")
        oc_high_ready = sem("oc_high_ready")
        oc_low_ready = sem("oc_low_ready")
        mix_gated = sem("mix_gated")
        m_ready = sem("m_ready")
        m_high_ready = sem("m_high_ready")
        m_low_ready = sem("m_low_ready")
        tap_mid_ready = sem("tap_mid_ready")
        tap_left_ready = sem("tap_left_ready")
        up_scaled = sem("up_scaled")
        taps_ready = sem("taps_ready")
        silu_ready = sem("silu_ready")
        u_ready = sem("u_ready")
        u_high_ready = sem("u_high_ready")
        u_low_ready = sem("u_low_ready")
        gfin_loaded = sem("gfin_loaded")
        y_ready = sem("y_ready")
        y_stored = sem("y_stored")

        def freed(group, i=None, per=0):
            return val(group + 1, i, per)

        def used(c, i=None, per=0):
            return val(c + 1, i, per)

        def chunk_slot(c):
            return c % N_RAW, 16 * (c // N_RAW + 1)

        def col(name, n=0, width=1):
            a = COL[name] + n
            return par[:, a:a + width]

        def head_cols(g):
            return K_COL + g * HD, Q_COL + 2 * g * HD, Q_COL + (2 * g + 1) * HD

        def pt_bank(h, k):
            return 4 + (h + k) % 4

        def kq_bank(g, b):
            return 5 + b if g < 2 else pt_bank(2 * g - 3, b)

        wi = w_in.rearrange("(k p) n -> p k n", p=P)
        wu = w_up.rearrange("(k p) n -> p k n", p=P)
        wd = w_down.rearrange("(k p) n -> p k n", p=P)
        wo = w_out.rearrange("(k p) n -> p k n", p=P)
        wa = w_attn_o.rearrange("(k p) n -> p k n", p=P)
        wc = w_conv_o.rearrange("(k p) n -> p k n", p=P)
        x_tiles = x.rearrange("(t p) d -> t p d", p=P)
        y_tiles = y.rearrange("(t p) d -> t p d", p=P)

        block = ctx.enter_context(nc.Block())

        @block.sync
        def _(sp):
            def load(c, src, i=None, per=0):
                slot, landed = chunk_slot(c)
                if c >= N_RAW or i is not None:
                    sp.wait_ge(low_split, val(c - N_RAW + 1, i, per))
                dst = w_raw[:, slot, :].rearrange("p (k n) -> p k n", k=src.shape[1])
                sp.dma_start(dst, src).then_inc(chunk_loaded[slot], 16)

            def load_pair(c, src_a, src_b, col_a, col_b, chunks, i=None, per=0):
                for half, (src, c0) in enumerate(((src_a, col_a), (src_b, col_b))):
                    for q in range(chunks):
                        load(c + half * chunks + q, src[:, 4 * q:4 * q + 4, bass.ds(c0, 256)], i, per)

            def load_wide(c, src, col0, i=None, per=0):
                for q in range(8):
                    load(c + q, src[:, 2 * q:2 * q + 2, bass.ds(col0, 512)], i, per)

            x_by_token = x.rearrange("(t p) d -> p t d", p=P)
            for n in range(4):
                part = slice(512 * n, 512 * n + 512)
                sp.dma_start(x_in[:, :, part], x_by_token[:, :, part]).then_inc(x_loaded[n], 16)
                if n in (0, 1):
                    load(GLU_C + n, wi[:, 4 * n:4 * n + 4, GLU_COL:GLU_COL + 256])
            for q in range(2, 8):
                c0 = GLU_COL + CONV_CH * (q // 4)
                load(GLU_C + q, wi[:, 4 * (q % 4):4 * (q % 4) + 4, c0:c0 + 256])
            with sp.Fori(0, 3) as i:
                load_pair(GLU_C + 8, wi, wi, i * 256 + (GLU_COL + 256),
                          i * 256 + (GLU_COL + CONV_CH + 256), 4, i, 8)
            load_wide(QKV_C, wi, K_COL)
            with sp.Fori(0, 2) as i:
                load_wide(QKV_C + 8, wi, i * 512 + Q_COL, i, 8)
            load_wide(QKV_C + 24, wi, V_COL)
            with sp.Fori(0, 8) as i:
                load_pair(GATE_C, wi, wi, i * 256 + GATE_COL, i * 256 + (GATE_COL + D), 4, i, 8)
            with sp.Fori(0, 8) as i:
                load_pair(MIX_C, wa, wc, i * 256, i * 256, 2, i, 4)
            sp.wait_ge(oc_low_ready, 4)
            for t in range(TT):
                sp.dma_start(x_res[:, t, :], x_tiles[t]).then_inc(xres_loaded, 16)
            with sp.Fori(0, 4) as i:
                load_wide(OUT_C, wo, i * 512, i, 8)
            for a in range(4):
                load_pair(FFN_C + 8 * a, wu, wu, 256 * a, FFN + 256 * a, 4)

            def load_down(c, r, i=None, per=0):
                for q in range(4):
                    for k in range(2):
                        src = wd[:, bass.ds(r + 2 * k, 2), 512 * q:512 * q + 512]
                        load(c + 2 * q + k, src, i, per)

            with sp.Fori(0, ROUNDS - 2) as i:
                load_down(FFN_C + 32, i * 4, i, 24)
                for a in range(2):
                    load_pair(FFN_C + 40 + 8 * a, wu, wu, i * 512 + (1024 + 256 * a),
                              i * 512 + (FFN + 1024 + 256 * a), 4, i, 24)
            for k in range(2):
                r = ROUNDS - 2 + k
                load_down(FFN_C + 32 + 24 * (ROUNDS - 2) + 8 * k, 4 * r)
            for t in range(TT):
                sp.wait_ge(y_ready, t + 1)
                sp.dma_start(y_tiles[t], x_res[:, t, :]).then_inc(y_stored, 16)
            sp.wait_ge(y_stored, 16 * TT)

        @block.gpsimd
        def _(pool):
            steps = [0]

            def step(ins):
                ins.then_inc(pool_step, 1)
                steps[0] += 1
                pool.wait_ge(pool_step, steps[0])

            step(pool.memset(ident[:, :], 0.0))
            pool.affine_select(out=ident[:, :], in_=ident[:, :], compare_op=ALU.not_equal, fill=1.0,
                               base=0, pattern=[[-1, P]], channel_multiplier=1).then_inc(consts_made, 1)
            pool.memset(mean_w[:, :], 1.0 / CONV_CH).then_inc(consts_made, 1)
            pool.memset(neg_half[:, :], -0.5).then_inc(consts_made, 1)
            pool.memset(conv[:, :, 0:REACH], 0.0).then_inc(consts_made, 1)
            pool.memset(conv[:, :, REACH + SEQ:PADDED], 0.0).then_inc(consts_made, 1)
            pool.wait_ge(consts_made, 5)

            def root(w):
                pool.wait_ge(meansq_ready, w + 1)
                pool.tensor_tensor(rstd[:, TT * w:TT * w + TT], meansq[:, TT * w:TT * w + TT],
                                   neg_half[:, :].to_broadcast([P, TT]), ALU.pow).then_inc(rstd_ready, 1)

            root(0)

            def centre(i):
                return conv[:, i, REACH:REACH + SEQ]

            for i in range(POOL_CONV_TILES):
                if i % 2 == 0:
                    pool.wait_ge(glu_done, i + 2)
                if i == 0:
                    pool.wait_ge(par_loaded, 16)
                w0 = COL["conv_w"] + i * CONV_K
                step(pool.tensor_tensor(pool_acc[:, :], conv[:, i, 0:SEQ],
                                        par[:, w0:w0 + 1].to_broadcast([P, SEQ]), ALU.mult))
                for k in range(1, CONV_K):
                    step(pool.tensor_tensor(pool_tap[:, :], conv[:, i, k:k + SEQ],
                                            par[:, w0 + k:w0 + k + 1].to_broadcast([P, SEQ]), ALU.mult))
                    step(pool.tensor_tensor(pool_acc[:, :], pool_acc[:, :], pool_tap[:, :], ALU.add))
                step(pool.tensor_tensor(centre(i), pool_acc[:, :],
                                        col("conv_b", i).to_broadcast([P, SEQ]), ALU.add))
            pool.wait_ge(o_ready, HEADS)
            step(pool.tensor_tensor(ch_sum[:, :], centre(0), centre(1), ALU.add))
            for i in range(2, KC):
                if i >= POOL_CONV_TILES:
                    pool.wait_ge(vec_conv_done, i - POOL_CONV_TILES + 1)
                ins = pool.tensor_tensor(ch_sum[:, :], ch_sum[:, :], centre(i), ALU.add)
                if i < KC - 1:
                    step(ins)
                else:
                    ins.then_inc(ch_sum_ready, 1)
            pool.wait_ge(ch_sq_ready, 2)
            pool.tensor_tensor(sq_sum[:, :], ch_sq[:, 0, :], ch_sq[:, 1, :], ALU.add).then_inc(ch_sq_added, 2)
            for i in range(2, KC):
                pool.wait_ge(ch_sq_ready, i + 1)
                pool.wait_ge(ch_sq_added, i)
                pool.tensor_tensor(sq_sum[:, :], sq_sum[:, :], ch_sq[:, i % 2, :],
                                   ALU.add).then_inc(ch_sq_added, 1)
            def mix_tile(b, i):
                if b == 0:
                    pool.wait_ge(mix_gated, i + 1)
                else:
                    pool.wait_ge(group_freed, i + freed(MIX_G))
                pool.wait_ge(m_low_ready, i * 2)
                pool.tensor_tensor(mix_m[:, b, :], mix_a[:, b, :], mix_c[:, b, :],
                                   ALU.add).then_inc(m_ready, 1)

            def one(t, j):
                return t[:, bass.ds(j, 1), :].rearrange("p a n -> p (a n)")

            with pool.Fori(0, KD // 2) as i:
                for b in range(2):
                    mix_tile(b, i)
                for b in range(2):
                    pool.wait_ge(m_high_ready, i * 2 + (b + 1))
                    pool.tensor_tensor(one(m_low, i * 2 + b), mix_m[:, b, :],
                                       one(m_high, i * 2 + b).bitcast(F32),
                                       ALU.subtract).then_inc(m_low_ready, 1)
            root(1)

            def u_lows(n, i=None):
                buf, k = n // 4 % 2, n % 4
                for b in range(2):
                    pool.wait_ge(u_high_ready, val(n + b + 1, i, 8))
                    pool.tensor_tensor(u_low[:, buf, k + b, :], f_u[:, b, :],
                                       u_high[:, buf, k + b, :].bitcast(F32),
                                       ALU.subtract).then_inc(u_low_ready, 1)

            with pool.Fori(0, KF // 8) as i:
                for n in range(0, 8, 2):
                    u_lows(n, i)
            for n in range(KF // 8 * 8, KF, 2):
                u_lows(n)
            root(2)

        @block.scalar
        def _(act):
            act.dma_start(par[:, :], cols).then_inc(par_loaded, 16)

            def split(c, i=None, per=0):
                slot, landed = chunk_slot(c)
                act.wait_ge(chunk_loaded[slot], val(landed, i, per * 16 // N_RAW))
                if c >= N_SPLIT or i is not None:
                    act.wait_ge(chunk_used, val(c - N_SPLIT + 1, i, per))
                act.activation(w_high[:, c % N_SPLIT, :], w_raw[:, slot, :], ACT.Copy).then_inc(high_split, 1)

            def squares(w, n, src):
                for t in range(TT):
                    if w + n + t > 0:
                        act.wait_ge(squares_summed, 16 * w + 4 * n + t)
                    act.activation(sq_junk[:, :], src[:, t, 512 * n:512 * n + 512], ACT.Square,
                                   accum_out=sq_part[:, 16 * w + 4 * t + n:16 * w + 4 * t + n + 1]
                                   ).then_inc(squares_summed, 1)

            def turned_high(w, n, s):
                for k in range(4 * n, 4 * n + 4):
                    act.wait_ge(x_turned, KD * w + k + 1)
                    act.activation(h_high[:, k, :], bank[s + k % 4][:, :], ACT.Copy,
                                   scale=col("g_ffn" if w else "g_mix", k)).then_inc(h_high_ready, 1)

            def glu_sigmoid(g):
                for b in range(2):
                    act.wait_ge(glu_scaled, 2 * g + b + 1)
                    act.activation(glu_gate[:, b, :], glu_gate[:, b, :], ACT.Sigmoid,
                                   bias=col("b_glu", KC + 2 * g + b)).then_inc(glu_gate_ready, 1)

            act.wait_ge(par_loaded, 16)
            for g in range(4):
                for q in range(8):
                    if g == 0 and q in (0, 1):
                        split(GLU_C + q)
                    if g == 0 and q < 4:
                        turned_high(0, q, 4)
                    if g > 0 or q > 1:
                        split(GLU_C + 8 * g + q)
                    if g == 1 and q == 0:
                        for dst, src in ((qkg[:, :, :], qk_g.partition_broadcast(P)),
                                         (rope_cs[:, :, :, :], rope),
                                         (b_qkv_all[:, :], b_qkv.partition_broadcast(P))):
                            act.dma_start(dst, src).then_inc(qkv_par_loaded, 16)
                    if g == 0 and q >= 4:
                        act.wait_ge(x_loaded[q - 4], 16)
                        squares(0, q - 4, x_in)
                    if g >= 1 and q == 3:
                        glu_sigmoid(g - 1)

            qk_cols = (K_COL, Q_COL, Q_COL + 512)
            for g in range(4):
                for q in range(8):
                    split(QKV_C + 8 * g + q)
                    if g == 0 and q == 3:
                        glu_sigmoid(3)
                    if g >= 1 and q == 2:
                        act.wait_ge(group_freed, freed(QKV_G + g - 1))
                        if g >= 2:
                            act.wait_ge(qk_ms_ready, g - 1)
                        act.activation(qk_sq[:, :, :].rearrange("p (t h) d -> p t (h d)", t=TT),
                                       qkv[:, :, qk_cols[g - 1]:qk_cols[g - 1] + 512],
                                       ACT.Square).then_inc(qk_squared, 1)
                    if g >= 1 and q == 3:
                        act.wait_ge(qk_ms_ready, g)
                        act.activation(qk_root[:, :], qk_ms[:, :], ACT.Sqrt).then_inc(qk_root_ready, 1)
            split(GATE_C)
            split(GATE_C + 1)

            def kq_evac(g):
                for b, c0 in enumerate(head_cols(g)):
                    act.wait_ge(kq_turned, 3 * g + b + 1)
                    act.activation(qkv_high[:, :, c0:c0 + HD],
                                   bank[kq_bank(g, b)][:, :].rearrange("p (t d) -> p t d", t=TT),
                                   ACT.Copy).then_inc(kq_high_ready, 1)

            def v_split(g):
                if g == 0:
                    act.wait_ge(group_freed, freed(QKV_G + 3))
                else:
                    act.wait_ge(o_summed, 2 * g)
                act.activation(v_high[:, :, :], qkv[:, :, V_COL + g * HD:V_COL + (g + 1) * HD],
                               ACT.Copy).then_inc(v_high_ready, 1)

            def exps(h):
                for t in range(TT):
                    n = 4 * h + t
                    act.wait_ge(exp_bias_ready, n + 1)
                    if h >= 2:
                        act.wait_ge(probs_turned, 4 * (h - 1))
                    act.activation(probs[:, h % 2, t, :], bank[t][:, :], ACT.Exp, bias=exp_bias[:, n:n + 1],
                                   scale=float(HD) ** -0.5,
                                   accum_out=row_sum[:, n:n + 1]).then_inc(exp_ready, 1)

            def pt_evac(h):
                for k in range(TT):
                    act.wait_ge(probs_turned, 4 * h + k + 1)
                    act.activation(pt_high[:, k, :], bank[pt_bank(h, k)][:, :],
                                   ACT.Copy).then_inc(pt_high_ready, 1)

            kq_evac(0)
            v_split(0)
            exps(0)
            kq_evac(1)
            exps(1)
            for h in range(HEADS):
                pt_evac(h)
                if h + 2 < HEADS:
                    exps(h + 2)
                act.wait_ge(o_summed, h + 1)
                act.activation(o_full[:, h, :], bank[pt_bank(h, 0)][:, :], ACT.Copy).then_inc(o_ready, 1)
                if h in (0, 2):
                    kq_evac(h // 2 + 2)
                if h % 2 == 1 and h + 1 < HEADS:
                    v_split((h + 1) // 2)

            def gate_out(g, b):
                j = 2 * g + b
                if b == 0:
                    act.wait_ge(gate_scaled, g + 1)
                else:
                    act.wait_ge(group_freed, freed(GATE_G + g))
                for gate, c0 in ((gate_a, 0), (gate_c, KD)):
                    act.activation(gate[:, j, :], gate[:, j, :], ACT.Sigmoid,
                                   bias=col("b_gate", c0 + j)).then_inc(gate_stored, 1)

            def oc_high(n):
                act.wait_ge(chunk_used, used(GATE_C + 7 * 8 + 4 + n))
                if n < 2:
                    act.activation(o_high[:, 4 * n:4 * n + 4, :], o_full[:, 4 * n:4 * n + 4, :],
                                   ACT.Copy).then_inc(oc_high_ready, 1)
                else:
                    k = 4 * (n - 2)
                    act.wait_ge(c_swished, k + 4)
                    act.activation(c_high[:, k:k + 4, :], conv[:, k:k + 4, REACH:REACH + SEQ],
                                   ACT.Copy).then_inc(oc_high_ready, 1)

            def centre(i):
                return conv[:, i, REACH:REACH + SEQ]

            for g in range(8):
                for q in range(8):
                    if g > 0 or q > 1:
                        split(GATE_C + 8 * g + q)
                    if g >= 1 and q in (2, 3):
                        gate_out(g - 1, q - 2)
                    if g == 5 and 3 <= q <= 6:
                        for i in (2 * (q - 3), 2 * (q - 3) + 1):
                            act.wait_ge(centred, i + 1)
                            if i >= 2:
                                act.wait_ge(ch_sq_added, i - 1 if i > 2 else 2)
                            act.activation(ch_sq[:, i % 2, :], centre(i), ACT.Square).then_inc(ch_sq_ready, 1)
                    if g == 6 and q == 1:
                        act.wait_ge(var_copied, 1)
                        act.activation(ch_sq[:, 0, :], var_sb[:, :], ACT.Sqrt).then_inc(ln_root_ready, 1)
                    if (g == 6 and q >= 5) or (g == 7 and q == 0):
                        pair = (q - 5) % 8
                        for i in (2 * pair, 2 * pair + 1):
                            act.wait_ge(c_normed, i + 1)
                            act.activation(centre(i), centre(i), ACT.Silu, bias=col("ln_b", i),
                                           scale=col("ln_g", i)).then_inc(c_swished, 1)
                    if g == 7 and q >= 6:
                        oc_high(q - 6)

            def m_highs(j, b, dst, i=None, per=0):
                act.wait_ge(m_ready, val(j + 1, i, per))
                act.activation(dst, mix_m[:, b, :], ACT.Copy).then_inc(m_high_ready, 1)

            for q in range(4):
                split(MIX_C + q)
                if q < 2:
                    oc_high(2 + q)
                if q in (2, 3):
                    gate_out(7, q - 2)
            with act.Fori(0, 7) as i:
                for q in range(4):
                    split(MIX_C + 4 + q, i, 4)
                    if q >= 2:
                        j = i * 2 + (q - 2)
                        m_highs(q - 2, q - 2, m_high[:, bass.ds(j, 1), :].rearrange("p a n -> p (a n)"), i, 2)
            for g in range(4):
                for q in range(8):
                    split(OUT_C + 8 * g + q)
                    if g == 0 and q in (2, 3):
                        m_highs(KD - 2 + q - 2, q - 2, m_high[:, KD - 2 + q - 2, :])
                    if g >= 1 and q == 3:
                        act.wait_ge(group_freed, freed(OUT_G + g - 1))
                        squares(1, g - 1, x_res)
                    if g >= 1 and q == 5:
                        turned_high(1, g - 1, 4 * ((g - 1) % 2))

            act.wait_ge(chunk_used, used(OUT_C + 31))
            act.dma_start(g_fin[:, :], g_final.partition_broadcast(P)).then_inc(gfin_loaded, 16)

            def up_slot(q, n, buf, i=None):
                a = n // 2 % 2
                for b in range(2):
                    ft = val(n + b, i, 8)
                    if q == 3:
                        act.wait_ge(up_scaled, ft + 1)
                        act.activation(f_gate[:, b, :], f_raw[:, b, :], ACT.Identity,
                                       bias=par[:, bass.ds(ft + COL["ffn_b"], 1)],
                                       scale=par[:, bass.ds(ft * 3 + (COL["ffn_w"] + 1), 1)]
                                       ).then_inc(tap_mid_ready, 1)
                    if q == 5:
                        act.wait_ge(taps_ready, ft + 1)
                        act.activation(f_gate[:, b, :], f_gate[:, b, :], ACT.Silu).then_inc(silu_ready, 1)
                    if q == 7:
                        act.wait_ge(u_ready, ft + 1)
                        act.activation(u_high[:, buf, 2 * a + b, :], f_u[:, b, :],
                                       ACT.Copy).then_inc(u_high_ready, 1)

            for g in range(4):
                for q in range(8):
                    split(FFN_C + 8 * g + q)
                    if g == 0 and q == 1:
                        turned_high(1, 3, 4)
                    if g == 0 and q == 3:
                        squares(1, 3, x_res)
                    if g >= 1:
                        up_slot(q, 2 * g - 2, (g - 1) // 2)

            def ffn_round(r, i=None):
                c = FFN_C + 32 + 24 * r
                for q in range(8):
                    split(c + q, i, 48)
                    up_slot(q, 4 * r + 6, (r + 1) % 2, i)
                for q in range(8):
                    split(c + 8 + q, i, 48)
                for q in range(8):
                    split(c + 16 + q, i, 48)
                    up_slot(q, 4 * r + 8, r % 2, i)

            with act.Fori(0, (ROUNDS - 3) // 2) as i:
                ffn_round(0, i)
                ffn_round(1, i)
            ffn_round(ROUNDS - 3)
            c = FFN_C + 32 + 24 * (ROUNDS - 2)
            for q in range(8):
                split(c + q)
                up_slot(q, KF - 2, (ROUNDS - 1) % 2)
            for q in range(8):
                split(c + 8 + q)
            act.wait_ge(group_freed, freed(DOWN_G + 6 * (ROUNDS - 2) + 7))
            for t in range(TT):
                if t > 0:
                    act.wait_ge(squares_summed, 32 + t)
                act.activation(y_junk[:, :], x_res[:, t, :], ACT.Square,
                               accum_out=sumsq[:, 2 * TT + t:2 * TT + t + 1]).then_inc(squares_summed, 1)

        @block.vector
        def _(dve):
            steps = [0]

            def step(ins, wait=True):
                ins.then_inc(vec_step, 1)
                steps[0] += 1
                if wait:
                    dve.wait_ge(vec_step, steps[0])

            def split(c, i=None, per=0):
                slot, _ = chunk_slot(c)
                b = c % N_SPLIT
                dve.wait_ge(high_split, val(c + 1, i, per))
                dve.tensor_tensor(w_low[:, b, :], w_raw[:, slot, :], w_high[:, b, :].bitcast(F32),
                                  ALU.subtract).then_inc(low_split, 1)

            def turned_low(w, n, s):
                for k in range(4 * n, 4 * n + 4):
                    dve.wait_ge(h_high_ready, KD * w + k + 1)
                    dve.scalar_tensor_tensor(out=h_low[:, k, :], in0=bank[s + k % 4][:, :],
                                             scalar=col("g_ffn" if w else "g_mix", k),
                                             in1=h_high[:, k, :].bitcast(F32), op0=ALU.mult,
                                             op1=ALU.subtract).then_inc(h_low_ready, 1)

            def mean_square(w):
                dve.wait_ge(squares_summed, 16 * w + 16)
                t4 = slice(TT * w, TT * w + TT)
                step(dve.tensor_reduce(sumsq[:, t4],
                                       sq_part[:, 16 * w:16 * w + 16].rearrange("p (t n) -> p t n", t=TT),
                                       AX.X, ALU.add))
                dve.tensor_scalar(meansq[:, t4], sumsq[:, t4], 1.0 / D, EPS, ALU.mult,
                                  ALU.add).then_inc(meansq_ready, 1)

            def copy_rstd(w):
                dve.wait_ge(rstd_spread, w + 1)
                dve.tensor_copy(rstd_all[:, :], bank[7][:, :]).then_inc(rstd_copied, 1)
                dve.wait_ge(rstd_copied, w + 1)

            def scaled(out, ps):
                return dve.tensor_tensor(out, ps[:, :], rstd_all[:, :], ALU.mult)

            def glu_slot(q, g):
                s = 4 * (g % 2)
                if q == 2:
                    dve.wait_ge(chunk_used, used(GLU_C + 8 * g + 7))
                    if g == 0:
                        dve.wait_ge(consts_made, 5)
                    else:
                        dve.wait_ge(glu_done, 2 * g)
                    for b in range(2):
                        scaled(glu_gate[:, b, :], bank[s + 2 + b]).then_inc(glu_scaled, 1)
                    for b in range(2):
                        ins = scaled(conv[:, 2 * g + b, REACH:REACH + SEQ], bank[s + b])
                    ins.then_inc(group_freed, 1)
                if q == 4:
                    dve.wait_ge(group_freed, freed(GLU_G + g))
                    for b in range(2):
                        dve.wait_ge(glu_gate_ready, 2 * g + b + 1)
                        tile = conv[:, 2 * g + b, REACH:REACH + SEQ]
                        dve.scalar_tensor_tensor(out=tile, in0=tile, scalar=col("b_glu", 2 * g + b),
                                                 in1=glu_gate[:, b, :], op0=ALU.add,
                                                 op1=ALU.mult).then_inc(glu_done, 1)

            dve.wait_ge(par_loaded, 16)
            for g in range(4):
                for q in range(8):
                    if g == 0 and q in (0, 1):
                        split(GLU_C + q)
                    if g == 0 and q < 4:
                        turned_low(0, q, 4)
                    if g == 1 and q == 0:
                        mean_square(0)
                    if g > 0 or q > 1:
                        split(GLU_C + 8 * g + q)
                    if g == 1 and q == 1:
                        copy_rstd(0)
                    if g >= 1:
                        glu_slot(q, g - 1)

            qk_cols = (K_COL, Q_COL, Q_COL + 512)

            def add_bias(e, c0):
                for t in range(TT):
                    ins = dve.scalar_tensor_tensor(out=qkv[:, t, c0:c0 + 512], in0=bank[4 * (e % 2) + t][:, :],
                                                   scalar=rstd[:, t:t + 1], in1=b_qkv_all[:, c0:c0 + 512],
                                                   op0=ALU.mult, op1=ALU.add)
                ins.then_inc(group_freed, 1)

            def qk_slot(q, e):
                c0 = qk_cols[e]
                h = qkv[:, :, c0:c0 + 512].rearrange("p t (h d) -> p t h d", h=4)
                if q == 1:
                    dve.wait_ge(chunk_used, used(QKV_C + 8 * e + 7))
                    add_bias(e, c0)
                if q == 3:
                    dve.wait_ge(qk_squared, e + 1)
                    step(dve.tensor_reduce(qk_ss[:, :], qk_sq[:, :, :], AX.X, ALU.add))
                    dve.tensor_scalar(qk_ms[:, :], qk_ss[:, :], 1.0 / HD, EPS, ALU.mult,
                                      ALU.add).then_inc(qk_ms_ready, 1)
                if q == 4:
                    dve.wait_ge(qk_root_ready, e + 1)
                    step(dve.reciprocal(qk_r0[:, :], qk_root[:, :]))
                    step(dve.tensor_tensor(qk_t[:, :], qk_r0[:, :], qk_r0[:, :], ALU.mult))
                    step(dve.tensor_tensor(qk_t[:, :], qk_t[:, :], qk_ms[:, :], ALU.mult))
                    step(dve.tensor_scalar(qk_t[:, :], qk_t[:, :], -0.5, 1.5, ALU.mult, ALU.add))
                    step(dve.tensor_tensor(qk_rstd[:, :], qk_r0[:, :], qk_t[:, :], ALU.mult))
                    dve.wait_ge(group_freed, freed(QKV_G + e))
                    for t in range(TT):
                        ins = dve.tensor_tensor(h[:, t], h[:, t],
                                                qk_rstd[:, 4 * t:4 * t + 4].unsqueeze(2).to_broadcast([P, 4, HD]),
                                                ALU.mult)
                    step(ins)
                if q == 5:
                    g = qkg[:, 1 if e == 0 else 0, :].unsqueeze(1).to_broadcast([P, 4, HD])
                    for t in range(TT):
                        ins = dve.tensor_tensor(h[:, t], h[:, t], g, ALU.mult)
                    step(ins)
                if q in (6, 7):
                    pairs = qkv[:, :, c0:c0 + 512].rearrange("p t (h j two) -> p t h j two", h=4, two=2)
                    for t in range(TT):
                        x0, x1 = pairs[:, t, :, :, 0], pairs[:, t, :, :, 1]
                        cos = rope_cs[:, 0, t, :].unsqueeze(1).to_broadcast([P, 4, HD // 2])
                        sin = rope_cs[:, 1, t, :].unsqueeze(1).to_broadcast([P, 4, HD // 2])
                        if q == 6:
                            if e >= 1 and t == 0:
                                dve.wait_ge(roped, e)
                            dve.tensor_tensor(rope_a[:, t], x0, cos, ALU.mult)
                            dve.tensor_tensor(rope_b[:, t], x1, sin, ALU.mult)
                            ins = dve.tensor_tensor(rope_d[:, t], x0, sin, ALU.mult)
                        else:
                            dve.tensor_tensor(x0, rope_a[:, t], rope_b[:, t], ALU.subtract)
                            ins = dve.tensor_tensor(x1, x1, cos, ALU.mult)
                    step(ins)
                    if q == 7:
                        for t in range(TT):
                            x1 = pairs[:, t, :, :, 1]
                            ins = dve.tensor_tensor(x1, x1, rope_d[:, t], ALU.add)
                        ins.then_inc(roped, 1)

            dve.wait_ge(qkv_par_loaded, 16 * 3)
            for g in range(4):
                for q in range(8):
                    split(QKV_C + 8 * g + q)
                    if g == 0:
                        glu_slot(q, 3)
                    if g >= 1:
                        qk_slot(q, g - 1)
            split(GATE_C)
            split(GATE_C + 1)
            dve.wait_ge(chunk_used, used(QKV_C + 31))
            add_bias(3, V_COL)

            def kq_evac(g):
                for b, c0 in enumerate(head_cols(g)):
                    dve.wait_ge(kq_high_ready, 3 * g + b + 1)
                    dve.tensor_tensor(kq_low[:, g % 2, b, :].rearrange("p (t d) -> p t d", t=TT),
                                      bank[kq_bank(g, b)][:, :].rearrange("p (t d) -> p t d", t=TT),
                                      qkv_high[:, :, c0:c0 + HD].bitcast(F32),
                                      ALU.subtract).then_inc(kq_low_ready, 1)

            def v_split(g):
                dve.wait_ge(v_high_ready, g + 1)
                dve.tensor_tensor(v_low[:, :, :], qkv[:, :, V_COL + g * HD:V_COL + (g + 1) * HD],
                                  v_high[:, :, :].bitcast(F32), ALU.subtract).then_inc(v_low_ready, 1)

            def maxima(h):
                done = {}
                for t in range(TT + 1):
                    if t < TT:
                        n = 4 * h + t
                        dve.wait_ge(scores_ready, n + 1)
                        step(dve.tensor_reduce(neg_max[:, n:n + 1], bank[t][:, :], AX.X, ALU.max, negate=True),
                             wait=False)
                        done[t] = steps[0]
                    if t > 0:
                        n = 4 * h + t - 1
                        dve.wait_ge(vec_step, done[t - 1])
                        dve.tensor_scalar(exp_bias[:, n:n + 1], neg_max[:, n:n + 1], float(HD) ** -0.5, None,
                                          ALU.mult).then_inc(exp_bias_ready, 1)

            def normalise(h):
                done = {}
                for t in range(TT + 1):
                    if t < TT:
                        n = 4 * h + t
                        dve.wait_ge(exp_ready, n + 1)
                        step(dve.reciprocal(row_inv[:, n:n + 1], row_sum[:, n:n + 1]), wait=False)
                        done[t] = steps[0]
                    if t > 0:
                        n = 4 * h + t - 1
                        dve.wait_ge(vec_step, done[t - 1])
                        dve.tensor_scalar(probs[:, h % 2, t - 1, :], probs[:, h % 2, t - 1, :],
                                          row_inv[:, n:n + 1], None, ALU.mult).then_inc(probs_ready, 1)

            def pt_evac(h):
                for k in range(TT):
                    dve.wait_ge(pt_high_ready, 4 * h + k + 1)
                    dve.tensor_tensor(pt_low[:, k, :], bank[pt_bank(h, k)][:, :],
                                      pt_high[:, k, :].bitcast(F32), ALU.subtract).then_inc(pt_low_ready, 1)

            kq_evac(0)
            v_split(0)
            maxima(0)
            kq_evac(1)
            normalise(0)
            maxima(1)
            normalise(1)
            for h in range(HEADS):
                pt_evac(h)
                if h + 2 < HEADS:
                    maxima(h + 2)
                    normalise(h + 2)
                if h in (0, 2):
                    kq_evac(h // 2 + 2)
                if h % 2 == 1 and h + 1 < HEADS:
                    v_split((h + 1) // 2)

            def centre(i):
                return conv[:, i, REACH:REACH + SEQ]

            def conv_taps(i, k0, k1):
                w0 = COL["conv_w"] + i * CONV_K
                for k in range(k0, k1):
                    if k == 0:
                        step(dve.tensor_scalar(vec_acc[:, :], conv[:, i, 0:SEQ], par[:, w0:w0 + 1],
                                               col("conv_b", i), ALU.mult, ALU.add))
                    elif k < CONV_K:
                        step(dve.scalar_tensor_tensor(out=vec_acc[:, :], in0=conv[:, i, k:k + SEQ],
                                                      scalar=par[:, w0 + k:w0 + k + 1], in1=vec_acc[:, :],
                                                      op0=ALU.mult, op1=ALU.add))
                    else:
                        dve.tensor_copy(centre(i), vec_acc[:, :]).then_inc(vec_conv_done, 1)
                        dve.wait_ge(vec_conv_done, i - POOL_CONV_TILES + 1)

            def oc_low(n):
                dve.wait_ge(oc_high_ready, n + 1)
                k = 4 * (n % 2)
                if n < 2:
                    low, high, full = o_low, o_high, o_full[:, k:k + 4, :]
                else:
                    low, high, full = c_low, c_high, conv[:, k:k + 4, REACH:REACH + SEQ]
                dve.tensor_tensor(low[:, k:k + 4, :], full, high[:, k:k + 4, :].bitcast(F32),
                                  ALU.subtract).then_inc(oc_low_ready, 1)

            def gates_scaled(g):
                dve.wait_ge(chunk_used, used(GATE_C + 8 * g + 7))
                s = 4 * (g % 2)
                for b in range(2):
                    scaled(gate_a[:, 2 * g + b, :], bank[s + b])
                    ins = scaled(gate_c[:, 2 * g + b, :], bank[s + 2 + b])
                    ins.then_inc(gate_scaled if b == 0 else group_freed, 1)

            dve.wait_ge(o_ready, HEADS)
            for g in range(8):
                for q in range(8):
                    if g > 0 or q > 1:
                        split(GATE_C + 8 * g + q)
                    if g < KC - POOL_CONV_TILES:
                        conv_taps(POOL_CONV_TILES + g, 4 * q, 4 * q + 4)
                    if g >= 1 and q == 2:
                        gates_scaled(g - 1)
                    if g == 5 and q == 1:
                        dve.wait_ge(mean_ready, 1)
                        dve.tensor_copy(mean_sb[:, :], bank[7][:, :]).then_inc(mean_copied, 1)
                        dve.wait_ge(mean_copied, 1)
                    if g == 5 and 2 <= q <= 5:
                        for i in (2 * (q - 2), 2 * (q - 2) + 1):
                            dve.tensor_tensor(centre(i), centre(i), mean_sb[:, :],
                                              ALU.subtract).then_inc(centred, 1)
                    if g == 6 and q == 1:
                        dve.wait_ge(var_ready, 1)
                        dve.tensor_scalar(var_sb[:, :], bank[3][:, :], EPS, None, ALU.add).then_inc(var_copied, 1)
                    if g == 6 and q == 3:
                        root, r0, t = ch_sq[:, 0, :], ch_sq[:, 1, :], sq_sum[:, :]
                        dve.wait_ge(ln_root_ready, 1)
                        step(dve.reciprocal(r0, root))
                        step(dve.tensor_tensor(t, r0, r0, ALU.mult))
                        step(dve.tensor_tensor(t, t, var_sb[:, :], ALU.mult))
                        step(dve.tensor_scalar(t, t, -0.5, 1.5, ALU.mult, ALU.add))
                        step(dve.tensor_tensor(ln_rstd[:, :], r0, t, ALU.mult))
                    if g == 6 and 4 <= q <= 7:
                        for i in (2 * (q - 4), 2 * (q - 4) + 1):
                            dve.tensor_tensor(centre(i), centre(i), ln_rstd[:, :],
                                              ALU.mult).then_inc(c_normed, 1)
                    if g == 7 and q >= 6:
                        oc_low(q - 6)

            def mix_slot(q, g, i=None):
                if q not in (1, 2):
                    return
                b, s = q - 1, 4 * (g % 2)
                j = val(2 * g + b, i, 4)
                if b == 0:
                    dve.wait_ge(chunk_used, used(MIX_C + 4 * g + 3, i, 8))
                    if g > 0:
                        dve.wait_ge(m_ready, val(2 * g, i, 4))
                for mixed, gate, ps in ((mix_a, gate_a, bank[s + b]), (mix_c, gate_c, bank[s + 2 + b])):
                    ins = dve.tensor_tensor(mixed[:, b, :], ps[:, :],
                                            gate[:, bass.ds(j, 1), :].rearrange("p a n -> p (a n)"), ALU.mult)
                ins.then_inc(mix_gated if b == 0 else group_freed, 1)

            for g in range(2):
                for q in range(4):
                    split(MIX_C + 4 * g + q)
                    if g == 0 and q < 2:
                        oc_low(2 + q)
                    if g == 0 and q == 2:
                        gates_scaled(7)
                    if g == 1:
                        if q == 1:
                            dve.wait_ge(gate_stored, 2 * KD)
                        mix_slot(q, 0)
            with dve.Fori(0, 3) as i:
                for g in (1, 2):
                    for q in range(4):
                        split(MIX_C + 4 * g + 4 + q, i, 8)
                        mix_slot(q, g, i)

            def out_slot(q, g):
                if q == 1:
                    dve.wait_ge(chunk_used, used(OUT_C + 8 * g + 7))
                    dve.wait_ge(xres_loaded, 16 * TT)
                    for t in range(TT):
                        piece = x_res[:, t, 512 * g:512 * g + 512]
                        ins = dve.tensor_tensor(piece, piece, bank[4 * (g % 2) + t][:, :], ALU.add)
                    ins.then_inc(group_freed, 1)

            for g in range(4):
                for q in range(8):
                    split(OUT_C + 8 * g + q)
                    if g == 0:
                        mix_slot(q, 7)
                    else:
                        out_slot(q, g - 1)
                    if g >= 1 and q == 5:
                        turned_low(1, g - 1, 4 * ((g - 1) % 2))

            def up_slot(q, n, last, group, i=None):
                after = freed(group, i, 12)
                s = 4 * (n // 2 % 2)
                if q == 2:
                    dve.wait_ge(chunk_used, used(last, i, 48))
                    if n >= 2:
                        dve.wait_ge(u_ready, val(n, i, 8))
                        dve.wait_ge(tap_mid_ready, val(n, i, 8))
                    for b in range(2):
                        scaled(f_raw[:, b, :], bank[s + b]).then_inc(up_scaled, 1)
                    for b in range(2):
                        ins = scaled(f_val[:, b, :], bank[s + 2 + b])
                    ins.then_inc(group_freed, 1)
                for b in range(2):
                    ft = val(n + b, i, 8)
                    gate = f_gate[:, b, :]
                    if q == 4:
                        dve.wait_ge(tap_mid_ready, ft + 1)
                        for tap, out, src, done in ((0, slice(1, SEQ), slice(0, SEQ - 1), tap_left_ready),
                                                    (2, slice(0, SEQ - 1), slice(1, SEQ), taps_ready)):
                            if tap == 2:
                                dve.wait_ge(tap_left_ready, ft + 1)
                            dve.scalar_tensor_tensor(out=gate[:, out], in0=f_raw[:, b, src],
                                                     scalar=par[:, bass.ds(ft * 3 + (COL["ffn_w"] + tap), 1)],
                                                     in1=gate[:, out], op0=ALU.mult, op1=ALU.add).then_inc(done, 1)
                    if q == 6:
                        dve.wait_ge(silu_ready, ft + 1)
                        if b == 0:
                            dve.wait_ge(group_freed, after)
                        if n >= 2:
                            dve.wait_ge(u_low_ready, val(n + b - 1, i, 8))
                        dve.tensor_tensor(f_u[:, b, :], gate, f_val[:, b, :], ALU.mult).then_inc(u_ready, 1)

            def down_out(r, q, i=None):
                first = FFN_C + 32 + 24 * r - 16 * (r == ROUNDS - 1)
                dve.wait_ge(chunk_used, used(first + 2 * q + 1, i, 48))
                dve.wait_ge(group_freed, freed(DOWN_G + 6 * r - 6 + q, i, 12))
                for t in range(TT):
                    piece = x_res[:, t, 512 * q:512 * q + 512]
                    ins = dve.tensor_tensor(piece, piece, bank[4 * (q % 2) + t][:, :], ALU.add)
                ins.then_inc(group_freed, 1)

            for g in range(4):
                for q in range(8):
                    if g == 1 and q == 0:
                        mean_square(1)
                    split(FFN_C + 8 * g + q)
                    if g == 0:
                        out_slot(q, 3)
                        if q == 1:
                            turned_low(1, 3, 4)
                    if g == 1 and q == 1:
                        copy_rstd(1)
                    if g >= 1:
                        up_slot(q, 2 * g - 2, FFN_C + 8 * g - 1, FFN_G + g - 1)

            def ffn_round(r, i=None):
                c = FFN_C + 32 + 24 * r
                for q in range(8):
                    split(c + q, i, 48)
                    up_slot(q, 4 * r + 6, c - 1, DOWN_G + 6 * r - 1, i)
                    if q in (3, 5, 7):
                        down_out(r, (q - 3) // 2, i)
                for q in range(8):
                    split(c + 8 + q, i, 48)
                    if q == 1:
                        down_out(r, 3, i)
                for q in range(8):
                    split(c + 16 + q, i, 48)
                    up_slot(q, 4 * r + 8, c + 15, DOWN_G + 6 * r + 4, i)

            with dve.Fori(0, (ROUNDS - 3) // 2) as i:
                ffn_round(0, i)
                ffn_round(1, i)
            ffn_round(ROUNDS - 3)
            c = FFN_C + 32 + 24 * (ROUNDS - 2)
            for q in range(16):
                split(c + q)
                if q < 8:
                    up_slot(q, KF - 2, c - 1, DOWN_G + 6 * (ROUNDS - 2) - 1)
                if q in (3, 5, 7, 9):
                    down_out(ROUNDS - 2, (q - 3) // 2)
                if q in (11, 13, 15):
                    down_out(ROUNDS - 1, (q - 11) // 2)
            down_out(ROUNDS - 1, 3)
            dve.wait_ge(gfin_loaded, 16)
            dve.wait_ge(squares_summed, 32 + TT)
            dve.tensor_scalar(meansq[:, 2 * TT:3 * TT], sumsq[:, 2 * TT:3 * TT], 1.0 / D, EPS, ALU.mult,
                              ALU.add).then_inc(meansq_ready, 1)
            dve.wait_ge(rstd_ready, 3)
            for t in range(TT):
                q = 2 * TT + t
                dve.scalar_tensor_tensor(out=x_res[:, t, :], in0=x_res[:, t, :], scalar=rstd[:, q:q + 1],
                                         in1=g_fin[:, :], op0=ALU.mult, op1=ALU.mult).then_inc(y_ready, 1)

        @block.tensor
        def _(pe):
            def products(ps, a_high, a_low, b_high, b_low, first, last):
                pe.matmul(ps, a_high, b_high, start=first, stop=False)
                pe.matmul(ps, a_high, b_low, start=False, stop=False)
                return pe.matmul(ps, a_low, b_high, start=False, stop=last)

            def pair_group(c, s, high, low, chunks=4, i=None, per=0, before=None, high2=None, low2=None):
                for n in range(2 * chunks):
                    half, q = n // chunks, n % chunks
                    xh, xl = (high, low) if half == 0 or high2 is None else (high2, low2)
                    if before is not None and n in before:
                        before[n]()
                    pe.wait_ge(low_split, val(c + n + 1, i, per))
                    slot = (c + n) % N_SPLIT
                    for kk in range(4):
                        k = 4 * q + kk
                        for b in range(2):
                            w = slice(256 * kk + P * b, 256 * kk + P * b + P)
                            ins = products(bank[s + 2 * half + b][:, :], w_high[:, slot, w], w_low[:, slot, w],
                                           xh[:, k, :], xl[:, k, :], k == 0, k == 4 * chunks - 1)
                    ins.then_inc(chunk_used, 1)

            def wide_group(c, s, high, low, chunks=8, i=None, per=0, before=None):
                for q in range(chunks):
                    if before is not None:
                        before(q)
                    pe.wait_ge(low_split, val(c + q + 1, i, per))
                    slot = (c + q) % N_SPLIT
                    for kk in range(2):
                        k = 2 * q + kk
                        w = slice(512 * kk, 512 * kk + 512)
                        for t in range(TT):
                            tok = slice(P * t, P * t + P)
                            ins = products(bank[s + t][:, :], high[:, k, tok], low[:, k, tok],
                                           w_high[:, slot, w], w_low[:, slot, w], k == 0, k == 2 * chunks - 1)
                    ins.then_inc(chunk_used, 1)

            def turn(w, n, s, src):
                for k in range(4 * n, 4 * n + 4):
                    for t in range(TT):
                        ins = pe.transpose(bank[s + k % 4][:, P * t:P * t + P],
                                           src[:, t, P * k:P * k + P], ident[:, :])
                    ins.then_inc(x_turned, 1)

            def turn_x_in(n):
                pe.wait_ge(x_loaded[n], 16)
                if n > 0:
                    pe.wait_ge(h_low_ready, 4 * n)
                turn(0, n, 4, x_in)

            def tiles_ready(w, q):
                pe.wait_ge(h_low_ready, KD * w + 4 * q + 4)

            def spread_rstd(w):
                pe.wait_ge(h_low_ready, KD * w + KD)
                pe.wait_ge(rstd_ready, w + 1)
                for t in range(TT):
                    n = TT * w + t
                    ins = pe.matmul(bank[7][:, P * t:P * t + P], rstd[:, n:n + 1].to_broadcast([P, P]),
                                    ident[:, :], start=True, stop=True)
                ins.then_inc(rstd_spread, 1)

            pe.wait_ge(consts_made, 5)
            turn_x_in(0)

            def first(q):
                if q < 3:
                    turn_x_in(q + 1)
                tiles_ready(0, q)

            pair_group(GLU_C, 0, h_high, h_low, before={q: partial(first, q) for q in range(4)})
            pair_group(GLU_C + 8, 4, h_high, h_low,
                       before={1: partial(spread_rstd, 0), 4: lambda: pe.wait_ge(rstd_copied, 1)})
            for g in range(2, 4):
                pe.wait_ge(group_freed, freed(GLU_G + g - 2))
                pair_group(GLU_C + 8 * g, 4 * (g % 2), h_high, h_low)
            with pe.Fori(0, 2) as i:
                for g in range(2):
                    pe.wait_ge(group_freed, i * 2 + freed(QKV_G + g - 2))
                    wide_group(QKV_C + 8 * g, 4 * g, h_high, h_low, 8, i, 16)

            def turn_kq(g):
                for b, c0 in enumerate(head_cols(g)):
                    if g == 1:
                        pe.wait_ge(kq_low_ready, b + 1)
                    for t in range(TT):
                        ins = pe.transpose(bank[kq_bank(g, b)][:, P * t:P * t + P],
                                           qkv[:, t, c0:c0 + HD], ident[:, :])
                    ins.then_inc(kq_turned, 1)

            def scores(h):
                g, b = h // 2, 1 + h % 2
                pe.wait_ge(kq_low_ready, 3 * (g + 1))
                k_high = qkv_high[:, :, head_cols(g)[0]:head_cols(g)[0] + HD]
                q0 = head_cols(g)[b]
                for t in range(TT):
                    if h >= 1:
                        pe.wait_ge(exp_ready, 4 * (h - 1) + t + 1)
                    products(bank[t][:, :], qkv_high[:, t, q0:q0 + HD], kq_low[:, g % 2, b, P * t:P * t + P],
                             k_high, kq_low[:, g % 2, 0, :], True, True).then_inc(scores_ready, 1)

            def turn_probs(h):
                pe.wait_ge(probs_ready, 4 * h + 4)
                for k in range(TT):
                    if h == 0 and k >= 1:
                        pe.wait_ge(kq_low_ready, 3 + k)
                    if h in (1, 3) and k < 3:
                        pe.wait_ge(kq_low_ready, 3 * (h + 3) // 2 + k + 1)
                    if h >= 1 and k == 3:
                        pe.wait_ge(o_ready, h)
                    for t in range(TT):
                        ins = pe.transpose(bank[pt_bank(h, k)][:, P * t:P * t + P],
                                           probs[:, h % 2, t, P * k:P * k + P], ident[:, :])
                    ins.then_inc(probs_turned, 1)

            def weighted_sum(h):
                pe.wait_ge(v_low_ready, h // 2 + 1)
                for k in range(TT):
                    pe.wait_ge(pt_low_ready, 4 * h + k + 1)
                    ins = products(bank[pt_bank(h, 0)][:, :], v_high[:, k, :], v_low[:, k, :],
                                   pt_high[:, k, :], pt_low[:, k, :], k == 0, k == TT - 1)
                ins.then_inc(o_summed, 1)

            pe.wait_ge(roped, 3)
            pe.wait_ge(group_freed, freed(QKV_G + 3))
            turn_kq(0)
            scores(0)
            turn_kq(1)
            scores(1)
            for h in range(HEADS):
                turn_probs(h)
                if h + 2 < HEADS:
                    scores(h + 2)
                weighted_sum(h)
                if h in (0, 2):
                    turn_kq(h // 2 + 2)

            pe.wait_ge(o_ready, HEADS)
            with pe.Fori(0, 2) as i:
                for g in range(2):
                    pe.wait_ge(group_freed, i * 2 + freed(GATE_G + g - 2))
                    pair_group(GATE_C + 8 * g, 4 * g, h_high, h_low, 4, i, 16)
            pe.wait_ge(group_freed, freed(GATE_G + 2))
            pair_group(GATE_C + 32, 0, h_high, h_low)
            pe.wait_ge(group_freed, freed(GATE_G + 3))
            pe.wait_ge(ch_sum_ready, 1)
            pe.matmul(bank[7][:, :], mean_w[:, :], ch_sum[:, :], start=True, stop=True).then_inc(mean_ready, 1)
            pair_group(GATE_C + 40, 4, h_high, h_low, before={4: lambda: pe.wait_ge(mean_copied, 1)})
            pe.wait_ge(group_freed, freed(GATE_G + 4))
            pe.wait_ge(ch_sq_added, KC)
            pe.matmul(bank[3][:, :], mean_w[:, :], sq_sum[:, :], start=True, stop=True).then_inc(var_ready, 1)
            pair_group(GATE_C + 48, 0, h_high, h_low, before={4: lambda: pe.wait_ge(var_copied, 1)})
            pe.wait_ge(group_freed, freed(GATE_G + 5))
            pair_group(GATE_C + 56, 4, h_high, h_low)

            with pe.Fori(0, 4) as i:
                for g in range(2):
                    pe.wait_ge(group_freed, i * 2 + freed(MIX_G + g - 2))
                    pair_group(MIX_C + 4 * g, 4 * g, o_high, o_low, 2, i, 8,
                               {n: partial(pe.wait_ge, oc_low_ready, n + 1) for n in range(4)}, c_high, c_low)

            def out_before(g, q):
                if q == 4 and g >= 1:
                    pe.wait_ge(group_freed, freed(OUT_G + g - 1))
                    turn(1, g - 1, 4 * ((g - 1) % 2), x_res)
                pe.wait_ge(m_low_ready, 2 * q + 2)

            for g in range(4):
                pe.wait_ge(group_freed, freed(OUT_G + g - 2))
                if g >= 2:
                    pe.wait_ge(h_low_ready, KD + 4 * (g - 1))
                wide_group(OUT_C + 8 * g, 4 * (g % 2), m_high, m_low, before=partial(out_before, g))

            def last_turn():
                pe.wait_ge(group_freed, freed(OUT_G + 3))
                turn(1, 3, 4, x_res)

            pe.wait_ge(h_low_ready, KD + 12)
            pair_group(FFN_C, 0, h_high, h_low, before={1: last_turn, 3: partial(tiles_ready, 1, 3)})
            pe.wait_ge(h_low_ready, KD + KD)
            pair_group(FFN_C + 8, 4, h_high, h_low,
                       before={1: partial(spread_rstd, 1), 4: lambda: pe.wait_ge(rstd_copied, 2)})
            for g in range(2, 4):
                pe.wait_ge(group_freed, freed(FFN_G + g - 2))
                pair_group(FFN_C + 8 * g, 4 * (g % 2), h_high, h_low)

            def down(r, c, group, i=None):
                for q in range(4):
                    pe.wait_ge(group_freed, freed(group + q - 2, i, 12))
                    wide_group(c + 2 * q, 4 * (q % 2), u_high[:, r % 2], u_low[:, r % 2], 2, i, 48,
                               lambda k: pe.wait_ge(u_low_ready, val(4 * r + 2 * k + 2, i, 8)))

            def ffn_round(r, i=None):
                c, group = FFN_C + 32 + 24 * r, DOWN_G + 6 * r
                down(r, c, group, i)
                for a in range(2):
                    pe.wait_ge(group_freed, freed(group + 2 + a, i, 12))
                    pair_group(c + 8 + 8 * a, 4 * a, h_high, h_low, 4, i, 48)

            with pe.Fori(0, (ROUNDS - 3) // 2) as i:
                ffn_round(0, i)
                ffn_round(1, i)
            ffn_round(ROUNDS - 3)
            c = FFN_C + 32 + 24 * (ROUNDS - 2)
            group = DOWN_G + 6 * (ROUNDS - 2)
            down(ROUNDS - 2, c, group)
            down(ROUNDS - 1, c + 8, group + 4)


def rope_tables():
    f32 = np.float32
    rows = SEQ // GRID_W
    row = np.repeat(np.arange(rows), GRID_W).astype(f32)
    column = np.tile(np.arange(GRID_W), rows).astype(f32)
    inv_freq = f32(ROPE_THETA) ** (-np.arange(0, HD // 2, 2, dtype=f32) / f32(HD // 2))
    angle = np.concatenate([row[:, None] * inv_freq, column[:, None] * inv_freq], axis=-1).astype(f32)
    return np.stack([np.cos(angle), np.sin(angle)]).astype(f32)


def kernel(x, norm_mix_g, w_in, b_in, q_norm_g, k_norm_g, w_attn_o, conv_dw_w, conv_dw_b, conv_ln_g,
           conv_ln_b, w_conv_o, w_out, norm_ffn_g, w_ffn_up, ffn_dw_w, ffn_dw_b, w_ffn_down, norm_final_g):
    import concourse.bacc as bacc
    from concourse.bass_utils import run_bass_kernel_spmd

    def tiles(v):
        return np.asarray(v).reshape(-1, P).T

    def taps(w):
        w = np.asarray(w)
        return w.reshape(w.shape[0], -1, P).transpose(2, 1, 0).reshape(P, -1)

    b = np.asarray(b_in)[0]
    cols = np.concatenate([
        tiles(norm_mix_g[0]), tiles(norm_ffn_g[0]), tiles(b[GLU_COL:GATE_COL]), tiles(b[GATE_COL:]),
        tiles(conv_dw_b[0]), tiles(conv_ln_g[0]), tiles(conv_ln_b[0]), taps(conv_dw_w[0]),
        taps(ffn_dw_w[0]), tiles(ffn_dw_b[0])], axis=1)
    rope = rope_tables().reshape(2, TT, P, HD // 2).transpose(2, 0, 1, 3)
    arrays = {
        "x_dram": np.asarray(x)[0], "w_in_dram": np.asarray(w_in)[0],
        "w_attn_o_dram": np.asarray(w_attn_o)[0], "w_conv_o_dram": np.asarray(w_conv_o)[0],
        "w_out_dram": np.asarray(w_out)[0], "w_up_dram": np.asarray(w_ffn_up)[0],
        "w_down_dram": np.asarray(w_ffn_down)[0], "cols_dram": cols, "b_qkv_dram": b[:GLU_COL],
        "qk_g_dram": np.stack([np.asarray(q_norm_g)[0], np.asarray(k_norm_g)[0]]),
        "g_final_dram": np.asarray(norm_final_g), "rope_dram": rope,
    }
    arrays = {name: np.ascontiguousarray(a) for name, a in arrays.items()}
    nc = bacc.Bacc("TRN2", target_bir_lowering=False, num_devices=1, dynamic_dma_scratch_size=1024)
    ins = [nc.dram_tensor(name, a.shape, mybir.dt.from_np(a.dtype), kind="ExternalInput").ap()
           for name, a in arrays.items()]
    y = nc.dram_tensor("y_dram", (SEQ, D), F32, kind="ExternalOutput").ap()
    build(nc, *ins, y)
    result = run_bass_kernel_spmd(nc, [arrays], core_ids=[0])
    return result.results[0]["y_dram"].reshape(1, SEQ, D)
```

```python
from contextlib import ExitStack
from functools import partial

import numpy as np

import concourse.bass as bass
import concourse.mybir as mybir

ACT = mybir.ActivationFunctionType
ALU = mybir.AluOpType
AX = mybir.AxisListType
F32 = mybir.dt.float32
F32R = mybir.dt.float32r

P = 128
SEQ = 512
D = 2048
HEADS = 8
KV_HEADS = 4
HD = 128
CONV_CH = 1024
CONV_K = 31
FFN = 5632
FFN_K = 3
GRID_W = 64
ROPE_THETA = 10000.0
EPS = 1e-6

TT = SEQ // P
KD = D // P
KC = CONV_CH // P
KA = HEADS
KF = FFN // P
ROUNDS = KF // 4
ATTN_Q = HEADS * HD
ATTN_KV = KV_HEADS * HD
Q_COL = 0
K_COL = ATTN_Q
V_COL = ATTN_Q + ATTN_KV
GLU_COL = ATTN_Q + 2 * ATTN_KV
GATE_COL = GLU_COL + 2 * CONV_CH
PADDED = SEQ + 32
REACH = CONV_K // 2
POOL_CONV_TILES = 4

COL = {}
_at = 0
for _name, _n in (("g_mix", KD), ("g_ffn", KD), ("b_glu", 2 * KC), ("b_gate", 2 * KD), ("conv_b", KC),
                  ("ln_g", KC), ("ln_b", KC), ("conv_w", KC * CONV_K), ("ffn_w", KF * FFN_K), ("ffn_b", KF)):
    COL[_name] = _at
    _at += _n
N_COLS = _at

GLU_C = 0
QKV_C = GLU_C + 4 * 8
GATE_C = QKV_C + 4 * 8
MIX_C = GATE_C + 8 * 8
OUT_C = MIX_C + 8 * 4
FFN_C = OUT_C + 4 * 8
GLU_G, QKV_G, GATE_G, MIX_G, OUT_G, FFN_G = 0, 4, 8, 16, 24, 28
DOWN_G = FFN_G + 4
N_RAW = 4
N_SPLIT = 2


def val(const, i=None, per=0):
    return const if i is None else i * per + const


def build(nc, x, w_in, w_attn_o, w_conv_o, w_out, w_up, w_down, cols, b_qkv, qk_g, g_final, rope, y):
    ctx = ExitStack()
    with ctx:
        base = (nc.sbuf_base + 63) // 32 * 32
        cursor = [base]

        def at(name, shape, dt, offset):
            return nc.alloc_sbuf_tensor_at(name, [P] + shape, dt, offset=offset)

        def region(nbytes):
            o = cursor[0]
            cursor[0] += (nbytes + 31) // 32 * 32
            return o

        KB = 1024
        r_ring = region(32 * KB)
        r_act = region(64 * KB)
        r_mix = region(64 * KB)
        r_conv = region(KC * PADDED * 4)
        r_o = region(16 * KB)
        r_cols = region(N_COLS * 4)
        r_ident = region(512)
        r_mean_w = region(512)
        r_qkg = region(1024)
        r_rope = region(2048)
        r_rstd_all = region(2048)
        r_small = region(1792)
        r_work = region(20 * KB)
        assert cursor[0] <= nc.sbuf_top, (cursor[0], nc.sbuf_top)

        w_raw = at("w_raw", [N_RAW, 1024], F32, r_ring)
        w_high = at("w_high", [N_SPLIT, 1024], F32R, r_ring + 16 * KB)
        w_low = at("w_low", [N_SPLIT, 1024], F32R, r_ring + 24 * KB)
        h_high = at("h_high", [KD, SEQ], F32R, r_act)
        h_low = at("h_low", [KD, SEQ], F32R, r_act + 32 * KB)
        o_high = at("o_high", [KA, SEQ], F32R, r_act)
        o_low = at("o_low", [KA, SEQ], F32R, r_act + 32 * KB)
        c_high = at("c_high", [KC, SEQ], F32R, r_act + 16 * KB)
        c_low = at("c_low", [KC, SEQ], F32R, r_act + 48 * KB)
        x_in = at("x_in", [TT, D], F32, r_mix)
        glu_gate = at("glu_gate", [2, SEQ], F32, r_mix + 32 * KB)
        qkv = at("qkv", [TT, D], F32, r_mix)
        qk_sq = at("qk_sq", [TT * 4, HD], F32, r_mix + 40 * KB)
        rope_a = at("rope_a", [TT, 4, HD // 2], F32, r_mix + 48 * KB)
        rope_b = at("rope_b", [TT, 4, HD // 2], F32, r_mix + 52 * KB)
        rope_d = at("rope_d", [TT, 4, HD // 2], F32, r_mix + 56 * KB)
        probs = at("probs", [2, TT, SEQ], F32, r_mix + 32 * KB)
        pt_high = at("pt_high", [TT, SEQ], F32R, r_mix + 48 * KB)
        pt_low = at("pt_low", [TT, SEQ], F32R, r_mix + 56 * KB)
        gate_a = at("gate_a", [KD, SEQ], F32, r_mix)
        gate_c = at("gate_c", [KD, SEQ], F32, r_mix + 32 * KB)
        m_high = at("m_high", [KD, SEQ], F32R, r_mix)
        m_low = at("m_low", [KD, SEQ], F32R, r_mix + 32 * KB)
        u_high = at("u_high", [2, 4, SEQ], F32R, r_mix)
        u_low = at("u_low", [2, 4, SEQ], F32R, r_mix + 16 * KB)
        g_fin = at("g_fin", [D], F32, r_mix + 32 * KB)
        y_junk = at("y_junk", [D], F32, r_mix + 40 * KB)
        x_g = at("x_g", [2, D // 2], F32, r_mix + 56 * KB)
        last_high = at("last_high", [8, 1024], F32R, r_act)
        last_low = at("last_low", [8, 1024], F32R, r_act + 32 * KB)
        f_raw = at("f_raw", [2, SEQ], F32, r_mix + 48 * KB)
        conv = at("conv", [KC, PADDED], F32, r_conv)
        b_qkv_all = at("b_qkv_all", [D], F32, r_o)
        o_full = at("o_full", [KA, SEQ], F32, r_o)
        x_res = at("x_res", [TT, D], F32, r_conv)
        par = at("par", [N_COLS], F32, r_cols)
        ident = at("ident", [P], F32, r_ident)
        mean_w = at("mean_w", [P], F32, r_mean_w)
        qkg = at("qkg", [2, HD], F32, r_qkg)
        rstd_all = at("rstd_all", [SEQ], F32, r_rstd_all)
        rope_cs = at("rope_cs", [2, TT, HD // 2], F32, r_rope)
        small = [r_small]

        def tiny(name, n):
            t = at(name, [n], F32, small[0])
            small[0] += (n * 4 + 31) // 32 * 32
            return t

        sq_part = tiny("sq_part", 3 * 16)
        sumsq = tiny("sumsq", 3 * TT)
        meansq = tiny("meansq", 3 * TT)
        rstd = tiny("rstd", 3 * TT)
        neg_half = tiny("neg_half", 1)
        qk_ss = tiny("qk_ss", 16)
        qk_ms = tiny("qk_ms", 16)
        qk_root = tiny("qk_root", 16)
        qk_r0 = tiny("qk_r0", 16)
        qk_t = tiny("qk_t", 16)
        qk_rstd = tiny("qk_rstd", 16)
        neg_max = tiny("neg_max", 4 * HEADS)
        exp_bias = tiny("exp_bias", 4 * HEADS)
        row_sum = tiny("row_sum", 4 * HEADS)
        row_inv = tiny("row_inv", 4 * HEADS)
        assert small[0] - r_small <= 1792
        sq_junk = at("sq_junk", [SEQ], F32, r_work + 16 * KB)
        qkv_high = at("qkv_high", [TT, D], F32R, r_mix)
        kq_low = at("kq_low", [2, 3, SEQ], F32R, r_work)
        v_high = at("v_high", [TT, HD], F32R, r_work + 12 * KB)
        v_low = at("v_low", [TT, HD], F32R, r_work + 14 * KB)
        pool_acc = at("pool_acc", [SEQ], F32, r_work + 16 * KB)
        pool_tap = at("pool_tap", [SEQ], F32, r_work + 18 * KB)
        vec_acc = at("vec_acc", [SEQ], F32, r_work)
        ch_sum = at("ch_sum", [SEQ], F32, r_work + 2 * KB)
        mean_sb = at("mean_sb", [SEQ], F32, r_work + 4 * KB)
        ch_sq = at("ch_sq", [2, SEQ], F32, r_work + 6 * KB)
        sq_sum = at("sq_sum", [SEQ], F32, r_work + 10 * KB)
        var_sb = at("var_sb", [SEQ], F32, r_work + 12 * KB)
        ln_rstd = at("ln_rstd", [SEQ], F32, r_work + 14 * KB)
        mix_a = at("mix_a", [2, SEQ], F32, r_work)
        mix_c = at("mix_c", [2, SEQ], F32, r_work + 4 * KB)
        mix_m = at("mix_m", [2, SEQ], F32, r_work + 8 * KB)
        f_gate = at("f_gate", [2, SEQ], F32, r_work + 8 * KB)
        f_val = at("f_val", [2, SEQ], F32, r_work + 12 * KB)
        f_u = at("f_u", [2, SEQ], F32, r_work + 16 * KB)

        bank = [ctx.enter_context(nc.psum_tensor(f"bank{b}", [P, 512], F32)) for b in range(8)]

        def sem(name):
            return ctx.enter_context(nc.semaphore(name))

        chunk_loaded = [sem(f"chunk_loaded{s}") for s in range(N_RAW)]
        high_split = sem("high_split")
        low_split = sem("low_split")
        chunk_used = sem("chunk_used")
        group_freed = sem("group_freed")
        x_loaded = [sem(f"x_loaded{t}") for t in range(TT)]
        x_head_loaded = sem("x_head_loaded")
        xres_loaded = sem("xres_loaded")
        par_loaded = sem("par_loaded")
        qkv_par_loaded = sem("qkv_par_loaded")
        consts_made = sem("consts_made")
        table_fetched = sem("table_fetched")
        squares_summed = sem("squares_summed")
        meansq_ready = sem("meansq_ready")
        rstd_ready = sem("rstd_ready")
        x_turned = sem("x_turned")
        rstd_spread = sem("rstd_spread")
        rstd_copied = sem("rstd_copied")
        h_high_ready = sem("h_high_ready")
        h_low_ready = sem("h_low_ready")
        glu_scaled = sem("glu_scaled")
        glu_gate_ready = sem("glu_gate_ready")
        glu_done = sem("glu_done")
        pool_step = sem("pool_step")
        vec_step = sem("vec_step")
        vec_conv_done = sem("vec_conv_done")
        ch_sum_ready = sem("ch_sum_ready")
        mean_ready = sem("mean_ready")
        mean_copied = sem("mean_copied")
        centred = sem("centred")
        ch_sq_ready = sem("ch_sq_ready")
        ch_sq_added = sem("ch_sq_added")
        var_ready = sem("var_ready")
        var_copied = sem("var_copied")
        ln_root_ready = sem("ln_root_ready")
        c_normed = sem("c_normed")
        c_swished = sem("c_swished")
        qk_squared = sem("qk_squared")
        qk_ms_ready = sem("qk_ms_ready")
        qk_root_ready = sem("qk_root_ready")
        roped = sem("roped")
        kq_turned = sem("kq_turned")
        kq_high_ready = sem("kq_high_ready")
        kq_low_ready = sem("kq_low_ready")
        v_high_ready = sem("v_high_ready")
        v_low_ready = sem("v_low_ready")
        scores_ready = sem("scores_ready")
        exp_bias_ready = sem("exp_bias_ready")
        exp_ready = sem("exp_ready")
        probs_ready = sem("probs_ready")
        probs_turned = sem("probs_turned")
        pt_high_ready = sem("pt_high_ready")
        pt_low_ready = sem("pt_low_ready")
        o_summed = sem("o_summed")
        o_ready = sem("o_ready")
        gate_scaled = sem("gate_scaled")
        gate_stored = sem("gate_stored")
        oc_high_ready = sem("oc_high_ready")
        oc_low_ready = sem("oc_low_ready")
        mix_gated = sem("mix_gated")
        m_ready = sem("m_ready")
        m_high_ready = sem("m_high_ready")
        m_low_ready = sem("m_low_ready")
        tap_mid_ready = sem("tap_mid_ready")
        tap_left_ready = sem("tap_left_ready")
        up_scaled = sem("up_scaled")
        taps_ready = sem("taps_ready")
        silu_ready = sem("silu_ready")
        u_ready = sem("u_ready")
        u_high_ready = sem("u_high_ready")
        u_low_ready = sem("u_low_ready")
        gfin_loaded = sem("gfin_loaded")
        last_summed = sem("last_summed")
        x_added = sem("x_added")
        x_g_ready = sem("x_g_ready")
        y_left_ready = sem("y_left_ready")
        y_right_ready = sem("y_right_ready")
        y_stored = sem("y_stored")

        def freed(group, i=None, per=0):
            return val(group + 1, i, per)

        def used(c, i=None, per=0):
            return val(c + 1, i, per)

        def chunk_slot(c):
            return c % N_RAW, 16 * (c // N_RAW + 1)

        def col(name, n=0, width=1):
            a = COL[name] + n
            return par[:, a:a + width]

        def head_cols(g):
            return K_COL + g * HD, Q_COL + 2 * g * HD, Q_COL + (2 * g + 1) * HD

        def pt_bank(h, k):
            return 4 + (h + k) % 4

        def kq_bank(g, b):
            return (3 * g + b) % 4 if g < 2 else pt_bank(2 * g - 3, b)

        END_C = FFN_C + 32 + 24 * (ROUNDS - 2)
        END_G = DOWN_G + 6 * (ROUNDS - 2)

        wi = w_in.rearrange("(k p) n -> p k n", p=P)
        wu = w_up.rearrange("(k p) n -> p k n", p=P)
        wd = w_down.rearrange("(k p) n -> p k n", p=P)
        wo = w_out.rearrange("(k p) n -> p k n", p=P)
        wa = w_attn_o.rearrange("(k p) n -> p k n", p=P)
        wc = w_conv_o.rearrange("(k p) n -> p k n", p=P)
        x_tiles = x.rearrange("(t p) d -> t p d", p=P)
        y_tiles = y.rearrange("(t p) d -> t p d", p=P)

        block = ctx.enter_context(nc.Block())

        @block.sync
        def _(sp):
            def load(c, src, i=None, per=0):
                slot, landed = chunk_slot(c)
                if c >= N_RAW or i is not None:
                    sp.wait_ge(low_split, val(c - N_RAW + 1, i, per))
                dst = w_raw[:, slot, :].rearrange("p (k n) -> p k n", k=src.shape[1])
                sp.dma_start(dst, src).then_inc(chunk_loaded[slot], 16)

            def load_pair(c, src_a, src_b, col_a, col_b, chunks, i=None, per=0):
                for half, (src, c0) in enumerate(((src_a, col_a), (src_b, col_b))):
                    for q in range(chunks):
                        load(c + half * chunks + q, src[:, 4 * q:4 * q + 4, bass.ds(c0, 256)], i, per)

            def load_wide(c, src, col0, i=None, per=0):
                for q in range(8):
                    load(c + q, src[:, 2 * q:2 * q + 2, bass.ds(col0, 512)], i, per)

            x_by_token = x.rearrange("(t p) d -> p t d", p=P)
            sp.dma_start(x_in[:, :, 0:256], x_by_token[:, :, 0:256]).then_inc(x_head_loaded, 16)
            for n in range(4):
                part = slice(512 * n + 256 * (n == 0), 512 * n + 512)
                sp.dma_start(x_in[:, :, part], x_by_token[:, :, part]).then_inc(x_loaded[n], 16)
                if n in (0, 1):
                    load(GLU_C + n, wi[:, 4 * n:4 * n + 4, GLU_COL:GLU_COL + 256])
            for q in range(2, 8):
                c0 = GLU_COL + CONV_CH * (q // 4)
                load(GLU_C + q, wi[:, 4 * (q % 4):4 * (q % 4) + 4, c0:c0 + 256])
            with sp.Fori(0, 3) as i:
                load_pair(GLU_C + 8, wi, wi, i * 256 + (GLU_COL + 256),
                          i * 256 + (GLU_COL + CONV_CH + 256), 4, i, 8)
            load_wide(QKV_C, wi, K_COL)
            with sp.Fori(0, 2) as i:
                load_wide(QKV_C + 8, wi, i * 512 + Q_COL, i, 8)
            load_wide(QKV_C + 24, wi, V_COL)
            with sp.Fori(0, 8) as i:
                load_pair(GATE_C, wi, wi, i * 256 + GATE_COL, i * 256 + (GATE_COL + D), 4, i, 8)
            with sp.Fori(0, 8) as i:
                load_pair(MIX_C, wa, wc, i * 256, i * 256, 2, i, 4)
            sp.wait_ge(oc_low_ready, 4)
            for q in range(8):
                load(OUT_C + q, wo[:, 2 * q:2 * q + 2, 0:512])
                if q % 2 == 1:
                    t = q // 2
                    sp.dma_start(x_res[:, t, :], x_tiles[t]).then_inc(xres_loaded, 16)
            with sp.Fori(0, 3) as i:
                load_wide(OUT_C + 8, wo, i * 512 + 512, i, 8)
            for a in range(4):
                load_pair(FFN_C + 8 * a, wu, wu, 256 * a, FFN + 256 * a, 4)

            def down_chunk(r, j):
                q, k = j // 2, j % 2
                return wd[:, bass.ds(r + 2 * k, 2), 512 * q:512 * q + 512]

            with sp.Fori(0, ROUNDS - 2) as i:
                for j in range(8):
                    load(FFN_C + 32 + j, down_chunk(i * 4, j), i, 24)
                for a in range(2):
                    load_pair(FFN_C + 40 + 8 * a, wu, wu, i * 512 + (1024 + 256 * a),
                              i * 512 + (FFN + 1024 + 256 * a), 4, i, 24)
            for j in range(8):
                for k in range(2):
                    load(END_C + 2 * j + k, down_chunk(4 * (ROUNDS - 2 + k), j))
            for t in range(TT):
                for half, ready in enumerate((y_left_ready, y_right_ready)):
                    part = slice(half * D // 2, (half + 1) * D // 2)
                    sp.wait_ge(ready, t + 1)
                    sp.dma_start(y_tiles[t][:, part], x_res[:, t, part]).then_inc(y_stored, 16)
            sp.wait_ge(y_stored, 16 * 2 * TT)

        @block.gpsimd
        def _(pool):
            steps = [0]

            def step(ins):
                ins.then_inc(pool_step, 1)
                steps[0] += 1
                pool.wait_ge(pool_step, steps[0])

            step(pool.memset(ident[:, :], 0.0))
            pool.affine_select(out=ident[:, :], in_=ident[:, :], compare_op=ALU.not_equal, fill=1.0,
                               base=0, pattern=[[-1, P]], channel_multiplier=1).then_inc(consts_made, 1)
            pool.memset(mean_w[:, :], 1.0 / CONV_CH).then_inc(consts_made, 1)
            pool.memset(neg_half[:, :], -0.5).then_inc(consts_made, 1)
            pool.memset(conv[:, :, 0:REACH], 0.0).then_inc(consts_made, 1)
            pool.memset(conv[:, :, REACH + SEQ:PADDED], 0.0).then_inc(consts_made, 1)
            pool.wait_ge(consts_made, 5)

            def root(w):
                pool.wait_ge(meansq_ready, w + 1)
                pool.tensor_tensor(rstd[:, TT * w:TT * w + TT], meansq[:, TT * w:TT * w + TT],
                                   neg_half[:, :].to_broadcast([P, TT]), ALU.pow).then_inc(rstd_ready, 1)

            root(0)

            def centre(i):
                return conv[:, i, REACH:REACH + SEQ]

            for i in range(POOL_CONV_TILES):
                if i % 2 == 0:
                    pool.wait_ge(glu_done, i + 2)
                if i == 0:
                    pool.wait_ge(par_loaded, 16)
                w0 = COL["conv_w"] + i * CONV_K
                step(pool.tensor_tensor(pool_acc[:, :], conv[:, i, 0:SEQ],
                                        par[:, w0:w0 + 1].to_broadcast([P, SEQ]), ALU.mult))
                for k in range(1, CONV_K):
                    step(pool.tensor_tensor(pool_tap[:, :], conv[:, i, k:k + SEQ],
                                            par[:, w0 + k:w0 + k + 1].to_broadcast([P, SEQ]), ALU.mult))
                    step(pool.tensor_tensor(pool_acc[:, :], pool_acc[:, :], pool_tap[:, :], ALU.add))
                step(pool.tensor_tensor(centre(i), pool_acc[:, :],
                                        col("conv_b", i).to_broadcast([P, SEQ]), ALU.add))
            pool.wait_ge(o_ready, HEADS)
            step(pool.tensor_tensor(ch_sum[:, :], centre(0), centre(1), ALU.add))
            for i in range(2, KC):
                if i >= POOL_CONV_TILES:
                    pool.wait_ge(vec_conv_done, i - POOL_CONV_TILES + 1)
                ins = pool.tensor_tensor(ch_sum[:, :], ch_sum[:, :], centre(i), ALU.add)
                if i < KC - 1:
                    step(ins)
                else:
                    ins.then_inc(ch_sum_ready, 1)
            pool.wait_ge(ch_sq_ready, 2)
            pool.tensor_tensor(sq_sum[:, :], ch_sq[:, 0, :], ch_sq[:, 1, :], ALU.add).then_inc(ch_sq_added, 2)
            for i in range(2, KC):
                pool.wait_ge(ch_sq_ready, i + 1)
                pool.wait_ge(ch_sq_added, i)
                pool.tensor_tensor(sq_sum[:, :], sq_sum[:, :], ch_sq[:, i % 2, :],
                                   ALU.add).then_inc(ch_sq_added, 1)

            def one(t, j):
                return t[:, bass.ds(j, 1), :].rearrange("p a n -> p (a n)")

            def mix_pair(n, i=None):
                for b in range(2):
                    if b == 0:
                        pool.wait_ge(mix_gated, val(n + 1, i, 1))
                    else:
                        pool.wait_ge(group_freed, freed(MIX_G + n, i, 1))
                    if n > 0:
                        pool.wait_ge(m_low_ready, val(2 * n, i, 2))
                    pool.tensor_tensor(mix_m[:, b, :], mix_a[:, b, :], mix_c[:, b, :],
                                       ALU.add).then_inc(m_ready, 1)
                for b in range(2):
                    j = val(2 * n + b, i, 2)
                    pool.wait_ge(m_high_ready, val(2 * n + b + 1, i, 2))
                    pool.tensor_tensor(one(m_low, j), mix_m[:, b, :], one(m_high, j).bitcast(F32),
                                       ALU.subtract).then_inc(m_low_ready, 1)

            mix_pair(0)
            with pool.Fori(0, KD // 2 - 1) as i:
                mix_pair(1, i)
            root(1)

            def u_lows(n, i=None):
                buf, k = n // 4 % 2, n % 4
                for b in range(2):
                    pool.wait_ge(u_high_ready, val(n + b + 1, i, 8))
                    pool.tensor_tensor(u_low[:, buf, k + b, :], f_u[:, b, :],
                                       u_high[:, buf, k + b, :].bitcast(F32),
                                       ALU.subtract).then_inc(u_low_ready, 1)

            with pool.Fori(0, KF // 8) as i:
                for n in range(0, 8, 2):
                    u_lows(n, i)
            for n in range(KF // 8 * 8, KF, 2):
                u_lows(n)
            pool.wait_ge(gfin_loaded, 16)
            for t in range(TT):
                for q in range(2):
                    part = slice(512 * q, 512 * q + 512)
                    pool.wait_ge(x_added, 4 * t + q + 1)
                    if t >= 2:
                        pool.wait_ge(y_left_ready, t - 1)
                    pool.tensor_tensor(x_g[:, t % 2, part], x_res[:, t, part], g_fin[:, part],
                                       ALU.mult).then_inc(x_g_ready, 1)
                n = 2 * TT + t
                pool.wait_ge(meansq_ready, 3 + t)
                pool.tensor_tensor(rstd[:, n:n + 1], meansq[:, n:n + 1], neg_half[:, :],
                                   ALU.pow).then_inc(rstd_ready, 1)

        @block.scalar
        def _(act):
            act.dma_start(par[:, :], cols).then_inc(par_loaded, 16)

            def split(c, i=None, per=0):
                slot, landed = chunk_slot(c)
                act.wait_ge(chunk_loaded[slot], val(landed, i, per * 16 // N_RAW))
                if c >= N_SPLIT or i is not None:
                    act.wait_ge(chunk_used, val(c - N_SPLIT + 1, i, per))
                act.activation(w_high[:, c % N_SPLIT, :], w_raw[:, slot, :], ACT.Copy).then_inc(high_split, 1)

            def squares(w, n, src):
                for t in range(TT):
                    if w + n + t > 0:
                        act.wait_ge(squares_summed, 16 * w + 4 * n + t)
                    act.activation(sq_junk[:, :], src[:, t, 512 * n:512 * n + 512], ACT.Square,
                                   accum_out=sq_part[:, 16 * w + 4 * t + n:16 * w + 4 * t + n + 1]
                                   ).then_inc(squares_summed, 1)

            def turned_high(w, n, s, tiles=range(4)):
                for k in [4 * n + b for b in tiles]:
                    act.wait_ge(x_turned, KD * w + k + 1)
                    act.activation(h_high[:, k, :], bank[s + k % 4][:, :], ACT.Copy,
                                   scale=col("g_ffn" if w else "g_mix", k)).then_inc(h_high_ready, 1)

            def glu_sigmoid(g):
                for b in range(2):
                    act.wait_ge(glu_scaled, 2 * g + b + 1)
                    act.activation(glu_gate[:, b, :], glu_gate[:, b, :], ACT.Sigmoid,
                                   bias=col("b_glu", KC + 2 * g + b)).then_inc(glu_gate_ready, 1)

            act.wait_ge(consts_made, 5)
            act.activation(sq_junk[:, 0:1], neg_half[:, :], ACT.Copy).then_inc(table_fetched, 1)
            act.wait_ge(table_fetched, 1)
            act.wait_ge(par_loaded, 16)
            for g in range(4):
                for q in range(8):
                    if g == 0 and q < 4:
                        turned_high(0, q, 4, (0, 1))
                    split(GLU_C + 8 * g + q)
                    if g == 0 and q < 4:
                        turned_high(0, q, 4, (2, 3))
                    if g == 1 and q == 0:
                        for dst, src in ((qkg[:, :, :], qk_g.partition_broadcast(P)),
                                         (rope_cs[:, :, :, :], rope),
                                         (b_qkv_all[:, :], b_qkv.partition_broadcast(P))):
                            act.dma_start(dst, src).then_inc(qkv_par_loaded, 16)
                    if g == 0 and q >= 4:
                        act.wait_ge(x_loaded[q - 4], 16)
                        squares(0, q - 4, x_in)
                    if g >= 1 and q == 3:
                        glu_sigmoid(g - 1)

            def kq_evac(g):
                for b, c0 in enumerate(head_cols(g)):
                    act.wait_ge(kq_turned, 3 * g + b + 1)
                    act.activation(qkv_high[:, :, c0:c0 + HD],
                                   bank[kq_bank(g, b)][:, :].rearrange("p (t d) -> p t d", t=TT),
                                   ACT.Copy).then_inc(kq_high_ready, 1)

            def v_split(g):
                if g == 0:
                    act.wait_ge(group_freed, freed(QKV_G + 3))
                else:
                    act.wait_ge(o_summed, 2 * g)
                act.activation(v_high[:, :, :], qkv[:, :, V_COL + g * HD:V_COL + (g + 1) * HD],
                               ACT.Copy).then_inc(v_high_ready, 1)

            def exps(h):
                for t in range(TT):
                    n = 4 * h + t
                    act.wait_ge(exp_bias_ready, n + 1)
                    if h >= 2:
                        act.wait_ge(probs_turned, 4 * (h - 1))
                    act.activation(probs[:, h % 2, t, :], bank[t][:, :], ACT.Exp, bias=exp_bias[:, n:n + 1],
                                   scale=float(HD) ** -0.5,
                                   accum_out=row_sum[:, n:n + 1]).then_inc(exp_ready, 1)

            def pt_evac(h):
                for k in range(TT):
                    act.wait_ge(probs_turned, 4 * h + k + 1)
                    act.activation(pt_high[:, k, :], bank[pt_bank(h, k)][:, :],
                                   ACT.Copy).then_inc(pt_high_ready, 1)

            qk_cols = (K_COL, Q_COL, Q_COL + 512)
            for g in range(4):
                for q in range(8):
                    split(QKV_C + 8 * g + q)
                    if g == 0 and q == 3:
                        glu_sigmoid(3)
                    if g >= 1 and q == 2:
                        act.wait_ge(group_freed, freed(QKV_G + g - 1))
                        if g >= 2:
                            act.wait_ge(qk_ms_ready, g - 1)
                        act.activation(qk_sq[:, :, :].rearrange("p (t h) d -> p t (h d)", t=TT),
                                       qkv[:, :, qk_cols[g - 1]:qk_cols[g - 1] + 512],
                                       ACT.Square).then_inc(qk_squared, 1)
                    if g >= 1 and q == 3:
                        act.wait_ge(qk_ms_ready, g)
                        act.activation(qk_root[:, :], qk_ms[:, :], ACT.Sqrt).then_inc(qk_root_ready, 1)
                    if g == 3 and q == 4:
                        kq_evac(0)
                    if g == 3 and q == 5:
                        kq_evac(1)
                    if g == 3 and q == 7:
                        exps(0)
            split(GATE_C)
            v_split(0)
            exps(1)
            for h in range(HEADS):
                pt_evac(h)
                if h + 2 < HEADS:
                    exps(h + 2)
                if h in (0, 2):
                    kq_evac(h // 2 + 2)
                act.wait_ge(o_summed, h + 1)
                act.activation(o_full[:, h, :], bank[pt_bank(h, 0)][:, :], ACT.Copy).then_inc(o_ready, 1)
                if h % 2 == 1 and h + 1 < HEADS:
                    v_split((h + 1) // 2)
            split(GATE_C + 1)

            def gate_out(g, b):
                j = 2 * g + b
                if b == 0:
                    act.wait_ge(gate_scaled, g + 1)
                else:
                    act.wait_ge(group_freed, freed(GATE_G + g))
                for gate, c0 in ((gate_a, 0), (gate_c, KD)):
                    act.activation(gate[:, j, :], gate[:, j, :], ACT.Sigmoid,
                                   bias=col("b_gate", c0 + j)).then_inc(gate_stored, 1)

            def oc_high(n):
                act.wait_ge(chunk_used, used(GATE_C + 7 * 8 + 4 + n))
                if n < 2:
                    act.activation(o_high[:, 4 * n:4 * n + 4, :], o_full[:, 4 * n:4 * n + 4, :],
                                   ACT.Copy).then_inc(oc_high_ready, 1)
                else:
                    k = 4 * (n - 2)
                    act.wait_ge(c_swished, k + 4)
                    act.activation(c_high[:, k:k + 4, :], conv[:, k:k + 4, REACH:REACH + SEQ],
                                   ACT.Copy).then_inc(oc_high_ready, 1)

            def centre(i):
                return conv[:, i, REACH:REACH + SEQ]

            for g in range(8):
                for q in range(8):
                    if g > 0 or q > 1:
                        split(GATE_C + 8 * g + q)
                    if g >= 1 and q in (2, 3):
                        gate_out(g - 1, q - 2)
                    if g == 5 and 3 <= q <= 6:
                        for i in (2 * (q - 3), 2 * (q - 3) + 1):
                            act.wait_ge(centred, i + 1)
                            if i >= 2:
                                act.wait_ge(ch_sq_added, i - 1 if i > 2 else 2)
                            act.activation(ch_sq[:, i % 2, :], centre(i), ACT.Square).then_inc(ch_sq_ready, 1)
                    if g == 6 and q == 1:
                        act.wait_ge(var_copied, 1)
                        act.activation(ch_sq[:, 0, :], var_sb[:, :], ACT.Sqrt).then_inc(ln_root_ready, 1)
                    if (g == 6 and q >= 5) or (g == 7 and q == 0):
                        pair = (q - 5) % 8
                        for i in (2 * pair, 2 * pair + 1):
                            act.wait_ge(c_normed, i + 1)
                            act.activation(centre(i), centre(i), ACT.Silu, bias=col("ln_b", i),
                                           scale=col("ln_g", i)).then_inc(c_swished, 1)
                    if g == 7 and q >= 6:
                        oc_high(q - 6)

            def m_highs(j, b, dst, i=None, per=0):
                act.wait_ge(m_ready, val(j + 1, i, per))
                act.activation(dst, mix_m[:, b, :], ACT.Copy).then_inc(m_high_ready, 1)

            for q in range(4):
                split(MIX_C + q)
                if q < 2:
                    oc_high(2 + q)
                if q in (2, 3):
                    gate_out(7, q - 2)
            with act.Fori(0, 7) as i:
                for q in range(4):
                    split(MIX_C + 4 + q, i, 4)
                    if q >= 2:
                        j = i * 2 + (q - 2)
                        m_highs(q - 2, q - 2, m_high[:, bass.ds(j, 1), :].rearrange("p a n -> p (a n)"), i, 2)
            for g in range(4):
                for q in range(8):
                    split(OUT_C + 8 * g + q)
                    if g == 0 and q in (2, 3):
                        m_highs(KD - 2 + q - 2, q - 2, m_high[:, KD - 2 + q - 2, :])
                    if g >= 1 and q == 3:
                        act.wait_ge(group_freed, freed(OUT_G + g - 1))
                        squares(1, g - 1, x_res)
                    if g >= 1 and q == 5:
                        turned_high(1, g - 1, 4 * ((g - 1) % 2))

            def up_slot(q, n, buf, i=None):
                a = n // 2 % 2
                for b in range(2):
                    ft = val(n + b, i, 8)
                    if q == 3:
                        act.wait_ge(up_scaled, ft + 1)
                        act.activation(f_gate[:, b, :], f_raw[:, b, :], ACT.Identity,
                                       bias=par[:, bass.ds(ft + COL["ffn_b"], 1)],
                                       scale=par[:, bass.ds(ft * 3 + (COL["ffn_w"] + 1), 1)]
                                       ).then_inc(tap_mid_ready, 1)
                    if q == 5:
                        act.wait_ge(taps_ready, ft + 1)
                        act.activation(f_gate[:, b, :], f_gate[:, b, :], ACT.Silu).then_inc(silu_ready, 1)
                    if q == 7:
                        act.wait_ge(u_ready, ft + 1)
                        act.activation(u_high[:, buf, 2 * a + b, :], f_u[:, b, :],
                                       ACT.Copy).then_inc(u_high_ready, 1)

            for g in range(4):
                for q in range(8):
                    split(FFN_C + 8 * g + q)
                    if g == 0 and q == 1:
                        turned_high(1, 3, 4)
                    if g == 0 and q == 3:
                        squares(1, 3, x_res)
                    if g == 1 and q == 0:
                        act.dma_start(g_fin[:, :], g_final.partition_broadcast(P)).then_inc(gfin_loaded, 16)
                    if g >= 1:
                        up_slot(q, 2 * g - 2, (g - 1) // 2)

            def ffn_round(r, i=None):
                c = FFN_C + 32 + 24 * r
                for q in range(8):
                    split(c + q, i, 48)
                    up_slot(q, 4 * r + 6, (r + 1) % 2, i)
                for q in range(8):
                    split(c + 8 + q, i, 48)
                for q in range(8):
                    split(c + 16 + q, i, 48)
                    up_slot(q, 4 * r + 8, r % 2, i)

            with act.Fori(0, (ROUNDS - 3) // 2) as i:
                ffn_round(0, i)
                ffn_round(1, i)
            ffn_round(ROUNDS - 3)
            for j in range(8):
                for k, dst in enumerate((w_high[:, j % N_SPLIT, :], last_high[:, j, :])):
                    n = END_C + 2 * j + k
                    slot, landed = chunk_slot(n)
                    act.wait_ge(chunk_loaded[slot], landed)
                    act.wait_ge(chunk_used, used(END_C + max(j - N_SPLIT, -1) if k else END_C + j - N_SPLIT))
                    act.activation(dst, w_raw[:, slot, :], ACT.Copy).then_inc(high_split, 1)
                up_slot(j, KF - 2, (ROUNDS - 1) % 2)
            for t in range(TT):
                for q in range(4):
                    part = slice(512 * q, 512 * q + 512)
                    act.wait_ge(x_added, 4 * t + q + 1)
                    if t > 0:
                        act.wait_ge(squares_summed, 32 + 4 * (t - 1) + q + 1)
                    act.activation(y_junk[:, part], x_res[:, t, part], ACT.Square,
                                   accum_out=sq_part[:, 32 + 4 * t + q:32 + 4 * t + q + 1]
                                   ).then_inc(squares_summed, 1)
                act.wait_ge(x_g_ready, 2 * t + 2)
                act.wait_ge(rstd_ready, 3 + t)
                act.activation(x_res[:, t, 0:D // 2], x_g[:, t % 2, :], ACT.Copy,
                               scale=rstd[:, 2 * TT + t:2 * TT + t + 1]).then_inc(y_left_ready, 1)

        @block.vector
        def _(dve):
            steps = [0]

            def step(ins, wait=True):
                ins.then_inc(vec_step, 1)
                steps[0] += 1
                if wait:
                    dve.wait_ge(vec_step, steps[0])

            def split(c, i=None, per=0):
                slot, _ = chunk_slot(c)
                b = c % N_SPLIT
                dve.wait_ge(high_split, val(c + 1, i, per))
                dve.tensor_tensor(w_low[:, b, :], w_raw[:, slot, :], w_high[:, b, :].bitcast(F32),
                                  ALU.subtract).then_inc(low_split, 1)

            def turned_low(w, n, s, tiles=range(4)):
                for k in [4 * n + b for b in tiles]:
                    dve.wait_ge(h_high_ready, KD * w + k + 1)
                    dve.scalar_tensor_tensor(out=h_low[:, k, :], in0=bank[s + k % 4][:, :],
                                             scalar=col("g_ffn" if w else "g_mix", k),
                                             in1=h_high[:, k, :].bitcast(F32), op0=ALU.mult,
                                             op1=ALU.subtract).then_inc(h_low_ready, 1)

            def mean_square(w):
                dve.wait_ge(squares_summed, 16 * w + 16)
                t4 = slice(TT * w, TT * w + TT)
                step(dve.tensor_reduce(sumsq[:, t4],
                                       sq_part[:, 16 * w:16 * w + 16].rearrange("p (t n) -> p t n", t=TT),
                                       AX.X, ALU.add))
                dve.tensor_scalar(meansq[:, t4], sumsq[:, t4], 1.0 / D, EPS, ALU.mult,
                                  ALU.add).then_inc(meansq_ready, 1)

            def copy_rstd(w):
                dve.wait_ge(rstd_spread, w + 1)
                dve.tensor_copy(rstd_all[:, :], bank[7][:, :]).then_inc(rstd_copied, 1)
                dve.wait_ge(rstd_copied, w + 1)

            def scaled(out, ps):
                return dve.tensor_tensor(out, ps[:, :], rstd_all[:, :], ALU.mult)

            def glu_slot(q, g):
                s = 4 * (g % 2)
                if q == 2:
                    dve.wait_ge(chunk_used, used(GLU_C + 8 * g + 7))
                    if g == 0:
                        dve.wait_ge(consts_made, 5)
                    else:
                        dve.wait_ge(glu_done, 2 * g)
                    for b in range(2):
                        scaled(glu_gate[:, b, :], bank[s + 2 + b]).then_inc(glu_scaled, 1)
                    for b in range(2):
                        ins = scaled(conv[:, 2 * g + b, REACH:REACH + SEQ], bank[s + b])
                    ins.then_inc(group_freed, 1)
                if q == 4:
                    dve.wait_ge(group_freed, freed(GLU_G + g))
                    for b in range(2):
                        dve.wait_ge(glu_gate_ready, 2 * g + b + 1)
                        tile = conv[:, 2 * g + b, REACH:REACH + SEQ]
                        dve.scalar_tensor_tensor(out=tile, in0=tile, scalar=col("b_glu", 2 * g + b),
                                                 in1=glu_gate[:, b, :], op0=ALU.add,
                                                 op1=ALU.mult).then_inc(glu_done, 1)

            dve.wait_ge(par_loaded, 16)
            for g in range(4):
                for q in range(8):
                    if g == 0 and q < 4:
                        turned_low(0, q, 4, (0, 1))
                    if g == 1 and q == 0:
                        mean_square(0)
                    split(GLU_C + 8 * g + q)
                    if g == 0 and q < 4:
                        turned_low(0, q, 4, (2, 3))
                    if g == 1 and q == 1:
                        copy_rstd(0)
                    if g >= 1:
                        glu_slot(q, g - 1)

            qk_cols = (K_COL, Q_COL, Q_COL + 512)

            def add_bias(e, c0):
                for t in range(TT):
                    ins = dve.scalar_tensor_tensor(out=qkv[:, t, c0:c0 + 512], in0=bank[4 * (e % 2) + t][:, :],
                                                   scalar=rstd[:, t:t + 1], in1=b_qkv_all[:, c0:c0 + 512],
                                                   op0=ALU.mult, op1=ALU.add)
                ins.then_inc(group_freed, 1)

            def qk_slot(q, e):
                c0 = qk_cols[e]
                h = qkv[:, :, c0:c0 + 512].rearrange("p t (h d) -> p t h d", h=4)
                if q == 1:
                    dve.wait_ge(chunk_used, used(QKV_C + 8 * e + 7))
                    add_bias(e, c0)
                if q == 3:
                    dve.wait_ge(qk_squared, e + 1)
                    step(dve.tensor_reduce(qk_ss[:, :], qk_sq[:, :, :], AX.X, ALU.add))
                    dve.tensor_scalar(qk_ms[:, :], qk_ss[:, :], 1.0 / HD, EPS, ALU.mult,
                                      ALU.add).then_inc(qk_ms_ready, 1)
                if q == 4:
                    dve.wait_ge(qk_root_ready, e + 1)
                    step(dve.reciprocal(qk_r0[:, :], qk_root[:, :]))
                    step(dve.tensor_tensor(qk_t[:, :], qk_r0[:, :], qk_r0[:, :], ALU.mult))
                    step(dve.tensor_tensor(qk_t[:, :], qk_t[:, :], qk_ms[:, :], ALU.mult))
                    step(dve.tensor_scalar(qk_t[:, :], qk_t[:, :], -0.5, 1.5, ALU.mult, ALU.add))
                    step(dve.tensor_tensor(qk_rstd[:, :], qk_r0[:, :], qk_t[:, :], ALU.mult))
                    dve.wait_ge(group_freed, freed(QKV_G + e))
                    for t in range(TT):
                        ins = dve.tensor_tensor(h[:, t], h[:, t],
                                                qk_rstd[:, 4 * t:4 * t + 4].unsqueeze(2).to_broadcast([P, 4, HD]),
                                                ALU.mult)
                    step(ins)
                if q == 5:
                    g = qkg[:, 1 if e == 0 else 0, :].unsqueeze(1).to_broadcast([P, 4, HD])
                    for t in range(TT):
                        ins = dve.tensor_tensor(h[:, t], h[:, t], g, ALU.mult)
                    step(ins)
                if q in (6, 7):
                    pairs = qkv[:, :, c0:c0 + 512].rearrange("p t (h j two) -> p t h j two", h=4, two=2)
                    for t in range(TT):
                        x0, x1 = pairs[:, t, :, :, 0], pairs[:, t, :, :, 1]
                        cos = rope_cs[:, 0, t, :].unsqueeze(1).to_broadcast([P, 4, HD // 2])
                        sin = rope_cs[:, 1, t, :].unsqueeze(1).to_broadcast([P, 4, HD // 2])
                        if q == 6:
                            if e >= 1 and t == 0:
                                dve.wait_ge(roped, e)
                            dve.tensor_tensor(rope_a[:, t], x0, cos, ALU.mult)
                            dve.tensor_tensor(rope_b[:, t], x1, sin, ALU.mult)
                            ins = dve.tensor_tensor(rope_d[:, t], x0, sin, ALU.mult)
                        else:
                            dve.tensor_tensor(x0, rope_a[:, t], rope_b[:, t], ALU.subtract)
                            ins = dve.tensor_tensor(x1, x1, cos, ALU.mult)
                    step(ins)
                    if q == 7:
                        for t in range(TT):
                            x1 = pairs[:, t, :, :, 1]
                            ins = dve.tensor_tensor(x1, x1, rope_d[:, t], ALU.add)
                        ins.then_inc(roped, 1)

            def kq_evac(g):
                for b, c0 in enumerate(head_cols(g)):
                    dve.wait_ge(kq_high_ready, 3 * g + b + 1)
                    dve.tensor_tensor(kq_low[:, g % 2, b, :].rearrange("p (t d) -> p t d", t=TT),
                                      bank[kq_bank(g, b)][:, :].rearrange("p (t d) -> p t d", t=TT),
                                      qkv_high[:, :, c0:c0 + HD].bitcast(F32),
                                      ALU.subtract).then_inc(kq_low_ready, 1)

            def v_split(g):
                dve.wait_ge(v_high_ready, g + 1)
                dve.tensor_tensor(v_low[:, :, :], qkv[:, :, V_COL + g * HD:V_COL + (g + 1) * HD],
                                  v_high[:, :, :].bitcast(F32), ALU.subtract).then_inc(v_low_ready, 1)

            def maxima(h):
                done = {}
                for t in range(TT + 1):
                    if t < TT:
                        n = 4 * h + t
                        dve.wait_ge(scores_ready, n + 1)
                        step(dve.tensor_reduce(neg_max[:, n:n + 1], bank[t][:, :], AX.X, ALU.max, negate=True),
                             wait=False)
                        done[t] = steps[0]
                    if t > 0:
                        n = 4 * h + t - 1
                        dve.wait_ge(vec_step, done[t - 1])
                        dve.tensor_scalar(exp_bias[:, n:n + 1], neg_max[:, n:n + 1], float(HD) ** -0.5, None,
                                          ALU.mult).then_inc(exp_bias_ready, 1)

            def normalise(h):
                done = {}
                for t in range(TT + 1):
                    if t < TT:
                        n = 4 * h + t
                        dve.wait_ge(exp_ready, n + 1)
                        step(dve.reciprocal(row_inv[:, n:n + 1], row_sum[:, n:n + 1]), wait=False)
                        done[t] = steps[0]
                    if t > 0:
                        n = 4 * h + t - 1
                        dve.wait_ge(vec_step, done[t - 1])
                        dve.tensor_scalar(probs[:, h % 2, t - 1, :], probs[:, h % 2, t - 1, :],
                                          row_inv[:, n:n + 1], None, ALU.mult).then_inc(probs_ready, 1)

            def pt_evac(h):
                for k in range(TT):
                    dve.wait_ge(pt_high_ready, 4 * h + k + 1)
                    dve.tensor_tensor(pt_low[:, k, :], bank[pt_bank(h, k)][:, :],
                                      pt_high[:, k, :].bitcast(F32), ALU.subtract).then_inc(pt_low_ready, 1)

            dve.wait_ge(qkv_par_loaded, 16 * 3)
            for g in range(4):
                for q in range(8):
                    split(QKV_C + 8 * g + q)
                    if g == 0:
                        glu_slot(q, 3)
                    if g >= 1:
                        qk_slot(q, g - 1)
                    if g == 3 and q == 4:
                        kq_evac(0)
                    if g == 3 and q == 5:
                        kq_evac(1)
            maxima(0)
            normalise(0)
            split(GATE_C)
            dve.wait_ge(chunk_used, used(QKV_C + 31))
            add_bias(3, V_COL)

            maxima(1)
            normalise(1)
            v_split(0)
            for h in range(HEADS):
                pt_evac(h)
                if h + 2 < HEADS:
                    maxima(h + 2)
                if h in (0, 2):
                    kq_evac(h // 2 + 2)
                if h + 2 < HEADS:
                    normalise(h + 2)
                if h % 2 == 1 and h + 1 < HEADS:
                    v_split((h + 1) // 2)
            split(GATE_C + 1)

            def centre(i):
                return conv[:, i, REACH:REACH + SEQ]

            def conv_taps(i, k0, k1):
                w0 = COL["conv_w"] + i * CONV_K
                for k in range(k0, k1):
                    if k == 0:
                        step(dve.tensor_scalar(vec_acc[:, :], conv[:, i, 0:SEQ], par[:, w0:w0 + 1],
                                               col("conv_b", i), ALU.mult, ALU.add))
                    elif k < CONV_K:
                        step(dve.scalar_tensor_tensor(out=vec_acc[:, :], in0=conv[:, i, k:k + SEQ],
                                                      scalar=par[:, w0 + k:w0 + k + 1], in1=vec_acc[:, :],
                                                      op0=ALU.mult, op1=ALU.add))
                    else:
                        dve.tensor_copy(centre(i), vec_acc[:, :]).then_inc(vec_conv_done, 1)
                        dve.wait_ge(vec_conv_done, i - POOL_CONV_TILES + 1)

            def oc_low(n):
                dve.wait_ge(oc_high_ready, n + 1)
                k = 4 * (n % 2)
                if n < 2:
                    low, high, full = o_low, o_high, o_full[:, k:k + 4, :]
                else:
                    low, high, full = c_low, c_high, conv[:, k:k + 4, REACH:REACH + SEQ]
                dve.tensor_tensor(low[:, k:k + 4, :], full, high[:, k:k + 4, :].bitcast(F32),
                                  ALU.subtract).then_inc(oc_low_ready, 1)

            def gates_scaled(g):
                dve.wait_ge(chunk_used, used(GATE_C + 8 * g + 7))
                s = 4 * (g % 2)
                for b in range(2):
                    scaled(gate_a[:, 2 * g + b, :], bank[s + b])
                    ins = scaled(gate_c[:, 2 * g + b, :], bank[s + 2 + b])
                    ins.then_inc(gate_scaled if b == 0 else group_freed, 1)

            dve.wait_ge(o_ready, HEADS)
            for g in range(8):
                for q in range(8):
                    if g > 0 or q > 1:
                        split(GATE_C + 8 * g + q)
                    if g < KC - POOL_CONV_TILES:
                        conv_taps(POOL_CONV_TILES + g, 4 * q, 4 * q + 4)
                    if g >= 1 and q == 2:
                        gates_scaled(g - 1)
                    if g == 5 and q == 1:
                        dve.wait_ge(mean_ready, 1)
                        dve.tensor_copy(mean_sb[:, :], bank[7][:, :]).then_inc(mean_copied, 1)
                        dve.wait_ge(mean_copied, 1)
                    if g == 5 and 2 <= q <= 5:
                        for i in (2 * (q - 2), 2 * (q - 2) + 1):
                            dve.tensor_tensor(centre(i), centre(i), mean_sb[:, :],
                                              ALU.subtract).then_inc(centred, 1)
                    if g == 6 and q == 1:
                        dve.wait_ge(var_ready, 1)
                        dve.tensor_scalar(var_sb[:, :], bank[3][:, :], EPS, None, ALU.add).then_inc(var_copied, 1)
                    if g == 6 and q == 3:
                        root, r0, t = ch_sq[:, 0, :], ch_sq[:, 1, :], sq_sum[:, :]
                        dve.wait_ge(ln_root_ready, 1)
                        step(dve.reciprocal(r0, root))
                        step(dve.tensor_tensor(t, r0, r0, ALU.mult))
                        step(dve.tensor_tensor(t, t, var_sb[:, :], ALU.mult))
                        step(dve.tensor_scalar(t, t, -0.5, 1.5, ALU.mult, ALU.add))
                        step(dve.tensor_tensor(ln_rstd[:, :], r0, t, ALU.mult))
                    if g == 6 and 4 <= q <= 7:
                        for i in (2 * (q - 4), 2 * (q - 4) + 1):
                            dve.tensor_tensor(centre(i), centre(i), ln_rstd[:, :],
                                              ALU.mult).then_inc(c_normed, 1)
                    if g == 7 and q >= 6:
                        oc_low(q - 6)

            def mix_slot(q, g, i=None):
                if q not in (1, 2):
                    return
                b, s = q - 1, 4 * (g % 2)
                j = val(2 * g + b, i, 4)
                if b == 0:
                    dve.wait_ge(chunk_used, used(MIX_C + 4 * g + 3, i, 8))
                    if g > 0:
                        dve.wait_ge(m_ready, val(2 * g, i, 4))
                for mixed, gate, ps in ((mix_a, gate_a, bank[s + b]), (mix_c, gate_c, bank[s + 2 + b])):
                    ins = dve.tensor_tensor(mixed[:, b, :], ps[:, :],
                                            gate[:, bass.ds(j, 1), :].rearrange("p a n -> p (a n)"), ALU.mult)
                ins.then_inc(mix_gated if b == 0 else group_freed, 1)

            for g in range(2):
                for q in range(4):
                    split(MIX_C + 4 * g + q)
                    if g == 0 and q < 2:
                        oc_low(2 + q)
                    if g == 0 and q == 2:
                        gates_scaled(7)
                    if g == 1:
                        if q == 1:
                            dve.wait_ge(gate_stored, 2 * KD)
                        mix_slot(q, 0)
            with dve.Fori(0, 3) as i:
                for g in (1, 2):
                    for q in range(4):
                        split(MIX_C + 4 * g + 4 + q, i, 8)
                        mix_slot(q, g, i)

            def out_slot(q, g):
                if q == 1:
                    dve.wait_ge(chunk_used, used(OUT_C + 8 * g + 7))
                    dve.wait_ge(xres_loaded, 16 * TT)
                    for t in range(TT):
                        piece = x_res[:, t, 512 * g:512 * g + 512]
                        ins = dve.tensor_tensor(piece, piece, bank[4 * (g % 2) + t][:, :], ALU.add)
                    ins.then_inc(group_freed, 1)

            for g in range(4):
                for q in range(8):
                    split(OUT_C + 8 * g + q)
                    if g == 0:
                        mix_slot(q, 7)
                    else:
                        out_slot(q, g - 1)
                    if g >= 1 and q == 5:
                        turned_low(1, g - 1, 4 * ((g - 1) % 2))

            def up_slot(q, n, last, group, i=None):
                after = freed(group, i, 12)
                s = 4 * (n // 2 % 2)
                if q == 2:
                    dve.wait_ge(chunk_used, used(last, i, 48))
                    if n >= 2:
                        dve.wait_ge(u_ready, val(n, i, 8))
                        dve.wait_ge(tap_mid_ready, val(n, i, 8))
                    for b in range(2):
                        scaled(f_raw[:, b, :], bank[s + b]).then_inc(up_scaled, 1)
                    for b in range(2):
                        ins = scaled(f_val[:, b, :], bank[s + 2 + b])
                    ins.then_inc(group_freed, 1)
                for b in range(2):
                    ft = val(n + b, i, 8)
                    gate = f_gate[:, b, :]
                    if q == 4:
                        dve.wait_ge(tap_mid_ready, ft + 1)
                        for tap, out, src, done in ((0, slice(1, SEQ), slice(0, SEQ - 1), tap_left_ready),
                                                    (2, slice(0, SEQ - 1), slice(1, SEQ), taps_ready)):
                            if tap == 2:
                                dve.wait_ge(tap_left_ready, ft + 1)
                            dve.scalar_tensor_tensor(out=gate[:, out], in0=f_raw[:, b, src],
                                                     scalar=par[:, bass.ds(ft * 3 + (COL["ffn_w"] + tap), 1)],
                                                     in1=gate[:, out], op0=ALU.mult, op1=ALU.add).then_inc(done, 1)
                    if q == 6:
                        dve.wait_ge(silu_ready, ft + 1)
                        if b == 0:
                            dve.wait_ge(group_freed, after)
                        if n >= 2:
                            dve.wait_ge(u_low_ready, val(n + b - 1, i, 8))
                        dve.tensor_tensor(f_u[:, b, :], gate, f_val[:, b, :], ALU.mult).then_inc(u_ready, 1)

            def down_out(r, q, i=None):
                dve.wait_ge(chunk_used, used(FFN_C + 32 + 24 * r + 2 * q + 1, i, 48))
                dve.wait_ge(group_freed, freed(DOWN_G + 6 * r - 6 + q, i, 12))
                for t in range(TT):
                    piece = x_res[:, t, 512 * q:512 * q + 512]
                    ins = dve.tensor_tensor(piece, piece, bank[4 * (q % 2) + t][:, :], ALU.add)
                ins.then_inc(group_freed, 1)

            for g in range(4):
                for q in range(8):
                    if g == 1 and q == 0:
                        mean_square(1)
                    split(FFN_C + 8 * g + q)
                    if g == 0:
                        out_slot(q, 3)
                        if q == 1:
                            turned_low(1, 3, 4)
                    if g == 1 and q == 1:
                        copy_rstd(1)
                    if g >= 1:
                        up_slot(q, 2 * g - 2, FFN_C + 8 * g - 1, FFN_G + g - 1)

            def ffn_round(r, i=None):
                c = FFN_C + 32 + 24 * r
                for q in range(8):
                    split(c + q, i, 48)
                    up_slot(q, 4 * r + 6, c - 1, DOWN_G + 6 * r - 1, i)
                    if q in (3, 5, 7):
                        down_out(r, (q - 3) // 2, i)
                for q in range(8):
                    split(c + 8 + q, i, 48)
                    if q == 1:
                        down_out(r, 3, i)
                for q in range(8):
                    split(c + 16 + q, i, 48)
                    up_slot(q, 4 * r + 8, c + 15, DOWN_G + 6 * r + 4, i)

            with dve.Fori(0, (ROUNDS - 3) // 2) as i:
                ffn_round(0, i)
                ffn_round(1, i)
            ffn_round(ROUNDS - 3)
            for j in range(8):
                for k, (high, low) in enumerate(((w_high[:, j % N_SPLIT, :], w_low[:, j % N_SPLIT, :]),
                                                 (last_high[:, j, :], last_low[:, j, :]))):
                    n = END_C + 2 * j + k
                    dve.wait_ge(high_split, n + 1)
                    dve.tensor_tensor(low, w_raw[:, chunk_slot(n)[0], :], high.bitcast(F32),
                                      ALU.subtract).then_inc(low_split, 1)
                up_slot(j, KF - 2, END_C - 1, END_G - 1)
                if j in (3, 5, 7):
                    down_out(ROUNDS - 2, (j - 3) // 2)
            down_out(ROUNDS - 2, 3)
            dve.wait_ge(gfin_loaded, 16)
            dve.wait_ge(group_freed, freed(END_G + 3))
            for t in range(TT):
                for q in range(4):
                    dve.wait_ge(last_summed, 4 * t + q + 1)
                    piece = x_res[:, t, 512 * q:512 * q + 512]
                    dve.tensor_tensor(piece, piece, bank[4 * (t % 2) + q][:, :], ALU.add).then_inc(x_added, 1)
                n = 2 * TT + t
                dve.wait_ge(squares_summed, 32 + 4 * t + 4)
                step(dve.tensor_reduce(sumsq[:, n:n + 1], sq_part[:, 32 + 4 * t:32 + 4 * t + 4], AX.X, ALU.add))
                dve.tensor_scalar(meansq[:, n:n + 1], sumsq[:, n:n + 1], 1.0 / D, EPS, ALU.mult,
                                  ALU.add).then_inc(meansq_ready, 1)
                dve.wait_ge(rstd_ready, 3 + t)
                right = slice(D // 2, D)
                dve.scalar_tensor_tensor(out=x_res[:, t, right], in0=x_res[:, t, right],
                                         scalar=rstd[:, n:n + 1], in1=g_fin[:, right],
                                         op0=ALU.mult, op1=ALU.mult).then_inc(y_right_ready, 1)

        @block.tensor
        def _(pe):
            def products(ps, a_high, a_low, b_high, b_low, first, last):
                pe.matmul(ps, a_high, b_high, start=first, stop=False)
                pe.matmul(ps, a_high, b_low, start=False, stop=False)
                return pe.matmul(ps, a_low, b_high, start=False, stop=last)

            def pair_group(c, s, high, low, chunks=4, i=None, per=0, before=None, high2=None, low2=None,
                           before_tile=None):
                for n in range(2 * chunks):
                    half, q = n // chunks, n % chunks
                    xh, xl = (high, low) if half == 0 or high2 is None else (high2, low2)
                    if before is not None and n in before:
                        before[n]()
                    pe.wait_ge(low_split, val(c + n + 1, i, per))
                    slot = (c + n) % N_SPLIT
                    for kk in range(4):
                        k = 4 * q + kk
                        if before_tile is not None:
                            before_tile(n, kk)
                        for b in range(2):
                            w = slice(256 * kk + P * b, 256 * kk + P * b + P)
                            ins = products(bank[s + 2 * half + b][:, :], w_high[:, slot, w], w_low[:, slot, w],
                                           xh[:, k, :], xl[:, k, :], k == 0, k == 4 * chunks - 1)
                    ins.then_inc(chunk_used, 1)

            def wide_group(c, s, high, low, chunks=8, i=None, per=0, before=None):
                for q in range(chunks):
                    if before is not None:
                        before(q)
                    pe.wait_ge(low_split, val(c + q + 1, i, per))
                    slot = (c + q) % N_SPLIT
                    for kk in range(2):
                        k = 2 * q + kk
                        w = slice(512 * kk, 512 * kk + 512)
                        for t in range(TT):
                            tok = slice(P * t, P * t + P)
                            ins = products(bank[s + t][:, :], high[:, k, tok], low[:, k, tok],
                                           w_high[:, slot, w], w_low[:, slot, w], k == 0, k == 2 * chunks - 1)
                    ins.then_inc(chunk_used, 1)

            def turn(w, n, s, src, tiles=range(4)):
                for k in [4 * n + b for b in tiles]:
                    for t in range(TT):
                        ins = pe.transpose(bank[s + k % 4][:, P * t:P * t + P],
                                           src[:, t, P * k:P * k + P], ident[:, :])
                    ins.then_inc(x_turned, 1)

            def turn_x_in(n):
                if n == 0:
                    pe.wait_ge(x_head_loaded, 16)
                    turn(0, n, 4, x_in, (0, 1))
                    pe.wait_ge(x_loaded[n], 16)
                    turn(0, n, 4, x_in, (2, 3))
                else:
                    pe.wait_ge(x_loaded[n], 16)
                    pe.wait_ge(h_low_ready, 4 * n)
                    turn(0, n, 4, x_in)

            def spread_rstd(w):
                pe.wait_ge(h_low_ready, KD * w + KD)
                pe.wait_ge(rstd_ready, w + 1)
                for t in range(TT):
                    n = TT * w + t
                    ins = pe.matmul(bank[7][:, P * t:P * t + P], rstd[:, n:n + 1].to_broadcast([P, P]),
                                    ident[:, :], start=True, stop=True)
                ins.then_inc(rstd_spread, 1)

            pe.wait_ge(consts_made, 5)
            turn_x_in(0)

            def first(n, kk):
                if n < 3 and kk == 2:
                    turn_x_in(n + 1)
                if n < 4:
                    pe.wait_ge(h_low_ready, 4 * n + kk + 1)

            pair_group(GLU_C, 0, h_high, h_low, before_tile=first)
            pair_group(GLU_C + 8, 4, h_high, h_low,
                       before={1: partial(spread_rstd, 0), 4: lambda: pe.wait_ge(rstd_copied, 1)})
            for g in range(2, 4):
                pe.wait_ge(group_freed, freed(GLU_G + g - 2))
                pair_group(GLU_C + 8 * g, 4 * (g % 2), h_high, h_low)
            for g in range(3):
                pe.wait_ge(group_freed, freed(QKV_G + g - 2))
                wide_group(QKV_C + 8 * g, 4 * (g % 2), h_high, h_low)

            def turn_kq(g):
                for b, c0 in enumerate(head_cols(g)):
                    if g == 1 and b > 0:
                        pe.wait_ge(kq_low_ready, b)
                    for t in range(TT):
                        ins = pe.transpose(bank[kq_bank(g, b)][:, P * t:P * t + P],
                                           qkv[:, t, c0:c0 + HD], ident[:, :])
                    ins.then_inc(kq_turned, 1)

            def scores(h):
                g, b = h // 2, 1 + h % 2
                pe.wait_ge(kq_low_ready, 3 * (g + 1))
                k_high = qkv_high[:, :, head_cols(g)[0]:head_cols(g)[0] + HD]
                q0 = head_cols(g)[b]
                for t in range(TT):
                    if h >= 1:
                        pe.wait_ge(exp_ready, 4 * (h - 1) + t + 1)
                    else:
                        pe.wait_ge(kq_low_ready, 6)
                    products(bank[t][:, :], qkv_high[:, t, q0:q0 + HD], kq_low[:, g % 2, b, P * t:P * t + P],
                             k_high, kq_low[:, g % 2, 0, :], True, True).then_inc(scores_ready, 1)

            def turn_probs(h):
                pe.wait_ge(probs_ready, 4 * h + 4)
                for k in range(TT):
                    if h in (1, 3) and k < 3:
                        pe.wait_ge(kq_low_ready, 3 * (h + 3) // 2 + k + 1)
                    if h >= 1 and k == 3:
                        pe.wait_ge(o_ready, h)
                    for t in range(TT):
                        ins = pe.transpose(bank[pt_bank(h, k)][:, P * t:P * t + P],
                                           probs[:, h % 2, t, P * k:P * k + P], ident[:, :])
                    ins.then_inc(probs_turned, 1)

            def weighted_sum(h):
                pe.wait_ge(v_low_ready, h // 2 + 1)
                for k in range(TT):
                    pe.wait_ge(pt_low_ready, 4 * h + k + 1)
                    ins = products(bank[pt_bank(h, 0)][:, :], v_high[:, k, :], v_low[:, k, :],
                                   pt_high[:, k, :], pt_low[:, k, :], k == 0, k == TT - 1)
                ins.then_inc(o_summed, 1)

            def v_before(q):
                if q == 3:
                    pe.wait_ge(roped, 2)
                    pe.wait_ge(group_freed, freed(QKV_G + 2))
                    turn_kq(0)
                if q == 4:
                    turn_kq(1)
                if q == 6:
                    scores(0)

            pe.wait_ge(group_freed, freed(QKV_G + 1))
            wide_group(QKV_C + 24, 4, h_high, h_low, before=v_before)
            scores(1)
            pe.wait_ge(roped, 3)
            pe.wait_ge(group_freed, freed(QKV_G + 3))
            for h in range(HEADS):
                turn_probs(h)
                if h + 2 < HEADS:
                    scores(h + 2)
                if h in (0, 2):
                    pe.wait_ge(pt_low_ready, 4 * h + 4)
                    turn_kq(h // 2 + 2)
                weighted_sum(h)

            pe.wait_ge(o_ready, HEADS)
            with pe.Fori(0, 2) as i:
                for g in range(2):
                    pe.wait_ge(group_freed, i * 2 + freed(GATE_G + g - 2))
                    pair_group(GATE_C + 8 * g, 4 * g, h_high, h_low, 4, i, 16)
            pe.wait_ge(group_freed, freed(GATE_G + 2))
            pair_group(GATE_C + 32, 0, h_high, h_low)
            pe.wait_ge(group_freed, freed(GATE_G + 3))
            pe.wait_ge(ch_sum_ready, 1)
            pe.matmul(bank[7][:, :], mean_w[:, :], ch_sum[:, :], start=True, stop=True).then_inc(mean_ready, 1)
            pair_group(GATE_C + 40, 4, h_high, h_low, before={4: lambda: pe.wait_ge(mean_copied, 1)})
            pe.wait_ge(group_freed, freed(GATE_G + 4))
            pe.wait_ge(ch_sq_added, KC)
            pe.matmul(bank[3][:, :], mean_w[:, :], sq_sum[:, :], start=True, stop=True).then_inc(var_ready, 1)
            pair_group(GATE_C + 48, 0, h_high, h_low, before={4: lambda: pe.wait_ge(var_copied, 1)})
            pe.wait_ge(group_freed, freed(GATE_G + 5))
            pair_group(GATE_C + 56, 4, h_high, h_low)

            with pe.Fori(0, 4) as i:
                for g in range(2):
                    pe.wait_ge(group_freed, i * 2 + freed(MIX_G + g - 2))
                    pair_group(MIX_C + 4 * g, 4 * g, o_high, o_low, 2, i, 8,
                               {n: partial(pe.wait_ge, oc_low_ready, n + 1) for n in range(4)}, c_high, c_low)

            def out_before(g, q):
                if q == 4 and g >= 1:
                    pe.wait_ge(group_freed, freed(OUT_G + g - 1))
                    turn(1, g - 1, 4 * ((g - 1) % 2), x_res)
                pe.wait_ge(m_low_ready, 2 * q + 2)

            for g in range(4):
                pe.wait_ge(group_freed, freed(OUT_G + g - 2))
                if g >= 2:
                    pe.wait_ge(h_low_ready, KD + 4 * (g - 1))
                wide_group(OUT_C + 8 * g, 4 * (g % 2), m_high, m_low, before=partial(out_before, g))

            def last_turn():
                pe.wait_ge(group_freed, freed(OUT_G + 3))
                turn(1, 3, 4, x_res)

            pe.wait_ge(h_low_ready, KD + 12)
            pair_group(FFN_C, 0, h_high, h_low,
                       before={1: last_turn, 3: lambda: pe.wait_ge(h_low_ready, KD + KD)})
            pair_group(FFN_C + 8, 4, h_high, h_low,
                       before={1: partial(spread_rstd, 1), 4: lambda: pe.wait_ge(rstd_copied, 2)})
            for g in range(2, 4):
                pe.wait_ge(group_freed, freed(FFN_G + g - 2))
                pair_group(FFN_C + 8 * g, 4 * (g % 2), h_high, h_low)

            def down(r, c, group, i=None):
                for q in range(4):
                    pe.wait_ge(group_freed, freed(group + q - 2, i, 12))
                    wide_group(c + 2 * q, 4 * (q % 2), u_high[:, r % 2], u_low[:, r % 2], 2, i, 48,
                               lambda k: pe.wait_ge(u_low_ready, val(4 * r + 2 * k + 2, i, 8)))

            def ffn_round(r, i=None):
                c, group = FFN_C + 32 + 24 * r, DOWN_G + 6 * r
                down(r, c, group, i)
                for a in range(2):
                    pe.wait_ge(group_freed, freed(group + 2 + a, i, 12))
                    pair_group(c + 8 + 8 * a, 4 * a, h_high, h_low, 4, i, 48)

            with pe.Fori(0, (ROUNDS - 3) // 2) as i:
                ffn_round(0, i)
                ffn_round(1, i)
            ffn_round(ROUNDS - 3)
            for q in range(4):
                pe.wait_ge(group_freed, freed(END_G + q - 2))
                wide_group(END_C + 2 * q, 4 * (q % 2), u_high[:, (ROUNDS - 2) % 2], u_low[:, (ROUNDS - 2) % 2],
                           2, before=lambda k: pe.wait_ge(low_split, END_C + 4 * q + 2 * k + 1))
            buf = (ROUNDS - 1) % 2
            pe.wait_ge(u_low_ready, KF)
            for t in range(TT):
                if t < 2:
                    pe.wait_ge(group_freed, freed(END_G + 2 + t))
                for q in range(4):
                    if t == 0:
                        pe.wait_ge(low_split, END_C + 4 * q + 4)
                    if t >= 2:
                        pe.wait_ge(x_added, 4 * (t - 2) + q + 1)
                    for k in range(4):
                        tok = slice(P * t, P * t + P)
                        w = slice(512 * (k % 2), 512 * (k % 2) + 512)
                        j = 2 * q + k // 2
                        ins = products(bank[4 * (t % 2) + q][:, :], u_high[:, buf, k, tok], u_low[:, buf, k, tok],
                                       last_high[:, j, w], last_low[:, j, w], k == 0, k == 3)
                    ins.then_inc(last_summed, 1)


def rope_tables():
    f32 = np.float32
    rows = SEQ // GRID_W
    row = np.repeat(np.arange(rows), GRID_W).astype(f32)
    column = np.tile(np.arange(GRID_W), rows).astype(f32)
    inv_freq = f32(ROPE_THETA) ** (-np.arange(0, HD // 2, 2, dtype=f32) / f32(HD // 2))
    angle = np.concatenate([row[:, None] * inv_freq, column[:, None] * inv_freq], axis=-1).astype(f32)
    return np.stack([np.cos(angle), np.sin(angle)]).astype(f32)


def kernel(x, norm_mix_g, w_in, b_in, q_norm_g, k_norm_g, w_attn_o, conv_dw_w, conv_dw_b, conv_ln_g,
           conv_ln_b, w_conv_o, w_out, norm_ffn_g, w_ffn_up, ffn_dw_w, ffn_dw_b, w_ffn_down, norm_final_g):
    import concourse.bacc as bacc
    from concourse.bass_utils import run_bass_kernel_spmd

    def tiles(v):
        return np.asarray(v).reshape(-1, P).T

    def taps(w):
        w = np.asarray(w)
        return w.reshape(w.shape[0], -1, P).transpose(2, 1, 0).reshape(P, -1)

    b = np.asarray(b_in)[0]
    cols = np.concatenate([
        tiles(norm_mix_g[0]), tiles(norm_ffn_g[0]), tiles(b[GLU_COL:GATE_COL]), tiles(b[GATE_COL:]),
        tiles(conv_dw_b[0]), tiles(conv_ln_g[0]), tiles(conv_ln_b[0]), taps(conv_dw_w[0]),
        taps(ffn_dw_w[0]), tiles(ffn_dw_b[0])], axis=1)
    rope = rope_tables().reshape(2, TT, P, HD // 2).transpose(2, 0, 1, 3)
    arrays = {
        "x_dram": np.asarray(x)[0], "w_in_dram": np.asarray(w_in)[0],
        "w_attn_o_dram": np.asarray(w_attn_o)[0], "w_conv_o_dram": np.asarray(w_conv_o)[0],
        "w_out_dram": np.asarray(w_out)[0], "w_up_dram": np.asarray(w_ffn_up)[0],
        "w_down_dram": np.asarray(w_ffn_down)[0], "cols_dram": cols, "b_qkv_dram": b[:GLU_COL],
        "qk_g_dram": np.stack([np.asarray(q_norm_g)[0], np.asarray(k_norm_g)[0]]),
        "g_final_dram": np.asarray(norm_final_g), "rope_dram": rope,
    }
    arrays = {name: np.ascontiguousarray(a) for name, a in arrays.items()}
    nc = bacc.Bacc("TRN2", target_bir_lowering=False, num_devices=1, dynamic_dma_scratch_size=1024)
    ins = [nc.dram_tensor(name, a.shape, mybir.dt.from_np(a.dtype), kind="ExternalInput").ap()
           for name, a in arrays.items()]
    y = nc.dram_tensor("y_dram", (SEQ, D), F32, kind="ExternalOutput").ap()
    build(nc, *ins, y)
    result = run_bass_kernel_spmd(nc, [arrays], core_ids=[0])
    return result.results[0]["y_dram"].reshape(1, SEQ, D)
```
